# Optimizing a Trainium2 kernel written in Bass

```python
import jax, jax.numpy as jnp
from jax import lax
import numpy as np
import math

D_MODEL = 1024
BATCH = 1
SEQ = 512
DEPTH = 1

D_MIX = 2 * D_MODEL
D_ML = D_MIX // 2
N_ML_HEADS = 4
ML_HEAD_DIM = D_ML // N_ML_HEADS
QK_CONV = 4
ML_CHUNK = 128
D_CV = D_MIX - D_ML
CV_KERNEL = 31
N_IN = 2 * D_ML + D_ML + D_ML + 2 * N_ML_HEADS + 2 * D_CV
D_FF = ((8 * D_MODEL // 3 + 127) // 128) * 128
FFN_KERNEL = 3
N_MOD = 6
EPS = 1e-6


def rms_norm(x, g):
    xf = x.astype(jnp.float32)
    y = xf * lax.rsqrt(jnp.mean(xf * xf, axis=-1, keepdims=True) + EPS)
    return (y * g.astype(jnp.float32)).astype(x.dtype)

def layer_norm(x, g, b):
    xf = x.astype(jnp.float32)
    mu = jnp.mean(xf, axis=-1, keepdims=True)
    var = jnp.mean(jnp.square(xf - mu), axis=-1, keepdims=True)
    y = (xf - mu) * lax.rsqrt(var + EPS)
    return (y * g.astype(jnp.float32) + b.astype(jnp.float32)).astype(x.dtype)

def causal_dwconv(x, w, b):
    K, C = w.shape
    y = lax.conv_general_dilated(
        x, w[:, None, :].astype(x.dtype), window_strides=(1,), padding=[(K - 1, 0)],
        dimension_numbers=("NWC", "WIO", "NWC"), feature_group_count=C)
    return y + b

def mlstm_chunkwise(q, k, v, i_pre, f_pre):
    Bsz, S, H, Dh = q.shape
    L = ML_CHUNK
    nc = S // L

    def chunks(t):
        t = t.astype(jnp.float32).reshape((Bsz, nc, L, H) + t.shape[3:])
        return jnp.moveaxis(t, (1, 3), (0, 2))

    qc = chunks(q)
    kc = chunks(k) * (Dh ** -0.5)
    vc = chunks(v)
    ic = chunks(i_pre)
    lfc = jax.nn.log_sigmoid(chunks(f_pre))
    causal = jnp.tril(jnp.ones((L, L), dtype=bool))

    def step(carry, inp):
        C, n, m = carry
        q_, k_, v_, i_, lf_ = inp
        b = jnp.cumsum(lf_, axis=-1)
        dmat = jnp.where(causal, b[..., :, None] - b[..., None, :] + i_[..., None, :], -jnp.inf)
        m_t = jnp.maximum(b + m[..., None], jnp.max(dmat, axis=-1))
        w_inter = jnp.exp(b + m[..., None] - m_t)
        scores = jnp.einsum("bhtd,bhsd->bhts", q_, k_) * jnp.exp(dmat - m_t[..., None])
        num = (w_inter[..., None] * jnp.einsum("bhtd,bhde->bhte", q_, C)
               + jnp.einsum("bhts,bhse->bhte", scores, v_))
        den = w_inter * jnp.einsum("bhtd,bhd->bht", q_, n) + jnp.sum(scores, axis=-1)
        h = num / jnp.maximum(jnp.abs(den), jnp.exp(-m_t))[..., None]
        b_last = b[..., -1]
        g = b_last[..., None] - b + i_
        m_new = jnp.maximum(b_last + m, jnp.max(g, axis=-1))
        decay = jnp.exp(b_last + m - m_new)
        kw = k_ * jnp.exp(g - m_new[..., None])[..., None]
        C = decay[..., None, None] * C + jnp.einsum("bhsd,bhse->bhde", kw, v_)
        n = decay[..., None] * n + jnp.sum(kw, axis=2)
        return (C, n, m_new), h

    init = (jnp.zeros((Bsz, H, Dh, Dh), jnp.float32),
            jnp.zeros((Bsz, H, Dh), jnp.float32),
            jnp.zeros((Bsz, H), jnp.float32))
    _, h = lax.scan(step, init, (qc, kc, vc, ic, lfc))
    return jnp.moveaxis(h, (0, 2), (1, 3)).reshape(Bsz, S, H, Dh)

def first_inputs(seed: int = 0) -> dict:
    key = jax.random.key(seed)
    ks = jax.random.split(key, 24)

    def nrm(k, shape, scale):
        return jax.random.normal(k, shape, jnp.float32) * scale

    def gain(k, shape):
        return 1.0 + nrm(k, shape, 0.05)

    Ly = DEPTH
    fbias = jnp.linspace(3.0, 6.0, N_ML_HEADS, dtype=jnp.float32)[None, :] + nrm(ks[9], (Ly, N_ML_HEADS), 0.1)
    return {
        "x": nrm(ks[0], (BATCH, SEQ, D_MODEL), 1.0),
        "c": nrm(ks[1], (BATCH, D_MODEL), 1.0),
        "ada_w": nrm(ks[2], (Ly, D_MODEL, N_MOD * D_MODEL), 0.5 * D_MODEL ** -0.5),
        "ada_b": nrm(ks[3], (Ly, N_MOD * D_MODEL), 0.02),
        "mix_pre_g": gain(ks[4], (Ly, D_MODEL)),
        "mix_post_g": gain(ks[5], (Ly, D_MODEL)),
        "w_in": nrm(ks[6], (Ly, D_MODEL, N_IN), D_MODEL ** -0.5),
        "qk_conv_w": nrm(ks[7], (Ly, QK_CONV, 2 * D_ML), QK_CONV ** -0.5),
        "qk_conv_b": nrm(ks[8], (Ly, 2 * D_ML), 0.02),
        "igate_b": nrm(ks[10], (Ly, N_ML_HEADS), 0.1),
        "fgate_b": fbias,
        "ml_norm_g": gain(ks[11], (Ly, D_ML)),
        "cv_dw_w": nrm(ks[12], (Ly, CV_KERNEL, D_CV), CV_KERNEL ** -0.5),
        "cv_dw_b": nrm(ks[13], (Ly, D_CV), 0.02),
        "cv_ln_g": gain(ks[14], (Ly, D_CV)),
        "cv_ln_b": nrm(ks[15], (Ly, D_CV), 0.02),
        "w_out": nrm(ks[16], (Ly, D_MIX, D_MODEL), D_MIX ** -0.5),
        "ffn_pre_g": gain(ks[17], (Ly, D_MODEL)),
        "ffn_post_g": gain(ks[18], (Ly, D_MODEL)),
        "ffn_up": nrm(ks[19], (Ly, D_MODEL, 2 * D_FF), D_MODEL ** -0.5),
        "ffn_conv_w": nrm(ks[20], (Ly, FFN_KERNEL, 2 * D_FF), FFN_KERNEL ** -0.5),
        "ffn_conv_b": nrm(ks[21], (Ly, 2 * D_FF), 0.02),
        "ffn_down": nrm(ks[22], (Ly, D_FF, D_MODEL), D_FF ** -0.5),
    }

def first_block(x, c, ada_w, ada_b, mix_pre_g, mix_post_g, w_in, qk_conv_w, qk_conv_b,
              igate_b, fgate_b, ml_norm_g, cv_dw_w, cv_dw_b, cv_ln_g, cv_ln_b, w_out,
              ffn_pre_g, ffn_post_g, ffn_up, ffn_conv_w, ffn_conv_b, ffn_down):
    Bsz, S, _ = x.shape
    H, Dh = N_ML_HEADS, ML_HEAD_DIM
    cond = jax.nn.silu(c)
    for l in range(DEPTH):
        mod = cond @ ada_w[l] + ada_b[l]
        sh1, sc1, g1, sh2, sc2, g2 = jnp.split(mod[:, None, :], N_MOD, axis=-1)

        u = rms_norm(x, mix_pre_g[l]) * (1.0 + sc1) + sh1
        proj = u @ w_in[l]
        qk_raw, v, o_pre, gates, glu = jnp.split(
            proj, [2 * D_ML, 3 * D_ML, 4 * D_ML, 4 * D_ML + 2 * H], axis=-1)

        qk = jax.nn.silu(causal_dwconv(qk_raw, qk_conv_w[l], qk_conv_b[l]))
        q, k = jnp.split(qk, 2, axis=-1)
        heads = lambda t: t.reshape(Bsz, S, H, Dh)
        h = mlstm_chunkwise(heads(q), heads(k), heads(v),
                            gates[..., :H] + igate_b[l], gates[..., H:] + fgate_b[l])
        h = rms_norm(h, ml_norm_g[l].reshape(H, Dh)).reshape(Bsz, S, D_ML)
        h = (h * jax.nn.sigmoid(o_pre.astype(jnp.float32))).astype(x.dtype)

        a, gt = jnp.split(glu, 2, axis=-1)
        y = causal_dwconv(a * jax.nn.sigmoid(gt), cv_dw_w[l], cv_dw_b[l])
        y = jax.nn.silu(layer_norm(y, cv_ln_g[l], cv_ln_b[l]))

        mix = jnp.concatenate([h, y], axis=-1) @ w_out[l]
        x = x + g1 * rms_norm(mix, mix_post_g[l])

        u = rms_norm(x, ffn_pre_g[l]) * (1.0 + sc2) + sh2
        up = causal_dwconv(u @ ffn_up[l], ffn_conv_w[l], ffn_conv_b[l])
        a, gt = jnp.split(up, 2, axis=-1)
        f = (jax.nn.silu(gt) * a) @ ffn_down[l]
        x = x + g2 * rms_norm(f, ffn_post_g[l])
    return x


DEPTH_2 = 2

CHUNK = 64
Q_BLOCK = 128
N_MIXERS = 2
FOX_HEADS = 16
FOX_HEAD_DIM = D_MODEL // FOX_HEADS
HGRN_EXPAND = 128
HGRN_HEADS = D_MODEL // HGRN_EXPAND
HGRN_HEAD_DIM = HGRN_EXPAND
D_FF_2 = -(-8 * D_MODEL // (3 * 256)) * 256
N_FOX = (DEPTH_2 + 1) // 2
N_HGRN = DEPTH_2 // 2


def rmsnorm(x, g):
    x32 = x.astype(jnp.float32)
    y = x32 * lax.rsqrt(jnp.mean(x32 * x32, axis=-1, keepdims=True) + EPS)
    return (y * g.astype(jnp.float32)).astype(x.dtype)

def fox_attention(h, w_in, b_f, w_out):
    bsz, seq, _ = h.shape
    proj = jnp.einsum('bsd,de->bse', h, w_in)
    q, k, v, f_logit = jnp.split(proj, [D_MODEL, 2 * D_MODEL, 3 * D_MODEL], axis=-1)

    def heads(t):
        return t.reshape(bsz, seq, FOX_HEADS, FOX_HEAD_DIM).transpose(0, 2, 1, 3)

    q = heads(q) * (FOX_HEAD_DIM ** -0.5)
    k = heads(k)
    v = heads(v)
    log_f = jax.nn.log_sigmoid(f_logit.astype(jnp.float32) + b_f.astype(jnp.float32))
    c = jnp.cumsum(log_f, axis=1).transpose(0, 2, 1)
    key_pos = jnp.arange(seq)

    def q_block(blk):
        start = blk * Q_BLOCK
        qb = lax.dynamic_slice_in_dim(q, start, Q_BLOCK, axis=2)
        cb = lax.dynamic_slice_in_dim(c, start, Q_BLOCK, axis=2)
        q_pos = start + jnp.arange(Q_BLOCK)
        logits = jnp.einsum('bhqd,bhkd->bhqk', qb, k).astype(jnp.float32)
        logits = logits + cb[:, :, :, None] - c[:, :, None, :]
        logits = jnp.where(q_pos[:, None] >= key_pos[None, :], logits, -jnp.inf)
        p = jax.nn.softmax(logits, axis=-1).astype(v.dtype)
        return jnp.einsum('bhqk,bhkd->bhqd', p, v)

    out = lax.map(q_block, jnp.arange(seq // Q_BLOCK))
    out = out.transpose(1, 0, 3, 2, 4).reshape(bsz, seq, D_MODEL)
    return jnp.einsum('bsd,de->bse', out, w_out)

def hgrn2_recurrence(h, w_in, lb, g_norm_w, w_out):
    bsz, seq, _ = h.shape
    n_chunks = seq // CHUNK
    proj = jnp.einsum('bsd,de->bse', h, w_in)
    q, f_logit, i_val, g = jnp.split(proj, [D_MODEL, 2 * D_MODEL, 3 * D_MODEL], axis=-1)
    f = lb + (1.0 - lb) * jax.nn.sigmoid(f_logit.astype(jnp.float32))
    log_f = jnp.log(f)
    k = 1.0 - f

    def to_chunks(t):
        t = t.astype(jnp.float32).reshape(bsz, n_chunks, CHUNK, HGRN_HEADS, HGRN_HEAD_DIM)
        return t.transpose(1, 0, 3, 2, 4)

    qc = to_chunks(q)
    kc = to_chunks(k)
    vc = to_chunks(i_val)
    bc = jnp.cumsum(to_chunks(log_f), axis=3)
    causal = jnp.arange(CHUNK)[:, None] >= jnp.arange(CHUNK)[None, :]

    def step(state, xs):
        q_t, k_t, v_t, b_t = xs
        o_inter = jnp.einsum('bhtk,bhkv->bhtv', q_t * jnp.exp(b_t), state)
        diff = b_t[:, :, :, None, :] - b_t[:, :, None, :, :]
        decay = jnp.exp(jnp.where(causal[:, :, None], diff, -jnp.inf))
        scores = jnp.einsum('bhtk,bhsk,bhtsk->bhts', q_t, k_t, decay)
        o = o_inter + jnp.einsum('bhts,bhsv->bhtv', scores, v_t)
        b_last = b_t[:, :, -1, :]
        k_dec = k_t * jnp.exp(b_last[:, :, None, :] - b_t)
        new_state = jnp.exp(b_last)[..., None] * state + jnp.einsum('bhsk,bhsv->bhkv', k_dec, v_t)
        return new_state, o

    state0 = jnp.zeros((bsz, HGRN_HEADS, HGRN_HEAD_DIM, HGRN_HEAD_DIM), jnp.float32)
    _, o = lax.scan(step, state0, (qc, kc, vc, bc))
    o = o.transpose(1, 0, 3, 2, 4).reshape(bsz, seq, HGRN_HEADS, HGRN_HEAD_DIM)
    g = g.astype(jnp.float32).reshape(bsz, seq, HGRN_HEADS, HGRN_HEAD_DIM)
    o = rmsnorm(o, g_norm_w) * jax.nn.silu(g)
    return jnp.einsum('bsd,de->bse', o.reshape(bsz, seq, D_MODEL).astype(h.dtype), w_out)

def swiglu_ffn(h, w_in, w_out):
    gate, up = jnp.split(jnp.einsum('bsd,df->bsf', h, w_in), 2, axis=-1)
    return jnp.einsum('bsf,fd->bsd', jax.nn.silu(gate) * up, w_out)

def second_inputs(seed: int = 0) -> dict:
    key = jax.random.key(seed)
    ks = jax.random.split(key, 11)
    f32 = jnp.float32

    def normal(k, shape, fan_in):
        return jax.random.normal(k, shape, f32) * (fan_in ** -0.5)

    x = jax.random.normal(ks[0], (BATCH, SEQ, D_MODEL), f32)
    fox_w_in = normal(ks[1], (N_FOX, D_MODEL, 3 * D_MODEL + FOX_HEADS), D_MODEL)
    fox_b_f = jax.random.uniform(ks[2], (N_FOX, FOX_HEADS), f32, 1.0, 4.0)
    fox_w_out = normal(ks[3], (N_FOX, D_MODEL, D_MODEL), D_MODEL)
    hgrn_w_in = normal(ks[4], (N_HGRN, D_MODEL, 4 * D_MODEL), D_MODEL)
    hgrn_lb_table = 0.5 * jax.random.normal(ks[5], (DEPTH_2 + 1, D_MODEL), f32)
    hgrn_gnorm = 1.0 + 0.02 * jax.random.normal(ks[6], (N_HGRN, HGRN_HEAD_DIM), f32)
    hgrn_w_out = normal(ks[7], (N_HGRN, D_MODEL, D_MODEL), D_MODEL)
    ffn_w_in = normal(ks[8], (DEPTH_2, D_MODEL, 2 * D_FF_2), D_MODEL)
    ffn_w_out = normal(ks[9], (DEPTH_2, D_FF_2, D_MODEL), D_FF_2)
    norm_gains = 1.0 + 0.02 * jax.random.normal(ks[10], (DEPTH_2, 4, D_MODEL), f32)
    return {'x': x, 'fox_w_in': fox_w_in, 'fox_b_f': fox_b_f, 'fox_w_out': fox_w_out,
            'hgrn_w_in': hgrn_w_in, 'hgrn_lb_table': hgrn_lb_table, 'hgrn_gnorm': hgrn_gnorm,
            'hgrn_w_out': hgrn_w_out, 'ffn_w_in': ffn_w_in, 'ffn_w_out': ffn_w_out,
            'norm_gains': norm_gains}

def second_block(x, fox_w_in, fox_b_f, fox_w_out, hgrn_w_in, hgrn_lb_table, hgrn_gnorm,
              hgrn_w_out, ffn_w_in, ffn_w_out, norm_gains):
    lower_bounds = jnp.cumsum(jax.nn.softmax(hgrn_lb_table.astype(jnp.float32), axis=0), axis=0)
    h = x
    for layer in range(DEPTH_2):
        j = layer // N_MIXERS
        hn = rmsnorm(h, norm_gains[layer, 0])
        if layer % N_MIXERS == 0:
            mixed = fox_attention(hn, fox_w_in[j], fox_b_f[j], fox_w_out[j])
        else:
            mixed = hgrn2_recurrence(hn, hgrn_w_in[j], lower_bounds[layer], hgrn_gnorm[j],
                                     hgrn_w_out[j])
        h = h + rmsnorm(mixed, norm_gains[layer, 1])
        hn = rmsnorm(h, norm_gains[layer, 2])
        h = h + rmsnorm(swiglu_ffn(hn, ffn_w_in[layer], ffn_w_out[layer]), norm_gains[layer, 3])
    return h


def setup_inputs(seed=0):
    out = dict(first_inputs(seed))
    for name, value in second_inputs(seed + 1).items():
        if name != "x":
            out[name + "_2"] = value
    return out


def reference(
    x, c, ada_w, ada_b, mix_pre_g, mix_post_g, w_in, qk_conv_w, qk_conv_b, igate_b, fgate_b,
    ml_norm_g, cv_dw_w, cv_dw_b, cv_ln_g, cv_ln_b, w_out, ffn_pre_g, ffn_post_g, ffn_up,
    ffn_conv_w, ffn_conv_b, ffn_down, fox_w_in_2, fox_b_f_2, fox_w_out_2, hgrn_w_in_2,
    hgrn_lb_table_2, hgrn_gnorm_2, hgrn_w_out_2, ffn_w_in_2, ffn_w_out_2, norm_gains_2,
):
    x = first_block(
        x, c, ada_w, ada_b, mix_pre_g, mix_post_g, w_in, qk_conv_w, qk_conv_b, igate_b, fgate_b,
        ml_norm_g, cv_dw_w, cv_dw_b, cv_ln_g, cv_ln_b, w_out, ffn_pre_g, ffn_post_g, ffn_up,
        ffn_conv_w, ffn_conv_b, ffn_down,
    )
    return second_block(
        x, fox_w_in_2, fox_b_f_2, fox_w_out_2, hgrn_w_in_2, hgrn_lb_table_2, hgrn_gnorm_2,
        hgrn_w_out_2, ffn_w_in_2, ffn_w_out_2, norm_gains_2,
    )


_drawn_inputs = setup_inputs


def setup_inputs(seed=0):
    import zlib

    import numpy as np

    out = dict(_drawn_inputs(seed))
    spreads = {}
    factors = {'qk_conv_b': 8.0,
     'igate_b': 200.0,
     'cv_ln_b': 4.023,
     'ffn_conv_b': 3.252,
     'hgrn_gnorm_2': 133.042}
    for name, (base, spread) in spreads.items():
        noise = np.random.default_rng([zlib.crc32(name.encode()), seed]).standard_normal(out[name].shape)
        drawn = base * np.exp(spread * noise) if base else spread * noise
        out[name] = __import__('jax').numpy.asarray(drawn.astype(out[name].dtype))
    for name, factor in factors.items():
        out[name] = (out[name] * factor).astype(out[name].dtype)
    return out
```

```python
import numpy as np
import concourse.bass as bass
from concourse import mybir
from contextlib import ExitStack

P = 128
T = 512
D = 1024
KT = D // P
NT = T // P
EPS = 1e-6
H1, DH1 = 4, 256
QK_TAPS, CV_TAPS, FF_TAPS = 4, 31, 3
FT = 2816 // P
FOX_H = 16
FOX_D = D // FOX_H
HG_H = 8
BIG = 1e30

C_GATE1 = 0
C_MIX = 1
C_WOUT1 = C_MIX + 12 * H1
C_UP1 = C_WOUT1 + 2 * KT
C_DOWN1 = C_UP1 + 2 * FT
C_GATE2 = C_DOWN1 + 3 * KT
C_FOX = C_GATE2 + 1
C_FOXOUT = C_FOX + 3 * KT
C_UP2 = C_FOXOUT + KT
C_DOWN2 = C_UP2 + 2 * FT
C_HG = C_DOWN2 + 3 * KT
C_HGOUT = C_HG + 4 * HG_H
C_UP3 = C_HGOUT + KT
C_DOWN3 = C_UP3 + 2 * FT
C_END = C_DOWN3 + 3 * KT
RAW, SPLIT = 4, 2
DOWN_K = (8, 8, 6)
ADA_COLS = 256
ADA_FIRST, ADA_ALL = 2 * D // ADA_COLS, 6 * D // ADA_COLS

HEAD_COLS = 2 * CV_TAPS + 2 + 4 * QK_TAPS + 4 + 2
FF_COLS = 2 * FF_TAPS + 2
_widths = [("c", KT), ("ada_b", 48), ("mix_pre", KT), ("mix_post", KT), ("gate1_b", 1), ("head", H1 * HEAD_COLS),
           ("ln_g", KT), ("ln_b", KT), ("ffn_pre", KT), ("ffn_post", KT), ("ff", FT * FF_COLS), ("fox_b", 1),
           ("lb", 24), ("gnorm", 1), ("gains", 64)]
COL, _at = {}, 0
for _name, _w in _widths:
    COL[_name] = _at
    _at += _w
NPRM = _at
HP_CVW, HP_CVB, HP_QKW, HP_QKB, HP_G = 0, 62, 64, 80, 84


class Steps:

    def __init__(self, ctx, nc, name, steps, credit=0):
        self.sem = ctx.enter_context(nc.semaphore(name))
        self.steps, self.n, self.credit, self.next = steps, len(steps), credit, 0

    def at(self, step, turn=0):
        return (turn + self.credit) * self.n + self.steps.index(step) + 1

    def open(self, eng):
        if self.credit:
            eng.sem_inc(self.sem, self.credit * self.n)

    def skip(self, eng, turn, *steps):
        eng.wait_ge(self.sem, self.at(steps[0], turn) - 1)
        for step in steps:
            assert self.steps[self.next] == step, (self.steps[self.next], step)
            self.next = (self.next + 1) % self.n
        eng.sem_inc(self.sem, len(steps))

    def did(self, ins, step):
        assert self.steps[self.next] == step, (self.steps[self.next], step)
        self.next = (self.next + 1) % self.n
        ins.then_inc(self.sem, 1)


def build(nc, xT, wstream, ada, params, outT, rows1, rows2):
    f32, f32r, bf16, i32 = mybir.dt.float32, mybir.dt.float32r, mybir.dt.bfloat16, mybir.dt.int32
    ALU, ACT = mybir.AluOpType, mybir.ActivationFunctionType
    ctx = ExitStack()
    ctx.__enter__()

    here = [(nc.sbuf_base + 31) // 32 * 32]

    def place(name, cols, dt=f32, shape=None):
        size = (cols * (2 if dt == bf16 else 4) + 31) // 32 * 32
        t = nc.alloc_sbuf_tensor_at(name, [P] + (shape or [cols]), dt, offset=here[0])
        here[0] += size
        return t

    x = place("x", KT * T, shape=[KT, T])
    raw = [place(f"raw{i}", D) for i in range(RAW)]
    w_hi = [place(f"w_hi{i}", D, f32r) for i in range(SPLIT)]
    w_lo = [place(f"w_lo{i}", D, f32r) for i in range(SPLIT)]
    prm = place("prm", NPRM)
    mod = place("mod", 48)
    cvec = place("cvec", KT)
    col_a = place("col_a", 6 * KT)
    zero_col = place("zero_col", KT)
    eps_col = place("eps_col", 2)
    ones = place("ones", P)
    ident = place("ident", P)
    ident_b = place("ident_b", P, bf16)
    late_b = place("late_b", P, bf16)
    early = place("early", P)
    levels = place("levels", 8 * P, i32, [8, P])
    u_hi = place("u_hi", KT * T, f32r, [KT, T])
    u_lo = place("u_lo", KT * T, f32r, [KT, T])
    sq = [place(f"sq{i}", T) for i in range(2)]
    acc = place("acc", T)
    var = place("var", T)
    rstd = place("rstd", T)
    mix_at = here[0]
    m = place("m", KT * T, shape=[KT, T])
    mix_end = here[0]
    phase_at = here[0]

    hm = place("hm", KT * T, shape=[KT, T])
    y = place("y", KT * T, shape=[KT, T])
    tmp_at = here[0]
    qk_raw = place("qk_raw", 4 * (T + 3), shape=[4, T + 3])
    qk = place("qk", 4 * T, shape=[4, T])
    vf = place("vf", 2 * T, shape=[2, T])
    vt = place("vt", 2 * T, shape=[2, NT, P])
    so = place("so", 2 * T, shape=[2, T])
    ypad = [place(f"ypad{i}", T + 30) for i in range(2)]
    sg = [place(f"sg{i}", T) for i in range(2)]
    bc = place("bc", 2 * T, shape=[2, T])
    dg = place("dg", T, shape=[NT, P])
    WOFF = [0, 512, 896, 1152]
    wt = place("wt", 1280)
    sp = place("sp", 1280)
    hp = place("hp", HEAD_COLS)
    dcol = place("dcol", 16, shape=[H1, NT])
    dcur = place("dcur", NT)
    top = here[0]
    here[0] = mix_at
    rz, rlf, rb, rm, rA, rD = [place(n, T) for n in ("rz", "rlf", "rb", "rm", "rA", "rD")]
    cA, cB = [place(n, T) for n in ("cA", "cB")]
    assert here[0] <= mix_end
    here[0] = tmp_at
    y_hi = place("y_hi", KT * T, f32r, [KT, T])
    y_lo = place("y_lo", KT * T, f32r, [KT, T])
    ada_buf = [place(f"ada_buf{i}", KT * ADA_COLS, shape=[KT, ADA_COLS]) for i in range(2)]
    ada_acc = place("ada_acc", 4 * ADA_COLS, shape=[4, ADA_COLS])
    top = max(top, here[0])
    here[0] = phase_at
    f_hi = place("f_hi", FT * T, f32r, [FT, T])
    f_lo = place("f_lo", FT * T, f32r, [FT, T])
    fprm = place("fprm", FF_COLS)
    top = max(top, here[0])
    here[0] = mix_at
    fraw = [place(f"fraw{i}", T + 2) for i in range(2)]
    fcv = [place(f"fcv{i}", T) for i in range(2)]
    fsi = place("fsi", T)
    fval = place("fval", T)
    assert here[0] <= mix_end
    here[0] = phase_at
    a_hi = place("a_hi", KT * T, f32r, [KT, T])
    a_lo = place("a_lo", KT * T, f32r, [KT, T])
    q_hi, q_lo, k_hi, k_lo = [place(n, T, f32r) for n in ("q_hi", "q_lo", "k_hi", "k_lo")]
    fv = place("fv", T)
    va_hi = place("va_hi", 8 * P, f32r, [2, NT, P])
    va_lo = place("va_lo", 8 * P, f32r, [2, NT, P])
    pr = [place(f"pr{i}", T) for i in range(2)]
    pt_hi = [place(f"pt_hi{i}", NT * T, f32r, [NT, T]) for i in range(2)]
    pt_lo = [place(f"pt_lo{i}", NT * T, f32r, [NT, T]) for i in range(2)]
    mx = place("mx", 2)
    top = max(top, here[0])
    here[0] = mix_at
    cbc = place("cbc", 2 * T, shape=[2, T])
    lg = [place(f"lg{i}", T) for i in range(2)]
    rs = place("rs", T)
    fo = place("fo", T)
    assert here[0] <= mix_end
    here[0] = mix_at
    fz, fl, fc, one_row = [place(n, T) for n in ("fz", "fl", "fc", "one_row")]
    here[0] = phase_at
    g_hi = place("g_hi", KT * T, f32r, [KT, T])
    g_lo = place("g_lo", KT * T, f32r, [KT, T])
    hq, hk, hf, hb, hv, hs = [place(n, T) for n in ("hq", "hk", "hf", "hb", "hv", "hs")]
    hvt = place("hvt", T, shape=[NT, P])
    he = [place(f"he{i}", T) for i in range(2)]
    hl = [place(f"hl{i}", T) for i in range(2)]
    hqd, hkd = place("hqd", T), place("hkd", T)
    hkx = place("hkx", 3 * P, shape=[3, P])
    hsc = place("hsc", NT * T, shape=[NT, T])
    ho, ho2 = place("ho", T), place("ho2", T)
    het = place("het", NT)
    lbcur = place("lbcur", 2)
    top = max(top, here[0])
    assert top <= nc.sbuf_usable_end, (top, nc.sbuf_usable_end)

    ps = [ctx.enter_context(nc.psum_tensor(f"ps{i}", [P, T], f32)) for i in range(8)]

    def sem(name):
        return ctx.enter_context(nc.semaphore(name))

    raw_landed = [sem(f"raw_landed{i}") for i in range(RAW)]
    chunk_hi, chunk_split, gemm_done = sem("chunk_hi"), sem("chunk_split"), sem("gemm_done")
    ff1_pads = sem("ff1_pads")
    ada_landed = [sem(f"ada_landed{i}") for i in range(2)]
    x_landed, prm_landed, const_ready = sem("x_landed"), sem("prm_landed"), sem("const_ready")
    turn_waited = sem("turn_waited")
    rows_out, bc_landed, out_landed = sem("rows_out"), sem("bc_landed"), sem("out_landed")

    ADA_BODY = 4
    s_ada = Steps(ctx, nc, "ada_dve", [f"piece{i}" for i in range(ADA_BODY)] + ["mod"], credit=1)
    p_ada = Steps(ctx, nc, "ada_pe", ["sums"])
    v_set = Steps(ctx, nc, "setup_dve", ["c", "xor", "float", "causal"] + [f"ge{i}" for i in range(7)] + [f"lv{i}" for i in range(8)])
    a_set = Steps(ctx, nc, "setup_act", ["sig_c"])
    v_col = Steps(ctx, nc, "cols_dve", ["a1", "g1", "a2", "g2"])

    class Norm:

        def __init__(self, name, post, pre):
            self.post, self.pre = post, pre
            if post:
                self.pe1 = Steps(ctx, nc, name + "_pe1", ["sum"])
                self.a1 = Steps(ctx, nc, name + "_act1", ["sd"])
                self.v1 = Steps(ctx, nc, name + "_dve1", ["var", "rstd"])
                self.vx = Steps(ctx, nc, name + "_dvex", ["t", "x"])
            if pre:
                self.asq = Steps(ctx, nc, name + "_actsq", ["sq"])
                self.pe2 = Steps(ctx, nc, name + "_pe2", ["sum"])
                self.a2 = Steps(ctx, nc, name + "_act2", ["sd"])
                self.v2 = Steps(ctx, nc, name + "_dve2", ["var", "rstd"])
                self.vt = Steps(ctx, nc, name + "_dvet", ["t"])
                self.ah = Steps(ctx, nc, name + "_acthi", ["hi"])
                self.vl = Steps(ctx, nc, name + "_dvelo", ["lo"])

    norms = [Norm("n0", False, True)] + [Norm(f"n{i}", True, i < 6) for i in range(1, 7)]

    class OutGemm:
        def __init__(self, name):
            self.act = Steps(ctx, nc, name + "_act", ["copy", "sq"], credit=2)
            self.dve = Steps(ctx, nc, name + "_dve", ["acc"], credit=2)

    outs = [OutGemm(f"og{i}") for i in range(6)]

    def matmuls(out, pairs, n_inc=None, start=True, stop=True):
        last = None
        for i, (a, b) in enumerate(pairs):
            last = nc.tensor.matmul(out, a, b, start=(start and i == 0), stop=(stop and i == len(pairs) - 1))
        return last

    def tri(ah, al, bh, bl):
        return [(ah, bh), (ah, bl), (al, bh)]

    def gemm_chunk(pe, chunk, slot, out, hi, lo, k0, nk, start, stop, tile_wait=None, hook=None):
        pe.wait_ge(chunk_split, chunk + 1)
        last = None
        for k in range(nk):
            if tile_wait:
                tile_wait(k0 + k)
            wh, wl = w_hi[slot][:, k * P:(k + 1) * P], w_lo[slot][:, k * P:(k + 1) * P]
            for i, (a, b) in enumerate(tri(wh, wl, hi(k), lo(k))):
                last = nc.tensor.matmul(out, a, b, start=(start and k == 0 and i == 0),
                                        stop=(stop and k == nk - 1 and i == 2))
            if k == nk - 1:
                last.then_inc(gemm_done, 1)
            if hook:
                hook(k)

    def u_tiles(k):
        return u_hi[:, k, :]

    def u_lows(k):
        return u_lo[:, k, :]

    def norm_pe(pe, N, og):
        if N.post:
            pe.wait_ge(og.dve.sem, og.dve.at("acc", KT - 1))
            N.pe1.did(nc.tensor.matmul(ps[5][:], ones[:], acc[:], start=True, stop=True), "sum")
        if N.pre:
            for n in range(KT):
                pe.wait_ge(N.asq.sem, N.asq.at("sq", n))
                N.pe2.did(nc.tensor.matmul(ps[7][:], ones[:], sq[n % 2][:], start=(n == 0), stop=(n == KT - 1)), "sum")

    def norm_act(act, N, shift):
        if N.post:
            act.wait_ge(N.v1.sem, N.v1.at("var"))
            N.a1.did(nc.scalar.activation(rstd[:], var[:], ACT.Sqrt), "sd")
        if N.pre:
            for n in range(KT):
                if N.post:
                    act.wait_ge(N.vx.sem, N.vx.at("x", n))
                elif n == 0:
                    act.wait_ge(x_landed, 16)
                if n >= 2:
                    act.wait_ge(N.pe2.sem, N.pe2.at("sum", n - 2))
                N.asq.did(nc.scalar.activation(sq[n % 2][:], x[:, n, :], ACT.Square), "sq")
            act.wait_ge(N.v2.sem, N.v2.at("var"))
            N.a2.did(nc.scalar.activation(rstd[:], var[:], ACT.Sqrt), "sd")
            for n in range(KT):
                act.wait_ge(N.vt.sem, N.vt.at("t", n))
                N.ah.did(nc.scalar.activation(u_hi[:, n, :], sq[n % 2][:], ACT.Identity, bias=shift(n)), "hi")

    def norm_dve(dve, N, gain, scale, shift, wait_cols=None):
        if N.post:
            dve.wait_ge(N.pe1.sem, N.pe1.at("sum"))
            N.v1.did(nc.vector.tensor_scalar(var[:], ps[5][:], 1.0 / D, EPS, ALU.mult, ALU.add), "var")
            dve.wait_ge(N.a1.sem, N.a1.at("sd"))
            N.v1.did(nc.vector.reciprocal(rstd[:], rstd[:]), "rstd")
            dve.wait_ge(N.v1.sem, N.v1.at("rstd"))

            def add(n):
                dve.wait_ge(N.vx.sem, N.vx.at("t", n))
                N.vx.did(nc.vector.scalar_tensor_tensor(x[:, n, :], m[:, n, :], gain(n), x[:, n, :],
                                                        ALU.mult, ALU.add), "x")

            for n in range(KT):
                N.vx.did(nc.vector.tensor_tensor(m[:, n, :], m[:, n, :], rstd[:], ALU.mult), "t")
                add(n)
        if N.pre:
            dve.wait_ge(N.pe2.sem, N.pe2.at("sum", KT - 1))
            N.v2.did(nc.vector.tensor_scalar(var[:], ps[7][:], 1.0 / D, EPS, ALU.mult, ALU.add), "var")
            dve.wait_ge(N.a2.sem, N.a2.at("sd"))
            N.v2.did(nc.vector.reciprocal(rstd[:], rstd[:]), "rstd")
            if wait_cols:
                wait_cols()
            dve.wait_ge(N.v2.sem, N.v2.at("rstd"))

            def low(n):
                dve.wait_ge(N.ah.sem, N.ah.at("hi", n))
                N.vl.did(nc.vector.scalar_tensor_tensor(u_lo[:, n, :], sq[n % 2][:], shift(n),
                                                        u_hi[:, n, :].bitcast(f32), ALU.add, ALU.subtract), "lo")

            for n in range(KT):
                if n >= 2:
                    low(n - 2)
                    dve.wait_ge(N.vl.sem, N.vl.at("lo", n - 2))
                N.vt.did(nc.vector.scalar_tensor_tensor(sq[n % 2][:], x[:, n, :], scale(n), rstd[:],
                                                        ALU.mult, ALU.mult), "t")
            low(KT - 2)
            low(KT - 1)

    def out_pe(pe, og, base, ks, hi, lo, first=None, extra=None):
        nch = len(ks)
        og_body = 2
        with pe.Fori(0, KT // og_body) as it:
            for s in range(og_body):
                pe.wait_ge(og.act.sem, og.act.at("sq", og_body * it + s - 2))
                for j, nk in enumerate(ks):
                    c = s * nch + j
                    gemm_chunk(pe, base + og_body * nch * it + c, (base + c) % SPLIT, ps[s][:],
                               lambda k, j=j: hi(8 * j + k), lambda k, j=j: lo(8 * j + k), 0, nk,
                               j == 0, j == nch - 1)
            if extra:
                extra(it)

    def out_act(act, og, base, ks):
        nch = len(ks)
        og.act.open(act)
        with act.Fori(0, KT // 2) as it:
            for s in range(2):
                act.wait_ge(gemm_done, base + 2 * nch * it + (s + 1) * nch)
                og.act.did(nc.scalar.activation(m[:, bass.ds(2 * it + s, 1), :], ps[s][:], ACT.Identity), "copy")
                act.wait_ge(og.dve.sem, og.dve.at("acc", 2 * it + s - 2))
                og.act.did(nc.scalar.activation(sq[s][:], ps[s][:], ACT.Square), "sq")

    def out_dve(dve, og, before=None, after=None):
        nc.vector.memset(acc[:], 0.0).then_inc(og.dve.sem, og.dve.credit * og.dve.n)
        with dve.Fori(0, KT // 2) as it:
            if before:
                before(it)
            for s in range(2):
                dve.wait_ge(og.act.sem, og.act.at("sq", 2 * it + s))
                dve.wait_ge(og.dve.sem, og.dve.at("acc", 2 * it + s - 1))
                og.dve.did(nc.vector.tensor_tensor(acc[:], acc[:], sq[s][:], ALU.add), "acc")
            if after:
                after(it)

    def prm_col(name, i=0):
        return prm[:, COL[name] + i:COL[name] + i + 1]

    def ada_dve_pieces(dve, turn):
        for s in range(ADA_BODY):
            b = s % 2
            dve.wait_ge(ada_landed[b], 32 * turn + 16 * (s // 2) + 16)
            for k in range(KT):
                if k == 0:
                    ins = nc.vector.tensor_scalar(ada_acc[:, s, :], ada_buf[b][:, 0, :], cvec[:, 0:1], None, ALU.mult)
                else:
                    dve.wait_ge(ada_link.sem, ada_link.at(f"l{s}{k - 1}", turn))
                    ins = nc.vector.scalar_tensor_tensor(ada_acc[:, s, :], ada_buf[b][:, k, :], cvec[:, k:k + 1],
                                                         ada_acc[:, s, :], ALU.mult, ALU.add)
                if k < KT - 1:
                    ada_link.did(ins, f"l{s}{k}")
                else:
                    s_ada.did(ins, f"piece{s}")

    ada_link = Steps(ctx, nc, "ada_link", [f"l{s}{k}" for s in range(ADA_BODY) for k in range(KT - 1)])

    def ada_dve_mod(dve, turn):
        dve.wait_ge(p_ada.sem, p_ada.at("sums", turn))
        n = ADA_BODY * ADA_COLS // P
        s_ada.did(nc.vector.tensor_tensor(mod[:, bass.ds(n * turn, n)], ps[6][:, 0:n],
                                          prm[:, bass.ds(COL["ada_b"] + n * turn, n)], ALU.add), "mod")

    def ada_pe(pe, turn):
        pe.wait_ge(s_ada.sem, s_ada.at("mod", turn - 1))
        pe.wait_ge(s_ada.sem, s_ada.at(f"piece{ADA_BODY - 1}", turn))
        last = None
        for s in range(ADA_BODY):
            for h in range(ADA_COLS // P):
                j = s * (ADA_COLS // P) + h
                last = nc.tensor.matmul(ps[6][:, j:j + 1], ada_acc[:, s, h * P:(h + 1) * P], ones[:, 0:1],
                                        start=True, stop=True)
        p_ada.did(last, "sums")

    v_gate = Steps(ctx, nc, "gate_dve", ["one", "zi", "zf", "lf", "b", "m", "A", "D", "dcol", "pad", "ysum0"])
    a_gate = Steps(ctx, nc, "gate_act", ["abs", "exp", "ln", "E"])
    p_gate = Steps(ctx, nc, "gate_pe", ["dT"])
    cv = lambda i: [f"cv{i}_{j}" for j in range(CV_TAPS)] + [f"y{i}", f"ys{i}"]
    c4 = [f"c{pr_}{j}_{t}" for pr_ in "qk" for t in range(QK_TAPS) for j in range(2)]
    v_mix = Steps(ctx, nc, "mix_dve", ["hp", "dc", "diag", "gt0", "gt1"] + cv(0) + c4 + cv(1)
                  + [f"sp{i}" for i in range(NT)]
                  + ["dm", "dn", "r", "r2", "vr", "rs", "q", "h0", "h1", "hg0", "hg1"], credit=1)
    a_mix = Steps(ctx, nc, "mix_act", ["sg0", "sg1"] + [f"dg{i}" for i in range(NT)] + [f"off{i}" for i in range(NT - 1)]
                  + ["rq0", "rq1", "rk0", "rk1", "v0", "v1", "so0", "so1", "sq0", "sq1", "sk0", "sk1",
                     "vt0", "vt1", "n0", "n1", "sd"], credit=1)
    p_mix = Steps(ctx, nc, "mix_pe", ["vt0", "vt1", "qk0", "qk1", "qk2", "qk3", "den", "num0", "num1", "hs"], credit=1)
    p_ln = Steps(ctx, nc, "ln_pe", ["mu"] + [f"s{n}" for n in range(KT)])
    a_ln = Steps(ctx, nc, "ln_act", [f"hh{n}" for n in range(KT)] + [f"sq{n}" for n in range(KT)] + ["sd"]
                 + [x_ for n in range(KT) for x_ in (f"silu{n}", f"hi{n}")])
    v_ln = Steps(ctx, nc, "ln_dve", [f"hl{n}" for n in range(KT)] + ["mu"] + [f"yc{n}" for n in range(KT)]
                 + ["var", "rstd"] + [f"t{n}" for n in range(KT)] + [f"lo{n}" for n in range(KT)])

    a_ff1 = Steps(ctx, nc, "ff1_act", ["g", "a", "silu", "hi"], credit=2)
    ff_c = [f"{n}{t}" for t in range(FF_TAPS) for n in "ga"]
    v_ff1 = Steps(ctx, nc, "ff1_dve", ["prm"] + ff_c + ["f", "lo"], credit=2)
    a_ff = [Steps(ctx, nc, f"ff{i}_act", ["silu", "hi"], credit=2) for i in (2, 3)]
    v_ff = [Steps(ctx, nc, f"ff{i}_dve", ["f", "lo"], credit=2) for i in (2, 3)]

    v_fg = Steps(ctx, nc, "fg_dve", ["one", "z", "lf", "c", "ones_hi", "ones_lo"])
    a_fg = Steps(ctx, nc, "fg_act", ["abs", "exp", "ln"])
    U = 2 * NT
    lagged = lambda first, then: [f"{first}0"] + [x_ for n in range(U) for x_ in
                                                  ([f"{first}{n + 1}"] if n + 1 < U else []) + [f"{then}{n}"]]
    v_fox0 = Steps(ctx, nc, "fox0_dve", ["ql", "kl"])
    a_fox0 = Steps(ctx, nc, "fox0_act", ["q", "k", "v"])
    v_fox = Steps(ctx, nc, "fox_dve", ["vl0", "vl1"] + lagged("N", "pl") + ["ql", "kl", "recip", "o0", "o1", "lo"], credit=1)
    a_fox = Steps(ctx, nc, "fox_act", ["vh0", "vh1"] + lagged("e", "ph") + ["q", "k", "v", "rs0", "rs1", "hi"], credit=1)
    fox_pe_steps = ["vT", "L0"]
    for n in range(U):
        fox_pe_steps += ([f"L{n + 1}"] if n + 1 < U else []) + [f"T{n}"] + (["pv0"] if n == NT + 1 else [])
    p_fox = Steps(ctx, nc, "fox_pe", fox_pe_steps + ["pv1"], credit=1)

    LEVELS = [64, 32, 16, 8, 4, 2, 1]
    v_hg0 = Steps(ctx, nc, "hgs_dve", ["mx", "mx2", "d0", "d1", "d2", "s", "s2", "r", "lb", "oml", "zero"])
    a_hg0 = Steps(ctx, nc, "hgs_act", ["e0", "e1", "e2", "q", "sig", "v", "g"])
    hg_steps = ["cur", "f", "k"] + [f"b{j}" for j in range(NT)] + ["dl64", "dr64"]
    for i, w in enumerate(LEVELS):
        if i + 1 < len(LEVELS):
            hg_steps += [f"dl{LEVELS[i + 1]}", f"dr{LEVELS[i + 1]}"]
        hg_steps += [f"ml{w}", f"mr{w}"]
        if i:
            hg_steps += [f"pc{LEVELS[i - 1]}"]
    v_hg = Steps(ctx, nc, "hg_dve", hg_steps + ["qd", "kd", "x20", "x31", "x30", "pc1", "pc0", "vr", "rstd", "o1", "o2",
                                                "lo"], credit=1)
    a_hg = Steps(ctx, nc, "hg_act", ["ln", "vt"] + [f"e{w}" for w in LEVELS] + ["et", "eb"]
                 + [f"ek{j}" for j in range(NT - 1)] + ["offA", "offB0", "offB1", "q", "sig", "v", "osq", "sd", "hi", "g"],
                 credit=1)
    p_hg = Steps(ctx, nc, "hg_pe", ["vT"] + [f"S{w}" for w in LEVELS] + ["S0", "offA", "offB", "pv", "ss"], credit=1)

    block = ctx.enter_context(nc.Block())

    @block.sync
    def _(sp_):
        sp_.dma_start(prm[:], params).then_inc(prm_landed, 16)
        sp_.dma_start(x[:], xT).then_inc(x_landed, 16)

        def load_ada(piece, s):
            src = ada[piece] if isinstance(piece, int) else ada[bass.ds(piece, 1), :, :].rearrange("o p c -> (o p) c")
            sp_.dma_start(ada_buf[s][:].rearrange("p k c -> p (k c)"), src).then_inc(ada_landed[s], 16)

        for p in range(ADA_FIRST):
            if p >= 2:
                sp_.wait_ge(s_ada.sem, s_ada.at(f"piece{(p - 2) % ADA_BODY}", (p - 2) // ADA_BODY))
            load_ada(p, p % 2)

        def load_chunk(c, slot, wait=True):
            if wait:
                sp_.wait_ge(chunk_split, c - RAW + 1)
            src = wstream[c] if isinstance(c, int) else wstream[bass.ds(c, 1), :, :].rearrange("o p c -> (o p) c")
            sp_.dma_start(raw[slot][:], src).then_inc(raw_landed[slot], 16)

        for c in range(RAW):
            load_chunk(c, c, wait=False)
        with sp_.Fori(1, C_WOUT1 // RAW) as it:
            for s in range(RAW):
                load_chunk(RAW * it + s, s)
        for c in range(C_WOUT1 // RAW * RAW, C_WOUT1):
            load_chunk(c, c % RAW)
        with sp_.Fori(0, 2 * KT // RAW) as it:
            for s in range(RAW):
                load_chunk(C_WOUT1 + RAW * it + s, (C_WOUT1 + s) % RAW)
                turn = ADA_FIRST // ADA_BODY + it
                if s >= 2:
                    sp_.wait_ge(s_ada.sem, s_ada.at(f"piece{s - 2}", turn))
                else:
                    sp_.wait_ge(s_ada.sem, s_ada.at(f"piece{s + 2}", turn - 1))
                    if s == 0 or s == 1:
                        sp_.wait_ge(v_ln.sem, v_ln.at("mu"))
                load_ada(ADA_FIRST + ADA_BODY * it + s, s % 2)
        rest = C_WOUT1 + 2 * KT
        with sp_.Fori(0, (C_END - rest) // RAW) as it:
            for s in range(RAW):
                load_chunk(rest + RAW * it + s, (rest + s) % RAW)
        for c in range(rest + (C_END - rest) // RAW * RAW, C_END):
            load_chunk(c, c % RAW)

    @block.gpsimd
    def _(pool):
        g = nc.gpsimd
        g.memset(ones[:], 1.0).then_inc(const_ready, 1)
        g.memset(ident[:], 0.0).then_inc(const_ready, 1)
        g.memset(early[:], 0.0).then_inc(const_ready, 1)
        g.memset(late_b[:], 0.0).then_inc(const_ready, 1)
        g.memset(ident_b[:], 0.0).then_inc(const_ready, 1)
        g.memset(zero_col[:], 0.0).then_inc(const_ready, 1)
        g.memset(eps_col[:], EPS).then_inc(const_ready, 1)
        pool.wait_ge(const_ready, 7)
        for t in (ident, ident_b):
            g.affine_select(out=t[:], in_=t[:], compare_op=ALU.not_equal, fill=1.0, base=0, pattern=[[-1, P]],
                            channel_multiplier=1).then_inc(const_ready, 1)
        g.affine_select(out=early[:], in_=early[:], compare_op=ALU.is_ge, fill=-BIG, base=0, pattern=[[1, P]],
                        channel_multiplier=-1).then_inc(const_ready, 1)
        g.affine_select(out=late_b[:], in_=late_b[:], compare_op=ALU.is_ge, fill=BIG, base=0, pattern=[[-1, P]],
                        channel_multiplier=1).then_inc(const_ready, 1)
        g.iota(levels[:, 0, :], pattern=[[0, P]], base=0, channel_multiplier=1).then_inc(const_ready, 1)
        g.iota(levels[:, 1, :], pattern=[[1, P]], base=0, channel_multiplier=0).then_inc(const_ready, 1)

        def split(c, rslot, slot, landed, wait=True):
            pool.wait_ge(raw_landed[rslot], landed)
            if wait:
                pool.wait_ge(gemm_done, c - SPLIT + 1)
            g.tensor_tensor(w_hi[slot][:], raw[rslot][:], ones[:, 0:1].to_broadcast([P, D]),
                            ALU.mult).then_inc(chunk_hi, 1)
            pool.wait_ge(chunk_hi, c + 1)
            g.tensor_tensor(w_lo[slot][:], raw[rslot][:], w_hi[slot][:].bitcast(f32),
                            ALU.subtract).then_inc(chunk_split, 1)

        for c in range(RAW):
            split(c, c, c % SPLIT, 16, wait=c >= SPLIT)
        with pool.Fori(1, C_END // RAW) as it:
            for s in range(RAW):
                split(RAW * it + s, s, s % SPLIT, 16 * it + 16)
        for c in range(C_END // RAW * RAW, C_END):
            split(c, c % RAW, c % SPLIT, 16 * (c // RAW + 1))

    @block.tensor
    def _(pe):
        pe.wait_ge(const_ready, 13)
        pe.wait_ge(v_set.sem, v_set.at("c"))
        norm_pe(pe, norms[0], None)
        for turn in range(ADA_FIRST // ADA_BODY):
            ada_pe(pe, turn)

        N0 = norms[0]
        gemm_chunk(pe, C_GATE1, 0, ps[5][:], u_tiles, u_lows, 0, KT, True, True,
                   tile_wait=lambda k: pe.wait_ge(N0.vl.sem, N0.vl.at("lo", k)))
        pe.wait_ge(v_gate.sem, v_gate.at("D"))
        for st in range(NT):
            last = nc.tensor.matmul(ps[4][:, st * H1:(st + 1) * H1], rD[0:H1, st * P:(st + 1) * P],
                                    ident[0:H1, 0:H1], start=True, stop=True)
        p_gate.did(last, "dT")

        p_mix.open(pe)
        with pe.Fori(0, H1) as h:
            before = {0: (a_mix, "v0", -1), 1: (a_mix, "v1", -1), 2: (a_mix, "so0", -1), 3: (a_mix, "so1", -1),
                      4: (a_mix, "sg0", 0), 5: (v_mix, "gt0", 0), 6: (a_mix, "sg1", 0), 7: (v_mix, "gt1", 0),
                      8: (a_mix, "rq0", 0), 9: (a_mix, "rq1", 0), 10: (a_mix, "rk0", 0), 11: (a_mix, "rk1", 0)}
            for j in range(12):
                S, step, back = before[j]
                pe.wait_ge(S.sem, S.at(step, h + back))
                gemm_chunk(pe, C_MIX + 12 * h + j, (C_MIX + j) % SPLIT, ps[j % 4][:], u_tiles, u_lows, 0, KT, True, True)
            pe.wait_ge(v_mix.sem, v_mix.at("hg1", h - 1))
            for e in range(2):
                pe.wait_ge(a_mix.sem, a_mix.at(f"v{e}", h))
                for st in range(NT):
                    last = nc.tensor.transpose(ps[4 + e][:, st * P:(st + 1) * P], vf[:, e, st * P:(st + 1) * P], ident[:])
                p_mix.did(last, f"vt{e}")
            bank = [6, 7, 4, 5]
            pe.wait_ge(a_mix.sem, a_mix.at("sk1", h))
            for st in range(NT):
                if st >= 2:
                    pe.wait_ge(a_mix.sem, a_mix.at(f"vt{st - 2}", h))
                p_mix.did(matmuls(ps[bank[st]][:, 0:T - st * P],
                                  [(qk[:, 2 + e, st * P:(st + 1) * P], qk[:, e, st * P:T]) for e in range(2)]), f"qk{st}")
            pe.wait_ge(v_mix.sem, v_mix.at(f"sp{NT - 1}", h))
            for name, b, w in (("den", 7, None), ("num0", 6, 0), ("num1", 4, 1)):
                for st in range(NT):
                    last = nc.tensor.matmul(ps[b][:, st * P:T], ones[:] if w is None else vt[:, w, st, :],
                                            sp[:, WOFF[st]:WOFF[st] + T - st * P], start=(st == 0), stop=(st == NT - 1))
                p_mix.did(last, name)
            for e in range(2):
                pe.wait_ge(a_mix.sem, a_mix.at(f"n{e}", h))
                last = nc.tensor.matmul(ps[5][:], ones[:], sq[e][:], start=(e == 0), stop=(e == 1))
            p_mix.did(last, "hs")

        pe.wait_ge(v_mix.sem, v_mix.at("hg1", H1 - 1))
        p_ln.did(nc.tensor.matmul(ps[4][:], ones[:], acc[:], start=True, stop=True), "mu")
        for n in range(KT):
            pe.wait_ge(a_ln.sem, a_ln.at(f"sq{n}"))
            p_ln.did(nc.tensor.matmul(ps[5][:], ones[:], sq[n % 2][:], start=(n == 0), stop=(n == KT - 1)), f"s{n}")
        pe.wait_ge(v_ln.sem, v_ln.at(f"lo{KT - 1}"))
        out_pe(pe, outs[0], C_WOUT1, (8, 8), lambda k: (u_hi if k < KT else y_hi)[:, k % KT, :],
               lambda k: (u_lo if k < KT else y_lo)[:, k % KT, :],
               extra=lambda it: ada_pe(pe, ADA_FIRST // ADA_BODY + it))

        def ffn_pe(N, base, dbase, read, og, prev):
            def read_wait(j, name, s):
                S, step = read[name]
                pe.wait_ge(S.sem, S.at(step, 2 * j + s - 2))
            pe.wait_ge(N.vl.sem, N.vl.at("lo", KT - 1))
            with pe.Fori(0, FT // 2) as it:
                for s in range(2):
                    for j, name in enumerate("ga"):
                        read_wait(it, name, s)
                        c = 2 * s + j
                        gemm_chunk(pe, base + 4 * it + c, (base + c) % SPLIT, ps[c][:], u_tiles, u_lows, 0, KT, True, True)
            S, step = prev
            pe.wait_ge(S.sem, S.at(step, FT - 1))
            out_pe(pe, og, dbase, DOWN_K, lambda k: f_hi[:, k, :], lambda k: f_lo[:, k, :])

        norm_pe(pe, norms[1], outs[0])
        ffn_pe(norms[1], C_UP1, C_DOWN1, {"g": (a_ff1, "g"), "a": (a_ff1, "a")}, outs[1], (v_ff1, "lo"))
        norm_pe(pe, norms[2], outs[1])

        N = norms[2]
        gemm_chunk(pe, C_GATE2, C_GATE2 % SPLIT, ps[3][:], u_tiles, u_lows, 0, KT, True, True,
                   tile_wait=lambda k: pe.wait_ge(N.vl.sem, N.vl.at("lo", k)))

        FOX_PAIRS = FOX_H // 2

        def fox_gemm(i, par, hook=lambda kk: None):
            for j, (S, step) in enumerate(((v_fox, "ql"), (v_fox, "kl"), (a_fox, "v"))):
                if not (isinstance(i, int) and i == 0):
                    pe.wait_ge(S.sem, S.at(step, i - 2))
                gemm_chunk(pe, C_FOX + 3 * i + j, (C_FOX + 3 * par + j) % SPLIT, ps[j][:], u_tiles, u_lows, 0, KT,
                           True, True, hook=lambda k, j=j: hook(KT * j + k))

        def fox_values(i):
            pe.wait_ge(a_fox.sem, a_fox.at("v", i - 1))
            pe.wait_ge(v_fox.sem, v_fox.at("o1", i - 1))
            for st in range(NT):
                last = nc.tensor.transpose(ps[3][:, st * P:(st + 1) * P], fv[:, st * P:(st + 1) * P], ident[:])
            p_fox.did(last, "vT")

        def fox_logits(i, n):
            a, r = divmod(n, NT)
            rows, qs, ks = slice(a * FOX_D, (a + 1) * FOX_D), slice(r * P, (r + 1) * P), slice(0, (r + 1) * P)
            if n == 0:
                pe.wait_ge(v_fox.sem, v_fox.at("kl", i - 1))
            if n >= 2:
                pe.wait_ge(v_fox.sem, v_fox.at(f"N{n - 2}", i))
            for j, (l_, r_) in enumerate(tri(q_hi[rows, qs], q_lo[rows, qs], k_hi[rows, ks], k_lo[rows, ks])):
                nc.tensor.matmul(ps[4 + n % 2][:, ks], l_, r_, start=(j == 0), stop=False)
            p_fox.did(nc.tensor.matmul(ps[4 + n % 2][:, qs], ident_b[:], late_b[:], start=False, stop=True), f"L{n}")

        def fox_turn(i, n):
            r = n % NT
            pe.wait_ge(a_fox.sem, a_fox.at(f"e{n}", i))
            if n >= 2:
                pe.wait_ge(v_fox.sem, v_fox.at(f"pl{n - 2}", i))
            for st in range(r + 1):
                last = nc.tensor.transpose(ps[6 + n % 2][:, st * P:(st + 1) * P], pr[n % 2][:, st * P:(st + 1) * P],
                                           ident[:])
            p_fox.did(last, f"T{n}")

        def fox_weigh(i, a):
            pe.wait_ge(v_fox.sem, v_fox.at(f"pl{NT * a + NT - 1}", i))
            for st in range(NT):
                ts = slice(st * P, T)
                for j, (l_, r_) in enumerate(tri(va_hi[:, a, st, :], va_lo[:, a, st, :], pt_hi[a][:, st, ts],
                                                 pt_lo[a][:, st, ts])):
                    last = nc.tensor.matmul(ps[3 + 4 * a][:, ts], l_, r_, start=(st == 0 and j == 0),
                                            stop=(st == NT - 1 and j == 2))
            p_fox.did(last, f"pv{a}")

        def fox_turn_pe(i, par, gemm=True):
            def hook(kk):
                if kk % 3 != 2:
                    return
                n = kk // 3
                if n + 1 < U:
                    fox_logits(i, n + 1)
                fox_turn(i, n)
                if n == NT + 1:
                    fox_weigh(i, 0)
            fox_values(i)
            fox_logits(i, 0)
            if gemm:
                fox_gemm(i + 1, par, hook)
            else:
                for kk in range(3 * KT):
                    hook(kk)
            fox_weigh(i, 1)

        p_fox.open(pe)
        fox_gemm(0, 0)
        pe.wait_ge(v_fg.sem, v_fg.at("ones_lo"))
        pe.wait_ge(v_fox0.sem, v_fox0.at("kl"))
        pe.wait_ge(a_fox0.sem, a_fox0.at("v"))
        with pe.Fori(0, FOX_PAIRS // 2 - 1) as it:
            for sub in range(2):
                fox_turn_pe(2 * it + sub, sub + 1)
        fox_turn_pe(FOX_PAIRS - 2, 1)
        fox_turn_pe(FOX_PAIRS - 1, 0, gemm=False)
        pe.wait_ge(v_fox.sem, v_fox.at("lo", FOX_PAIRS - 1))
        out_pe(pe, outs[2], C_FOXOUT, (KT,), lambda k: a_hi[:, k, :], lambda k: a_lo[:, k, :])
        norm_pe(pe, norms[3], outs[2])
        ffn_pe(norms[3], C_UP2, C_DOWN2, {"g": (a_ff[0], "silu"), "a": (v_ff[0], "f")}, outs[3], (v_ff[0], "lo"))
        norm_pe(pe, norms[4], outs[3])

        N4 = norms[4]

        def hg_gemm(i, hook=lambda kk: None):
            for j, step in enumerate(("q", "sig", "v", "g")):
                if not (isinstance(i, int) and i == 0):
                    pe.wait_ge(a_hg.sem, a_hg.at(step, i - 2))
                gemm_chunk(pe, C_HG + 4 * i + j, (C_HG + j) % SPLIT, ps[j][:], u_tiles, u_lows, 0, KT, True, True,
                           hook=lambda k, j=j: hook(KT * j + k))

        def hg_level(i, n):
            src = hl[n % 2] if n < len(LEVELS) else None
            b = 5 + n % 2
            if n >= 2:
                pe.wait_ge(v_hg.sem, v_hg.at(f"pc{LEVELS[n - 2]}", i))
            if src is not None:
                pe.wait_ge(v_hg.sem, v_hg.at(f"mr{LEVELS[n]}", i))
            for t in range(NT):
                ts = slice(t * P, (t + 1) * P)
                last = nc.tensor.matmul(ps[b][:, ts], (hk if src is None else src)[:, ts],
                                        (hq if src is None else src)[:, ts], start=True, stop=True)
            p_hg.did(last, f"S{LEVELS[n]}" if src is not None else "S0")

        def hg_off(i, which):
            tile_ = lambda t_, j: t_[:, j * P:(j + 1) * P]
            if which == "offA":
                pe.wait_ge(v_hg.sem, v_hg.at("x30", i))
                blocks_ = [(tile_(hkd, 0), 1), (hkx[:, 0, :], 2), (hkx[:, 2, :], 3)]
                bank_ = 7
            else:
                pe.wait_ge(a_hg.sem, a_hg.at("vt", i))
                blocks_ = [(tile_(hkd, 1), 2), (hkx[:, 1, :], 3), (tile_(hkd, 2), 3)]
                bank_ = 4
            for n, (l_, t) in enumerate(blocks_):
                last = nc.tensor.matmul(ps[bank_][:, n * P:(n + 1) * P], l_, tile_(hqd, t), start=True, stop=True)
            p_hg.did(last, which)

        def hg_weigh(i):
            pe.wait_ge(v_hg.sem, v_hg.at("pc0", i))
            pe.wait_ge(a_hg.sem, a_hg.at("offB1", i))
            for c in range(NT):
                last = nc.tensor.matmul(ps[5][:, c * P:T], hvt[:, c, :], hsc[:, c, c * P:T], start=(c == 0),
                                        stop=(c == NT - 1))
            p_hg.did(last, "pv")

        def hg_turn_pe(i, gemm=True):
            def hook(kk):
                n, rest_ = divmod(kk, 3)
                if rest_ != 2:
                    return
                if n < len(LEVELS) + 1:
                    hg_level(i, n)
                elif n == len(LEVELS) + 1:
                    hg_off(i, "offA")
                    hg_off(i, "offB")
            pe.wait_ge(a_hg.sem, a_hg.at("hi", i - 1))
            for st in range(NT):
                last = nc.tensor.transpose(ps[4][:, st * P:(st + 1) * P], hv[:, st * P:(st + 1) * P], ident[:])
            p_hg.did(last, "vT")
            if gemm:
                hg_gemm(i + 1, hook)
            else:
                for kk in range(4 * KT):
                    hook(kk)
            hg_weigh(i)
            pe.wait_ge(a_hg.sem, a_hg.at("osq", i))
            p_hg.did(nc.tensor.matmul(ps[6][:], ones[:], ho2[:], start=True, stop=True), "ss")

        p_hg.open(pe)
        pe.wait_ge(N4.vl.sem, N4.vl.at("lo", KT - 1))
        hg_gemm(0)
        pe.wait_ge(a_hg0.sem, a_hg0.at("g"))
        with pe.Fori(0, HG_H - 1) as i:
            hg_turn_pe(i)
        hg_turn_pe(HG_H - 1, gemm=False)
        pe.wait_ge(v_hg.sem, v_hg.at("lo", HG_H - 1))
        out_pe(pe, outs[4], C_HGOUT, (KT,), lambda k: g_hi[:, k, :], lambda k: g_lo[:, k, :])
        norm_pe(pe, norms[5], outs[4])
        ffn_pe(norms[5], C_UP3, C_DOWN3, {"g": (a_ff[1], "silu"), "a": (v_ff[1], "f")}, outs[5], (v_ff[1], "lo"))
        norm_pe(pe, norms[6], outs[5])

    @block.scalar
    def _(act):
        A = nc.scalar.activation
        act.wait_ge(prm_landed, 16)
        a_set.did(A(cvec[:], prm[:, COL["c"]:COL["c"] + KT], ACT.Sigmoid), "sig_c")
        act.wait_ge(const_ready, 13)
        norm_act(act, norms[0], lambda n: mod[:, n:n + 1])

        act.wait_ge(v_gate.sem, v_gate.at("zf"))
        a_gate.did(A(rb[0:H1, :], rlf[0:H1, :], ACT.Abs), "abs")
        act.wait_ge(a_gate.sem, a_gate.at("abs"))
        a_gate.did(A(rb[0:H1, :], rb[0:H1, :], ACT.Exp, scale=-1.0), "exp")
        act.wait_ge(a_gate.sem, a_gate.at("exp"))
        a_gate.did(A(rb[0:H1, :], rb[0:H1, :], ACT.Ln, bias=1.0), "ln")
        act.wait_ge(v_gate.sem, v_gate.at("A"))
        a_gate.did(A(rm[0:H1, :], rm[0:H1, :], ACT.Exp, scale=-1.0), "E")
        act.dma_start(rows1[0], rA[0:H1, :]).then_inc(rows_out, 16)
        act.wait_ge(a_gate.sem, a_gate.at("E"))
        act.dma_start(rows1[1], rm[0:H1, :]).then_inc(rows_out, 16)
        act.wait_ge(rows_out, 32)

        act.wait_ge(v_gate.sem, v_gate.at("ysum0"))
        a_mix.open(act)
        with act.Fori(0, H1) as h:
            act.wait_ge(v_mix.sem, v_mix.at("dn", h - 1))
            act.dma_start(bc[:], rows1[:, bass.ds(h, 1), :].rearrange("a h t -> h a t").to_broadcast([P, 2, T]))\
               .then_inc(bc_landed, 16)
            for j in range(2):
                act.wait_ge(gemm_done, C_MIX + 12 * h + 2 * j + 1)
                act.wait_ge(v_mix.sem, v_mix.at(f"gt{j}", h - 1))
                a_mix.did(A(sg[j][:], ps[2 * j][:], ACT.Sigmoid), f"sg{j}")
            act.wait_ge(v_mix.sem, v_mix.at("diag", h))
            act.wait_ge(bc_landed, 16 * h + 16)
            for st in range(NT):
                a_mix.did(A(wt[:, WOFF[st]:WOFF[st] + P], dg[:, st, :], ACT.Exp, bias=dcur[:, st:st + 1]), f"dg{st}")
            for st in range(NT - 1):
                a_mix.did(A(wt[:, WOFF[st] + P:WOFF[st] + T - st * P], bc[:, 0, (st + 1) * P:T], ACT.Exp,
                            bias=dcur[:, st:st + 1]), f"off{st}")
            for j, name in enumerate(("rq0", "rq1", "rk0", "rk1")):
                act.wait_ge(gemm_done, C_MIX + 12 * h + 4 + j + 1)
                if j == 0:
                    act.wait_ge(v_mix.sem, v_mix.at(f"ck1_{QK_TAPS - 1}", h - 1))
                a_mix.did(A(qk_raw[:, j, 3:], ps[j][:], ACT.Identity), name)
            for j in range(2):
                act.wait_ge(gemm_done, C_MIX + 12 * h + 8 + j + 1)
                if j == 0:
                    act.wait_ge(p_mix.sem, p_mix.at("vt1", h - 1))
                a_mix.did(A(vf[:, j, :], ps[j][:], ACT.Identity), f"v{j}")
            for j in range(2):
                act.wait_ge(gemm_done, C_MIX + 12 * h + 10 + j + 1)
                if j == 0:
                    act.wait_ge(v_mix.sem, v_mix.at("hg1", h - 1))
                a_mix.did(A(so[:, j, :], ps[2 + j][:], ACT.Sigmoid), f"so{j}")
            for j, name in enumerate(("sq0", "sq1", "sk0", "sk1")):
                act.wait_ge(v_mix.sem, v_mix.at(f"c{'qk'[j // 2]}{j % 2}_{QK_TAPS - 1}", h))
                a_mix.did(A(qk[:, j, :], qk[:, j, :], ACT.Silu, bias=hp[:, HP_QKB + j:HP_QKB + j + 1]), name)
            for e in range(2):
                act.wait_ge(p_mix.sem, p_mix.at(f"vt{e}", h))
                a_mix.did(A(vt[:, e, :, :], ps[4 + e][:], ACT.Identity), f"vt{e}")
            for e in range(2):
                act.wait_ge(p_mix.sem, p_mix.at(f"num{e}", h))
                a_mix.did(A(sq[e][:], ps[6 if e == 0 else 4][:], ACT.Square), f"n{e}")
            act.wait_ge(v_mix.sem, v_mix.at("vr", h))
            a_mix.did(A(cB[:], cA[:], ACT.Sqrt, bias=eps_col[:, 0:1]), "sd")

        act.wait_ge(v_mix.sem, v_mix.at("hg1", H1 - 1))
        for n in range(KT):
            a_ln.did(A(u_hi[:, n, :], hm[:, n, :], ACT.Identity), f"hh{n}")
        for n in range(KT):
            act.wait_ge(v_ln.sem, v_ln.at(f"yc{n}"))
            if n >= 2:
                act.wait_ge(p_ln.sem, p_ln.at(f"s{n - 2}"))
            a_ln.did(A(sq[n % 2][:], y[:, n, :], ACT.Square), f"sq{n}")
        act.wait_ge(v_ln.sem, v_ln.at("var"))
        a_ln.did(A(rstd[:], var[:], ACT.Sqrt), "sd")
        for n in range(KT):
            act.wait_ge(v_ln.sem, v_ln.at(f"t{n}"))
            a_ln.did(A(y[:, n, :], y[:, n, :], ACT.Silu, bias=prm_col("ln_b", n), scale=prm_col("ln_g", n)), f"silu{n}")
            act.wait_ge(a_ln.sem, a_ln.at(f"silu{n}"))
            a_ln.did(A(y_hi[:, n, :], y[:, n, :], ACT.Identity), f"hi{n}")
        out_act(act, outs[0], C_WOUT1, (8, 8))
        norm_act(act, norms[1], lambda n: mod[:, 24 + n:25 + n])

        act.wait_ge(ff1_pads, 2)
        a_ff1.open(act)
        with act.Fori(0, FT // 2) as it:
            for s in range(2):
                j = 2 * it + s
                for n, name in enumerate("ga"):
                    act.wait_ge(gemm_done, C_UP1 + 4 * it + 2 * s + n + 1)
                    act.wait_ge(v_ff1.sem, v_ff1.at(f"{name}{FF_TAPS - 1}", j - 1))
                    a_ff1.did(A(fraw[n][:, 2:], ps[2 * s + n][:], ACT.Identity), name)
                act.wait_ge(v_ff1.sem, v_ff1.at(f"g{FF_TAPS - 1}", j))
                a_ff1.did(A(fsi[:], fcv[0][:], ACT.Silu, bias=fprm[:, 6:7]), "silu")
                act.wait_ge(v_ff1.sem, v_ff1.at("f", j))
                a_ff1.did(A(f_hi[:, bass.ds(j, 1), :], fval[:], ACT.Identity), "hi")
        out_act(act, outs[1], C_DOWN1, DOWN_K)
        norm_act(act, norms[2], lambda n: zero_col[:, n:n + 1])

        act.wait_ge(v_fg.sem, v_fg.at("z"))
        a_fg.did(A(fl[0:FOX_H, :], fz[0:FOX_H, :], ACT.Abs), "abs")
        act.wait_ge(a_fg.sem, a_fg.at("abs"))
        a_fg.did(A(fl[0:FOX_H, :], fl[0:FOX_H, :], ACT.Exp, scale=-1.0), "exp")
        act.wait_ge(a_fg.sem, a_fg.at("exp"))
        a_fg.did(A(fl[0:FOX_H, :], fl[0:FOX_H, :], ACT.Ln, bias=1.0), "ln")
        act.wait_ge(v_fg.sem, v_fg.at("c"))
        act.dma_start(rows2, fc[0:FOX_H, :]).then_inc(rows_out, 16)
        act.wait_ge(rows_out, 48)

        def fox_round(S, i, what):
            j = "qkv".index(what)
            act.wait_ge(gemm_done, C_FOX + 3 * i + j + 1)
            if S is a_fox and what in "qk":
                act.wait_ge(p_fox.sem, p_fox.at(f"L{U - 1}", i - 1))
            if S is a_fox and what == "v":
                act.wait_ge(p_fox.sem, p_fox.at("vT", i - 1))
            if what == "q":
                ins = A(q_hi[:], ps[0][:], ACT.Identity, scale=-float(FOX_D) ** -0.5)
            else:
                ins = A({"k": k_hi, "v": fv}[what][:], ps[j][:], ACT.Identity)
            S.did(ins, what)

        def fox_cbc(i):
            act.dma_start(cbc[:], rows2[bass.ds(2 * i, 2), :].unsqueeze(0).to_broadcast([P, 2, T]) if not isinstance(i, int)
                          else rows2[2 * i:2 * i + 2, :].unsqueeze(0).to_broadcast([P, 2, T])).then_inc(bc_landed, 16)

        fox_cbc(0)
        for what in "qkv":
            fox_round(a_fox0, 0, what)

        def fox_act_turn(i, nxt=True):
            for a in range(2):
                act.wait_ge(p_fox.sem, p_fox.at("vT", i))
                act.wait_ge(p_fox.sem, p_fox.at("pv1", i - 1))
                a_fox.did(A(va_hi[:, a, :, a * FOX_D:(a + 1) * FOX_D],
                            ps[3][:].rearrange("p (s c) -> p s c", c=P)[:, :, a * FOX_D:(a + 1) * FOX_D], ACT.Identity),
                          f"vh{a}")

            def expo(n):
                r = n % NT
                act.wait_ge(v_fox.sem, v_fox.at(f"N{n}", i))
                if n >= 2:
                    act.wait_ge(p_fox.sem, p_fox.at(f"T{n - 2}", i))
                a_fox.did(A(pr[n % 2][:, 0:(r + 1) * P], lg[n % 2][:, 0:(r + 1) * P], ACT.Exp, scale=-1.0,
                            bias=mx[:, n % 2:n % 2 + 1]), f"e{n}")

            def high(n):
                a, r = divmod(n, NT)
                act.wait_ge(p_fox.sem, p_fox.at(f"T{n}", i))
                a_fox.did(A(pt_hi[a][:, 0:r + 1, r * P:(r + 1) * P],
                            ps[6 + n % 2][:, 0:(r + 1) * P].rearrange("p (s c) -> p s c", c=P), ACT.Identity), f"ph{n}")

            expo(0)
            for n in range(U):
                if n + 1 < U:
                    expo(n + 1)
                high(n)
            if nxt:
                act.wait_ge(v_fox.sem, v_fox.at(f"N{U - 1}", i))
                fox_cbc(i + 1)
                for what in "qkv":
                    fox_round(a_fox, i + 1, what)
            else:
                a_fox.skip(act, i, "q", "k", "v")
            for a in range(2):
                act.wait_ge(p_fox.sem, p_fox.at(f"pv{a}", i))
                o = (1 - a) * FOX_D
                a_fox.did(A(rs[a * FOX_D:(a + 1) * FOX_D, :], ps[3 + 4 * a][o:o + FOX_D, :], ACT.Identity), f"rs{a}")
            act.wait_ge(v_fox.sem, v_fox.at("o1", i))
            dst = a_hi[:, bass.ds(i, 1), :] if not isinstance(i, int) else a_hi[:, i, :]
            a_fox.did(A(dst, fo[:], ACT.Identity), "hi")

        a_fox.open(act)
        act.wait_ge(v_fg.sem, v_fg.at("ones_lo"))
        PAIRS = FOX_H // 2
        with act.Fori(0, PAIRS // 2 - 1) as it:
            for sub in range(2):
                fox_act_turn(2 * it + sub)
        fox_act_turn(PAIRS - 2)
        fox_act_turn(PAIRS - 1, nxt=False)
        out_act(act, outs[2], C_FOXOUT, (KT,))
        norm_act(act, norms[3], lambda n: zero_col[:, n:n + 1])

        def ffn_act(aS, vS, base):
            aS.open(act)
            with act.Fori(0, FT // 2) as it:
                for s in range(2):
                    j = 2 * it + s
                    act.wait_ge(gemm_done, base + 4 * it + 2 * s + 1)
                    act.wait_ge(vS.sem, vS.at("f", j - 2))
                    aS.did(A(fcv[s][:], ps[2 * s][:], ACT.Silu), "silu")
                    act.wait_ge(vS.sem, vS.at("f", j))
                    aS.did(A(f_hi[:, bass.ds(j, 1), :], fraw[s][:, 0:T], ACT.Identity), "hi")

        ffn_act(a_ff[0], v_ff[0], C_UP2)
        out_act(act, outs[3], C_DOWN2, DOWN_K)
        norm_act(act, norms[4], lambda n: zero_col[:, n:n + 1])

        for r in range(3):
            act.wait_ge(v_hg0.sem, v_hg0.at(f"d{r}"))
            a_hg0.did(A(col_a[:, 8 * r:8 * r + 8], col_a[:, 8 * r:8 * r + 8], ACT.Exp), f"e{r}")
        HGF = {"q": (0, hq, ACT.Identity), "sig": (1, hf, ACT.Sigmoid), "v": (2, hv, ACT.Identity), "g": (3, hs, ACT.Silu)}

        def hg_read(S, i, what):
            j, dst, func = HGF[what]
            act.wait_ge(gemm_done, C_HG + 4 * i + j + 1)
            S.did(A(dst[:], ps[j][:], func), what)

        for what in HGF:
            hg_read(a_hg0, 0, what)

        def hg_act_turn(i, nxt=True):
            act.wait_ge(v_hg.sem, v_hg.at("k", i))
            a_hg.did(A(hf[:], hf[:], ACT.Ln), "ln")
            act.wait_ge(p_hg.sem, p_hg.at("vT", i))
            a_hg.did(A(hvt[:], ps[4][:], ACT.Identity), "vt")
            for n, w in enumerate(LEVELS):
                act.wait_ge(v_hg.sem, v_hg.at(f"dr{w}", i))
                a_hg.did(A(he[n % 2][:], he[n % 2][:], ACT.Exp), f"e{w}")
            last_cols = hb[:].rearrange("p (j c) -> p j c", c=P)[:, :, P - 1:P]
            a_hg.did(A(het[:], last_cols, ACT.Exp), "et")
            act.wait_ge(v_hg.sem, v_hg.at("mr2", i))
            a_hg.did(A(he[1][:], hb[:], ACT.Exp), "eb")
            act.wait_ge(v_hg.sem, v_hg.at("mr1", i))
            for j in range(NT - 1):
                a_hg.did(A(he[0][:, j * P:(j + 1) * P], hb[:, j * P:(j + 1) * P], ACT.Exp, scale=-1.0,
                           bias=hb[:, (j + 1) * P - 1:(j + 1) * P]), f"ek{j}")
            act.wait_ge(p_hg.sem, p_hg.at("offA", i))
            a_hg.did(A(hsc[:, 0, P:T], ps[7][:, 0:3 * P], ACT.Identity), "offA")
            act.wait_ge(p_hg.sem, p_hg.at("offB", i))
            a_hg.did(A(hsc[:, 1, 2 * P:T], ps[4][:, 0:2 * P], ACT.Identity), "offB0")
            a_hg.did(A(hsc[:, 2, 3 * P:T], ps[4][:, 2 * P:3 * P], ACT.Identity), "offB1")
            if nxt:
                act.wait_ge(v_hg.sem, v_hg.at("x30", i))
                act.wait_ge(p_hg.sem, p_hg.at("S0", i))
                for what in ("q", "sig", "v"):
                    hg_read(a_hg, i + 1, what)
            else:
                a_hg.skip(act, i, "q", "sig", "v")
            did = a_hg.did
            act.wait_ge(p_hg.sem, p_hg.at("pv", i))
            did(A(ho2[:], ps[5][:], ACT.Square), "osq")
            act.wait_ge(v_hg.sem, v_hg.at("vr", i))
            did(A(ho[:], ho[:], ACT.Sqrt), "sd")
            act.wait_ge(v_hg.sem, v_hg.at("o2", i))
            dst = g_hi[:, bass.ds(i, 1), :] if not isinstance(i, int) else g_hi[:, i, :]
            did(A(dst, ho[:], ACT.Identity), "hi")
            if nxt:
                hg_read(a_hg, i + 1, "g")

        a_hg.open(act)
        with act.Fori(0, HG_H - 1) as i:
            hg_act_turn(i)
        hg_act_turn(HG_H - 1, nxt=False)
        out_act(act, outs[4], C_HGOUT, (KT,))
        norm_act(act, norms[5], lambda n: zero_col[:, n:n + 1])
        ffn_act(a_ff[1], v_ff[1], C_UP3)
        out_act(act, outs[5], C_DOWN3, DOWN_K)
        norm_act(act, norms[6], None)
        for n in range(KT):
            act.wait_ge(norms[6].vx.sem, norms[6].vx.at("x", n))
            act.dma_start(outT[:, n, :], x[:, n, :]).then_inc(out_landed, 16)
        act.wait_ge(out_landed, 16 * KT)

    @block.vector
    def _(dve):
        V = nc.vector

        dve.wait_ge(a_set.sem, a_set.at("sig_c"))
        v_set.did(V.tensor_tensor(cvec[:], cvec[:], prm[:, COL["c"]:COL["c"] + KT], ALU.mult), "c")
        dve.wait_ge(const_ready, 13)
        v_set.did(V.tensor_tensor(levels[:, 2, :], levels[:, 0, :], levels[:, 1, :], ALU.bitwise_xor), "xor")
        dve.wait_ge(v_set.sem, v_set.at("xor"))
        v_set.did(V.tensor_copy(m[:, 7, 0:P], levels[:, 2, :]), "float")
        dve.wait_ge(v_set.sem, v_set.at("float"))
        v_set.did(V.tensor_tensor(m[:, 7, 0:P], m[:, 7, 0:P], early[:], ALU.add), "causal")
        dve.wait_ge(v_set.sem, v_set.at("causal"))
        for n, w in enumerate(LEVELS):
            v_set.did(V.tensor_scalar(m[:, n, 0:P], m[:, 7, 0:P], float(w), None, ALU.is_ge), f"ge{n}")
        dve.wait_ge(v_set.sem, v_set.at("ge6"))
        v_set.did(V.tensor_copy(levels[:, 0, :], m[:, 0, 0:P]), "lv0")
        for n in range(1, len(LEVELS)):
            v_set.did(V.tensor_tensor(levels[:, n, :], m[:, n, 0:P], m[:, n - 1, 0:P], ALU.subtract), f"lv{n}")
        v_set.did(V.tensor_scalar(levels[:, 7, :], m[:, 7, 0:P], 0.0, None, ALU.is_equal), "lv7")

        def first_mod():
            s_ada.open(dve)
            for turn in range(ADA_FIRST // ADA_BODY):
                ada_dve_pieces(dve, turn)
                ada_dve_mod(dve, turn)
            dve.wait_ge(s_ada.sem, s_ada.at("mod", ADA_FIRST // ADA_BODY - 1))
            v_col.did(V.scalar_tensor_tensor(col_a[:, 0:KT], mod[:, 8:16], 1.0, prm[:, COL["mix_pre"]:COL["mix_pre"] + KT],
                                             ALU.add, ALU.mult), "a1")
            dve.wait_ge(v_col.sem, v_col.at("a1"))

        dve.wait_ge(x_landed, 16)
        norm_dve(dve, norms[0], None, lambda n: col_a[:, n:n + 1], lambda n: mod[:, n:n + 1], first_mod)

        H = slice(0, H1)
        v_gate.did(V.memset(cA[0:H1, :], 1.0), "one")
        dve.wait_ge(gemm_done, C_GATE1 + 1)
        v_gate.did(V.tensor_scalar(rz[H, :], ps[5][0:H1, :], prm[0:H1, COL["gate1_b"]:COL["gate1_b"] + 1], None, ALU.add), "zi")
        v_gate.did(V.tensor_scalar(rlf[H, :], ps[5][32:32 + H1, :], prm[32:32 + H1, COL["gate1_b"]:COL["gate1_b"] + 1],
                                   None, ALU.add), "zf")
        dve.wait_ge(a_gate.sem, a_gate.at("ln"))
        dve.wait_ge(v_gate.sem, v_gate.at("zf"))
        v_gate.did(V.scalar_tensor_tensor(rlf[H, :], rlf[H, :], 0.0, rb[H, :], ALU.min, ALU.subtract), "lf")
        dve.wait_ge(v_gate.sem, v_gate.at("lf"))
        v_gate.did(V.tensor_tensor_scan(rb[H, :], cA[H, :], rlf[H, :], 0.0, ALU.mult, ALU.add), "b")
        v_gate.did(V.tensor_tensor_scan(rm[H, :], rlf[H, :], rz[H, :], 0.0, ALU.add, ALU.max), "m")
        dve.wait_ge(v_gate.sem, v_gate.at("m"))
        v_gate.did(V.tensor_tensor(rA[H, :], rb[H, :], rm[H, :], ALU.subtract), "A")
        v_gate.did(V.tensor_tensor(rD[H, :], rz[H, :], rb[H, :], ALU.subtract), "D")
        dve.wait_ge(p_gate.sem, p_gate.at("dT"))
        v_gate.did(V.tensor_copy(dcol[:], ps[4][:, 0:NT * H1].rearrange("p (s h) -> p h s", h=H1)), "dcol")
        V.memset(ypad[0][:, 0:30], 0.0)
        V.memset(ypad[1][:, 0:30], 0.0)
        v_gate.did(V.memset(qk_raw[:, :, 0:3], 0.0), "pad")
        v_gate.did(V.memset(acc[:], 0.0), "ysum0")

        v_mix.open(dve)
        with dve.Fori(0, H1) as h:
            dve.wait_ge(v_gate.sem, v_gate.at("ysum0"))
            dve.wait_ge(v_mix.sem, v_mix.at("hg1", h - 1))
            v_mix.did(V.tensor_copy(hp[:], prm[:, bass.ds(COL["head"] + HEAD_COLS * h, HEAD_COLS)]), "hp")
            v_mix.did(V.tensor_copy(dcur[:], dcol[:, bass.ds(h, 1), :]), "dc")
            dve.wait_ge(bc_landed, 16 * h + 16)
            v_mix.did(V.tensor_tensor(dg[:], bc[:, 0, :].rearrange("p (s c) -> p s c", c=P),
                                      early[:].unsqueeze(1).to_broadcast([P, NT, P]), ALU.add), "diag")
            for j in range(2):
                dve.wait_ge(gemm_done, C_MIX + 12 * h + 2 * j + 2)
                dve.wait_ge(a_mix.sem, a_mix.at(f"sg{j}", h))
                v_mix.did(V.tensor_tensor(ypad[j][:, 30:], ps[2 * j + 1][:], sg[j][:], ALU.mult), f"gt{j}")

            def conv31(i):
                for j in range(CV_TAPS):
                    ch = (cA, cB)[j % 2]
                    wj = hp[:, HP_CVW + CV_TAPS * i + j:HP_CVW + CV_TAPS * i + j + 1]
                    src = ypad[i][:, j:j + T]
                    if j == 0:
                        dve.wait_ge(v_mix.sem, v_mix.at(f"gt{i}", h))
                    if j >= 2:
                        dve.wait_ge(v_mix.sem, v_mix.at(f"cv{i}_{j - 2}", h))
                        v_mix.did(V.scalar_tensor_tensor(ch[:], src, wj, ch[:], ALU.mult, ALU.add), f"cv{i}_{j}")
                    else:
                        v_mix.did(V.tensor_scalar(ch[:], src, wj, None, ALU.mult), f"cv{i}_{j}")
                dve.wait_ge(v_mix.sem, v_mix.at(f"cv{i}_{CV_TAPS - 1}", h))
                dst = y[:, bass.ds(2 * h + i, 1), :]
                v_mix.did(V.scalar_tensor_tensor(dst, cA[:], hp[:, HP_CVB + i:HP_CVB + i + 1], cB[:], ALU.add, ALU.add), f"y{i}")
                dve.wait_ge(v_mix.sem, v_mix.at(f"y{i}", h))
                v_mix.did(V.tensor_tensor(acc[:], acc[:], dst, ALU.add), f"ys{i}")

            conv31(0)
            for p_, part in enumerate("qk"):
                dve.wait_ge(a_mix.sem, a_mix.at(f"r{part}1", h))
                for t in range(QK_TAPS):
                    for j in range(2):
                        n = 2 * p_ + j
                        wj = hp[:, HP_QKW + QK_TAPS * n + t:HP_QKW + QK_TAPS * n + t + 1]
                        src = qk_raw[:, n, t:t + T]
                        if t == 0:
                            ins = V.tensor_scalar(qk[:, n, :], src, wj, None, ALU.mult)
                        else:
                            dve.wait_ge(v_mix.sem, v_mix.at(f"c{part}{j}_{t - 1}", h))
                            ins = V.scalar_tensor_tensor(qk[:, n, :], src, wj, qk[:, n, :], ALU.mult, ALU.add)
                        v_mix.did(ins, f"c{part}{j}_{t}")
            conv31(1)
            bank = [6, 7, 4, 5]
            dve.wait_ge(a_mix.sem, a_mix.at(f"off{NT - 2}", h))
            for st in range(NT):
                w = T - st * P
                dve.wait_ge(p_mix.sem, p_mix.at(f"qk{st}", h))
                v_mix.did(V.scalar_tensor_tensor(sp[:, WOFF[st]:WOFF[st] + w], ps[bank[st]][:, 0:w], float(DH1) ** -0.5,
                                                 wt[:, WOFF[st]:WOFF[st] + w], ALU.mult, ALU.mult), f"sp{st}")
            dve.wait_ge(p_mix.sem, p_mix.at("den", h))
            v_mix.did(V.scalar_tensor_tensor(var[:], ps[7][:], -1.0, bc[:, 1, :], ALU.mult, ALU.max), "dm")
            dve.wait_ge(v_mix.sem, v_mix.at("dm", h))
            v_mix.did(V.tensor_tensor(var[:], ps[7][:], var[:], ALU.max), "dn")
            dve.wait_ge(v_mix.sem, v_mix.at("dn", h))
            v_mix.did(V.reciprocal(rstd[:], var[:]), "r")
            dve.wait_ge(v_mix.sem, v_mix.at("r", h))
            v_mix.did(V.tensor_tensor(cA[:], rstd[:], rstd[:], ALU.mult), "r2")
            dve.wait_ge(v_mix.sem, v_mix.at("r2", h))
            dve.wait_ge(p_mix.sem, p_mix.at("hs", h))
            v_mix.did(V.scalar_tensor_tensor(cA[:], ps[5][:], 1.0 / DH1, cA[:], ALU.mult, ALU.mult), "vr")
            dve.wait_ge(a_mix.sem, a_mix.at("sd", h))
            v_mix.did(V.reciprocal(cB[:], cB[:]), "rs")
            dve.wait_ge(v_mix.sem, v_mix.at("rs", h))
            v_mix.did(V.tensor_tensor(rstd[:], rstd[:], cB[:], ALU.mult), "q")
            dve.wait_ge(v_mix.sem, v_mix.at("q", h))
            for e in range(2):
                v_mix.did(V.tensor_tensor((cA, cB)[e][:], ps[6 if e == 0 else 4][:], rstd[:], ALU.mult), f"h{e}")
            for e in range(2):
                dve.wait_ge(v_mix.sem, v_mix.at(f"h{e}", h))
                v_mix.did(V.scalar_tensor_tensor(hm[:, bass.ds(2 * h + e, 1), :], (cA, cB)[e][:],
                                                 hp[:, HP_G + e:HP_G + e + 1], so[:, e, :], ALU.mult, ALU.mult), f"hg{e}")

        for n in range(KT):
            dve.wait_ge(a_ln.sem, a_ln.at(f"hh{n}"))
            v_ln.did(V.tensor_tensor(u_lo[:, n, :], hm[:, n, :], u_hi[:, n, :].bitcast(f32), ALU.subtract), f"hl{n}")
        dve.wait_ge(p_ln.sem, p_ln.at("mu"))
        v_ln.did(V.tensor_scalar(var[:], ps[4][:], 1.0 / D, None, ALU.mult), "mu")
        dve.wait_ge(v_ln.sem, v_ln.at("mu"))
        for n in range(KT):
            v_ln.did(V.tensor_tensor(y[:, n, :], y[:, n, :], var[:], ALU.subtract), f"yc{n}")
        dve.wait_ge(p_ln.sem, p_ln.at(f"s{KT - 1}"))
        dve.wait_ge(v_ln.sem, v_ln.at(f"yc{KT - 1}"))
        v_ln.did(V.tensor_scalar(var[:], ps[5][:], 1.0 / D, EPS, ALU.mult, ALU.add), "var")
        dve.wait_ge(a_ln.sem, a_ln.at("sd"))
        v_ln.did(V.reciprocal(rstd[:], rstd[:]), "rstd")
        dve.wait_ge(v_ln.sem, v_ln.at("rstd"))
        for n in range(KT):
            v_ln.did(V.tensor_tensor(y[:, n, :], y[:, n, :], rstd[:], ALU.mult), f"t{n}")
        for n in range(KT):
            dve.wait_ge(a_ln.sem, a_ln.at(f"hi{n}"))
            v_ln.did(V.tensor_tensor(y_lo[:, n, :], y[:, n, :], y_hi[:, n, :].bitcast(f32), ALU.subtract), f"lo{n}")

        first = ADA_FIRST // ADA_BODY
        out_dve(dve, outs[0], lambda it: ada_dve_pieces(dve, first + it), lambda it: ada_dve_mod(dve, first + it))
        dve.wait_ge(s_ada.sem, s_ada.at("mod", ADA_ALL // ADA_BODY - 1))
        for name, o, src, gain in (("g1", 8, 16, "mix_post"), ("a2", 16, 32, "ffn_pre"), ("g2", 24, 40, "ffn_post")):
            g_ = prm[:, COL[gain]:COL[gain] + KT]
            if name == "a2":
                ins = V.scalar_tensor_tensor(col_a[:, o:o + KT], mod[:, src:src + KT], 1.0, g_, ALU.add, ALU.mult)
            else:
                ins = V.tensor_tensor(col_a[:, o:o + KT], mod[:, src:src + KT], g_, ALU.mult)
            v_col.did(ins, name)
        dve.wait_ge(v_col.sem, v_col.at("g2"))
        norm_dve(dve, norms[1], lambda n: col_a[:, 8 + n:9 + n], lambda n: col_a[:, 16 + n:17 + n],
                 lambda n: mod[:, 24 + n:25 + n])

        V.memset(fraw[0][:, 0:2], 0.0).then_inc(ff1_pads, 1)
        V.memset(fraw[1][:, 0:2], 0.0).then_inc(ff1_pads, 1)
        v_ff1.open(dve)
        with dve.Fori(0, FT // 2) as it:
            for s in range(2):
                j = 2 * it + s
                dve.wait_ge(a_ff1.sem, a_ff1.at("silu", j - 1))
                v_ff1.did(V.tensor_copy(fprm[:], prm[:, bass.ds(COL["ff"] + FF_COLS * j, FF_COLS)]), "prm")
                dve.wait_ge(v_ff1.sem, v_ff1.at("prm", j))
                for t in range(FF_TAPS):
                    for n, name in enumerate("ga"):
                        if t == 0:
                            dve.wait_ge(a_ff1.sem, a_ff1.at(name, j))
                        wj = fprm[:, FF_TAPS * n + t:FF_TAPS * n + t + 1]
                        src = fraw[n][:, t:t + T]
                        if t == 0:
                            ins = V.tensor_scalar(fcv[n][:], src, wj, None, ALU.mult)
                        else:
                            dve.wait_ge(v_ff1.sem, v_ff1.at(f"{name}{t - 1}", j))
                            ins = V.scalar_tensor_tensor(fcv[n][:], src, wj, fcv[n][:], ALU.mult, ALU.add)
                        v_ff1.did(ins, f"{name}{t}")
                dve.wait_ge(a_ff1.sem, a_ff1.at("silu", j))
                dve.wait_ge(v_ff1.sem, v_ff1.at(f"a{FF_TAPS - 1}", j))
                v_ff1.did(V.scalar_tensor_tensor(fval[:], fcv[1][:], fprm[:, 7:8], fsi[:], ALU.add, ALU.mult), "f")
                dve.wait_ge(a_ff1.sem, a_ff1.at("hi", j))
                dve.wait_ge(v_ff1.sem, v_ff1.at("f", j))
                v_ff1.did(V.tensor_tensor(f_lo[:, bass.ds(j, 1), :], fval[:], f_hi[:, bass.ds(j, 1), :].bitcast(f32),
                                          ALU.subtract), "lo")
        out_dve(dve, outs[1])
        gains = lambda layer, which: (lambda n: prm_col("gains", 32 * layer + 8 * which + n))
        zero = lambda n: zero_col[:, n:n + 1]
        norm_dve(dve, norms[2], lambda n: col_a[:, 24 + n:25 + n], gains(0, 0), zero)

        R = slice(0, FOX_H)
        v_fg.did(V.memset(one_row[R, :], 1.0), "one")
        dve.wait_ge(gemm_done, C_GATE2 + 1)
        v_fg.did(V.tensor_scalar(fz[R, :], ps[3][R, :], prm[R, COL["fox_b"]:COL["fox_b"] + 1], None, ALU.add), "z")
        dve.wait_ge(a_fg.sem, a_fg.at("ln"))
        dve.wait_ge(v_fg.sem, v_fg.at("z"))
        v_fg.did(V.scalar_tensor_tensor(fl[R, :], fz[R, :], 0.0, fl[R, :], ALU.min, ALU.subtract), "lf")
        dve.wait_ge(v_fg.sem, v_fg.at("lf"))
        v_fg.did(V.tensor_tensor_scan(fc[R, :], one_row[R, :], fl[R, :], 0.0, ALU.mult, ALU.add), "c")
        ones3 = ones[:, 0:FOX_D].unsqueeze(1).to_broadcast([P, NT, FOX_D])
        for a in range(2):
            o = (1 - a) * FOX_D
            ins = V.tensor_copy(va_hi[:, a, :, o:o + FOX_D], ones3)
        v_fg.did(ins, "ones_hi")
        for a in range(2):
            o = (1 - a) * FOX_D
            ins = V.memset(va_lo[:, a, :, o:o + FOX_D].bitcast(f32), 0.0)
        v_fg.did(ins, "ones_lo")

        def fox_low(S, aS, i, what, at=None):
            dve.wait_ge(aS.sem, aS.at(what[0], *at))
            if what == "ql":
                S.did(V.scalar_tensor_tensor(q_lo[:], ps[0][:], -float(FOX_D) ** -0.5, q_hi[:].bitcast(f32),
                                             ALU.mult, ALU.subtract), "ql")
            else:
                S.did(V.tensor_tensor(k_lo[:], ps[1][:], k_hi[:].bitcast(f32), ALU.subtract), "kl")

        for what in ("ql", "kl"):
            fox_low(v_fox0, a_fox0, 0, what, (0,))

        def fox_dve_turn(i, nxt=True):
            dve.wait_ge(bc_landed, 16 * H1 + 16 * (i + 1))
            for a in range(2):
                cols = slice(a * FOX_D, (a + 1) * FOX_D)
                dve.wait_ge(a_fox.sem, a_fox.at("vh1", i))
                v_fox.did(V.tensor_tensor(va_lo[:, a, :, cols], ps[3][:].rearrange("p (s c) -> p s c", c=P)[:, :, cols],
                                          va_hi[:, a, :, cols].bitcast(f32), ALU.subtract), f"vl{a}")

            def negated(n):
                a, r = divmod(n, NT)
                w = (r + 1) * P
                dve.wait_ge(p_fox.sem, p_fox.at(f"L{n}", i))
                if n >= 2:
                    dve.wait_ge(a_fox.sem, a_fox.at(f"e{n - 2}", i))
                dve.sem_inc(turn_waited, 1)
                v_fox.did(V.tensor_tensor_reduce(out=lg[n % 2][:, 0:w], in0=ps[4 + n % 2][:, 0:w], in1=cbc[:, a, 0:w],
                                                 scale=1.0, scalar=BIG, op0=ALU.add, op1=ALU.min,
                                                 accum_out=mx[:, n % 2:n % 2 + 1]), f"N{n}")

            def low(n):
                a, r = divmod(n, NT)
                dve.wait_ge(a_fox.sem, a_fox.at(f"ph{n}", i))
                cols = slice(r * P, (r + 1) * P)
                v_fox.did(V.tensor_tensor(pt_lo[a][:, 0:r + 1, cols],
                                          ps[6 + n % 2][:, 0:(r + 1) * P].rearrange("p (s c) -> p s c", c=P),
                                          pt_hi[a][:, 0:r + 1, cols].bitcast(f32), ALU.subtract), f"pl{n}")

            negated(0)
            for n in range(U):
                if n + 1 < U:
                    negated(n + 1)
                low(n)
            if nxt:
                for what in ("ql", "kl"):
                    fox_low(v_fox, a_fox, i + 1, what, (i,))
            else:
                v_fox.skip(dve, i, "ql", "kl")
            dve.wait_ge(a_fox.sem, a_fox.at("rs1", i))
            v_fox.did(V.reciprocal(rs[:], rs[:]), "recip")
            dve.wait_ge(v_fox.sem, v_fox.at("recip", i))
            for a in range(2):
                rows = slice(a * FOX_D, (a + 1) * FOX_D)
                v_fox.did(V.tensor_tensor(fo[rows, :], ps[3 + 4 * a][rows, :], rs[rows, :], ALU.mult), f"o{a}")
            at_ = (lambda t: t[:, bass.ds(i, 1), :]) if not isinstance(i, int) else (lambda t: t[:, i, :])
            dve.wait_ge(a_fox.sem, a_fox.at("hi", i))
            v_fox.did(V.tensor_tensor(at_(a_lo), fo[:], at_(a_hi).bitcast(f32), ALU.subtract), "lo")

        v_fox.open(dve)
        PAIRS = FOX_H // 2
        with dve.Fori(0, PAIRS // 2 - 1) as it:
            for sub in range(2):
                fox_dve_turn(2 * it + sub)
        fox_dve_turn(PAIRS - 2)
        fox_dve_turn(PAIRS - 1, nxt=False)
        out_dve(dve, outs[2])
        norm_dve(dve, norms[3], gains(0, 1), gains(0, 2), zero)

        def ffn_dve(vS, aS, base):
            vS.open(dve)
            with dve.Fori(0, FT // 2) as it:
                for s in range(2):
                    j = 2 * it + s
                    dve.wait_ge(gemm_done, base + 4 * it + 2 * s + 2)
                    dve.wait_ge(aS.sem, aS.at("silu", j))
                    dve.wait_ge(aS.sem, aS.at("hi", j - 2))
                    vS.did(V.tensor_tensor(fraw[s][:, 0:T], ps[2 * s + 1][:], fcv[s][:], ALU.mult), "f")
                    dve.wait_ge(aS.sem, aS.at("hi", j))
                    dve.wait_ge(vS.sem, vS.at("f", j))
                    vS.did(V.tensor_tensor(f_lo[:, bass.ds(j, 1), :], fraw[s][:, 0:T],
                                           f_hi[:, bass.ds(j, 1), :].bitcast(f32), ALU.subtract), "lo")

        ffn_dve(v_ff[0], a_ff[0], C_UP2)
        out_dve(dve, outs[3])
        norm_dve(dve, norms[4], gains(0, 3), gains(1, 0), zero)

        lb_row = lambda r: prm[:, COL["lb"] + 8 * r:COL["lb"] + 8 * r + 8]
        ca = lambda r: col_a[:, 8 * r:8 * r + 8]
        v_hg0.did(V.tensor_tensor(ca(3), lb_row(0), lb_row(1), ALU.max), "mx")
        dve.wait_ge(v_hg0.sem, v_hg0.at("mx"))
        v_hg0.did(V.tensor_tensor(ca(3), ca(3), lb_row(2), ALU.max), "mx2")
        dve.wait_ge(v_hg0.sem, v_hg0.at("mx2"))
        for r in range(3):
            v_hg0.did(V.tensor_tensor(ca(r), lb_row(r), ca(3), ALU.subtract), f"d{r}")
        dve.wait_ge(a_hg0.sem, a_hg0.at("e2"))
        v_hg0.did(V.tensor_tensor(ca(3), ca(0), ca(1), ALU.add), "s")
        dve.wait_ge(v_hg0.sem, v_hg0.at("s"))
        v_hg0.did(V.tensor_tensor(ca(4), ca(3), ca(2), ALU.add), "s2")
        dve.wait_ge(v_hg0.sem, v_hg0.at("s2"))
        v_hg0.did(V.reciprocal(ca(4), ca(4)), "r")
        dve.wait_ge(v_hg0.sem, v_hg0.at("r"))
        v_hg0.did(V.tensor_tensor(ca(4), ca(3), ca(4), ALU.mult), "lb")
        dve.wait_ge(v_hg0.sem, v_hg0.at("lb"))
        v_hg0.did(V.tensor_scalar(ca(5), ca(4), -1.0, 1.0, ALU.mult, ALU.add), "oml")
        v_hg0.did(V.memset(hsc[:], 0.0), "zero")
        dve.wait_ge(v_hg0.sem, v_hg0.at("zero"))

        diag = hsc[:].rearrange("p c t -> p (c t)")

        def hg_dve_turn(i, nxt=True):
            w_ = lambda step: dve.wait_ge(v_hg.sem, v_hg.at(step, i))
            one_ = lambda o: col_a[:, bass.ds(o + i, 1)] if not isinstance(i, int) else col_a[:, o + i:o + i + 1]
            dve.wait_ge(v_hg.sem, v_hg.at("lo", i - 1))
            V.tensor_copy(lbcur[:, 1:2], one_(40))
            v_hg.did(V.tensor_copy(lbcur[:, 0:1], one_(32)), "cur")
            w_("cur")
            dve.wait_ge(a_hg0.sem, a_hg0.at("sig"))
            dve.wait_ge(a_hg.sem, a_hg.at("g", i - 1))
            v_hg.did(V.tensor_scalar(hf[:], hf[:], lbcur[:, 1:2], lbcur[:, 0:1], ALU.mult, ALU.add), "f")
            w_("f")
            v_hg.did(V.tensor_scalar(hk[:], hf[:], -1.0, 1.0, ALU.mult, ALU.add), "k")
            dve.wait_ge(a_hg.sem, a_hg.at("ln", i))
            for j in range(NT):
                ts = slice(j * P, (j + 1) * P)
                v_hg.did(V.tensor_tensor_scan(hb[:, ts], ones[:], hf[:, ts], 0.0, ALU.mult, ALU.add), f"b{j}")
            w_(f"b{NT - 1}")

            def halves(t, w):
                v = t[:].rearrange("p (n c) -> p n c", c=2 * w)
                return v[:, :, 0:w], v[:, :, w:2 * w]

            def diffs(n):
                w = LEVELS[n]
                if n >= 2:
                    w_(f"mr{LEVELS[n - 2]}")
                left, right = halves(hb, w)
                mid = left[:, :, w - 1:w].to_broadcast([P, T // (2 * w), w])
                dl, dr = halves(he[n % 2], w)
                v_hg.did(V.tensor_tensor(dl, mid, left, ALU.subtract), f"dl{w}")
                v_hg.did(V.tensor_tensor(dr, right, mid, ALU.subtract), f"dr{w}")

            def weighted(n):
                w = LEVELS[n]
                dve.wait_ge(a_hg.sem, a_hg.at(f"e{w}", i))
                if n >= 2:
                    dve.wait_ge(p_hg.sem, p_hg.at(f"S{LEVELS[n - 2]}", i))
                el, er = halves(he[n % 2], w)
                kl, _ = halves(hk, w)
                _, qr = halves(hq, w)
                ol, or_ = halves(hl[n % 2], w)
                v_hg.did(V.tensor_tensor(ol, kl, el, ALU.mult), f"ml{w}")
                v_hg.did(V.tensor_tensor(or_, qr, er, ALU.mult), f"mr{w}")

            def pick(n, step, pe_step):
                dve.wait_ge(p_hg.sem, p_hg.at(pe_step, i))
                if n:
                    w_(f"pc{LEVELS[n - 1]}")
                dve.sem_inc(turn_waited, 1)
                v_hg.did(V.copy_predicated(bass.AP(hsc, 0, [[NT * T, P], [T + P, NT], [1, P]]),
                                           levels[:, n, :].unsqueeze(1).to_broadcast([P, NT, P]),
                                           ps[5 + n % 2][:].rearrange("p (c t) -> p c t", t=P)), step)

            diffs(0)
            for n, w in enumerate(LEVELS):
                if n + 1 < len(LEVELS):
                    diffs(n + 1)
                weighted(n)
                if n:
                    pick(n - 1, f"pc{LEVELS[n - 1]}", f"S{LEVELS[n - 1]}")
            dve.wait_ge(a_hg.sem, a_hg.at("eb", i))
            v_hg.did(V.tensor_tensor(hqd[:], hq[:], he[1][:], ALU.mult), "qd")
            dve.wait_ge(a_hg.sem, a_hg.at(f"ek{NT - 2}", i))
            v_hg.did(V.tensor_tensor(hkd[:, 0:3 * P], hk[:, 0:3 * P], he[0][:, 0:3 * P], ALU.mult), "kd")
            w_("kd")
            v_hg.did(V.tensor_scalar(hkx[:, 0, :], hkd[:, 0:P], het[:, 1:2], None, ALU.mult), "x20")
            v_hg.did(V.tensor_scalar(hkx[:, 1, :], hkd[:, P:2 * P], het[:, 2:3], None, ALU.mult), "x31")
            w_("x20")
            v_hg.did(V.tensor_scalar(hkx[:, 2, :], hkx[:, 0, :], het[:, 2:3], None, ALU.mult), "x30")
            pick(6, "pc1", "S1")
            pick(7, "pc0", "S0")
            dve.wait_ge(p_hg.sem, p_hg.at("ss", i))
            v_hg.did(V.tensor_scalar(ho[:], ps[6][:], 1.0 / P, EPS, ALU.mult, ALU.add), "vr")
            dve.wait_ge(a_hg.sem, a_hg.at("sd", i))
            v_hg.did(V.reciprocal(ho2[:], ho[:]), "rstd")
            w_("rstd")
            v_hg.did(V.tensor_tensor(ho[:], ps[5][:], ho2[:], ALU.mult), "o1")
            w_("o1")
            v_hg.did(V.scalar_tensor_tensor(ho[:], ho[:], prm_col("gnorm"), hs[:], ALU.mult, ALU.mult), "o2")
            at_ = (lambda t: t[:, bass.ds(i, 1), :]) if not isinstance(i, int) else (lambda t: t[:, i, :])
            dve.wait_ge(a_hg.sem, a_hg.at("hi", i))
            v_hg.did(V.tensor_tensor(at_(g_lo), ho[:], at_(g_hi).bitcast(f32), ALU.subtract), "lo")

        v_hg.open(dve)
        with dve.Fori(0, HG_H - 1) as i:
            hg_dve_turn(i)
        hg_dve_turn(HG_H - 1, nxt=False)
        out_dve(dve, outs[4])
        norm_dve(dve, norms[5], gains(1, 1), gains(1, 2), zero)
        ffn_dve(v_ff[1], a_ff[1], C_UP3)
        out_dve(dve, outs[5])
        norm_dve(dve, norms[6], gains(1, 3), None, None)

    ctx.close()


def _tiles(a):
    return np.ascontiguousarray(a.reshape(-1, P, a.shape[1]).transpose(1, 0, 2))


def _columns(v):
    return v.reshape(-1, P).T


def _stream(ins):
    out = np.zeros((C_END, P, D), np.float32)

    def chunk(c, w):
        w = w.reshape(-1, P, w.shape[1])
        out[c].reshape(P, KT, P)[:, :w.shape[0], :w.shape[2]] = w.transpose(1, 0, 2)

    def cols(w, n):
        return w[:, n * P:(n + 1) * P]

    w = ins["w_in"][0]
    g = 4 * D
    gates = out[C_GATE1].reshape(P, KT, P)
    gates[:, :, 0:H1] = w[:, g:g + H1].reshape(KT, P, H1).transpose(1, 0, 2)
    gates[:, :, 32:32 + H1] = w[:, g + H1:g + 2 * H1].reshape(KT, P, H1).transpose(1, 0, 2)
    a = w[:, g + 2 * H1:]
    for h in range(H1):
        parts = [cols(a, KT + 2 * h), cols(a, 2 * h), cols(a, KT + 2 * h + 1), cols(a, 2 * h + 1)]
        parts += [cols(w, KT * p + 2 * h + e) for p in range(4) for e in range(2)]
        for j, part in enumerate(parts):
            chunk(C_MIX + 12 * h + j, part)
    for n in range(KT):
        for j in range(2):
            chunk(C_WOUT1 + 2 * n + j, cols(ins["w_out"][0][D * j:D * (j + 1)], n))

    def ffn(up, down, c_up, c_down, gate_first):
        for j in range(FT):
            first, second = (j, FT + j) if gate_first else (FT + j, j)
            chunk(c_up + 2 * j, cols(up, first))
            chunk(c_up + 2 * j + 1, cols(up, second))
        for n in range(KT):
            k = 0
            for j, nk in enumerate(DOWN_K):
                chunk(c_down + 3 * n + j, cols(down[k * P:(k + nk) * P], n))
                k += nk

    ffn(ins["ffn_up"][0], ins["ffn_down"][0], C_UP1, C_DOWN1, False)
    w = ins["fox_w_in_2"][0]
    chunk(C_GATE2, w[:, 3 * D:])
    for i in range(KT):
        for j in range(3):
            chunk(C_FOX + 3 * i + j, cols(w, KT * j + i))
        chunk(C_FOXOUT + i, cols(ins["fox_w_out_2"][0], i))
    ffn(ins["ffn_w_in_2"][0], ins["ffn_w_out_2"][0], C_UP2, C_DOWN2, True)
    for i in range(KT):
        for j in range(4):
            chunk(C_HG + 4 * i + j, cols(ins["hgrn_w_in_2"][0], KT * j + i))
        chunk(C_HGOUT + i, cols(ins["hgrn_w_out_2"][0], i))
    ffn(ins["ffn_w_in_2"][1], ins["ffn_w_out_2"][1], C_UP3, C_DOWN3, True)
    return out


def _params(ins):
    out = np.zeros((P, NPRM), np.float32)

    def put(name, block_, at=0):
        out[:block_.shape[0], COL[name] + at:COL[name] + at + block_.shape[1]] = block_

    put("c", _columns(ins["c"][0]))
    put("ada_b", _columns(ins["ada_b"][0]))
    for name, key in (("mix_pre", "mix_pre_g"), ("mix_post", "mix_post_g"), ("ffn_pre", "ffn_pre_g"),
                      ("ffn_post", "ffn_post_g"), ("ln_g", "cv_ln_g"), ("ln_b", "cv_ln_b")):
        put(name, _columns(ins[key][0]))
    out[0:H1, COL["gate1_b"]] = ins["igate_b"][0]
    out[32:32 + H1, COL["gate1_b"]] = ins["fgate_b"][0]
    for h in range(H1):
        at = HEAD_COLS * h
        for e in range(2):
            ch = slice((2 * h + e) * P, (2 * h + e + 1) * P)
            put("head", ins["cv_dw_w"][0][:, ch].T, at + HP_CVW + CV_TAPS * e)
            put("head", ins["cv_dw_b"][0][ch][:, None], at + HP_CVB + e)
            put("head", ins["ml_norm_g"][0][ch][:, None], at + HP_G + e)
            for p in range(2):
                qc = slice(D * p + ch.start, D * p + ch.stop)
                put("head", ins["qk_conv_w"][0][:, qc].T, at + HP_QKW + QK_TAPS * (2 * p + e))
                put("head", ins["qk_conv_b"][0][qc][:, None], at + HP_QKB + 2 * p + e)
    for j in range(FT):
        for n, tile in enumerate((FT + j, j)):
            ch = slice(tile * P, (tile + 1) * P)
            put("ff", ins["ffn_conv_w"][0][:, ch].T, FF_COLS * j + FF_TAPS * n)
            put("ff", ins["ffn_conv_b"][0][ch][:, None], FF_COLS * j + 2 * FF_TAPS + n)
    out[0:FOX_H, COL["fox_b"]] = ins["fox_b_f_2"][0]
    for r in range(3):
        put("lb", _columns(ins["hgrn_lb_table_2"][r]), 8 * r)
    put("gnorm", ins["hgrn_gnorm_2"][0][:, None])
    for layer in range(2):
        for which in range(4):
            put("gains", _columns(ins["norm_gains_2"][layer, which]), 32 * layer + 8 * which)
    return out


def kernel(**inputs):
    import concourse.bacc as bacc
    from concourse.bass_utils import run_bass_kernel_spmd

    ins = {k: np.asarray(v) for k, v in inputs.items()}
    n_ada = ADA_ALL
    arrays = {
        "xT": _tiles(ins["x"][0].T),
        "wstream": _stream(ins),
        "ada": np.ascontiguousarray(ins["ada_w"][0].reshape(KT, P, n_ada, ADA_COLS).transpose(2, 1, 0, 3)
                                    ).reshape(n_ada, P, KT * ADA_COLS),
        "params": _params(ins),
    }
    nc = bacc.Bacc("TRN2", target_bir_lowering=False, num_devices=1)
    f32 = mybir.dt.float32
    aps = [nc.dram_tensor(f"in_{k}", list(a.shape), f32, kind="ExternalInput").ap() for k, a in arrays.items()]
    out = nc.dram_tensor("out_T", [P, KT, T], f32, kind="ExternalOutput").ap()
    rows1 = nc.dram_tensor("gate_rows", [2, H1, T], f32, kind="Internal").ap()
    rows2 = nc.dram_tensor("decay_rows", [FOX_H, T], f32, kind="Internal").ap()
    build(nc, *aps, out, rows1, rows2)
    r = run_bass_kernel_spmd(nc, [{f"in_{k}": a for k, a in arrays.items()}], core_ids=[0])
    y = np.asarray(r.results[0]["out_T"])
    return np.ascontiguousarray(y.transpose(2, 1, 0)).reshape(1, T, D)
```

```python
import numpy as np
import concourse.bass as bass
from concourse import mybir
from contextlib import ExitStack

P = 128
T = 512
D = 1024
KT = D // P
NT = T // P
EPS = 1e-6
LN_EXP = "natural_log_exp_and_others"
POOL_TILES = (1, 3, 5, 6, 7)
H1, DH1 = 4, 256
QK_TAPS, CV_TAPS, FF_TAPS = 4, 31, 3
FT = 2816 // P
FOX_H = 16
FOX_D = D // FOX_H
HG_H = 8
BIG = 1e30

C_GATE1 = 0
C_MIX = 1
C_WOUT1 = C_MIX + 12 * H1
C_UP1 = C_WOUT1 + 2 * KT
C_DOWN1 = C_UP1 + 2 * FT
C_GATE2 = C_DOWN1 + 3 * KT
C_FOX = C_GATE2 + 1
C_FOXOUT = C_FOX + 3 * KT
C_UP2 = C_FOXOUT + KT
C_DOWN2 = C_UP2 + 2 * FT
C_HG = C_DOWN2 + 3 * KT
C_HGOUT = C_HG + 4 * HG_H
C_UP3 = C_HGOUT + KT
C_DOWN3 = C_UP3 + 2 * FT
C_END = C_DOWN3 + 3 * KT
RAW, SPLIT = 4, 2
DOWN_K = (8, 7, 7)
ADA_COLS = 256
ADA_FIRST, ADA_ALL = 2 * D // ADA_COLS, 6 * D // ADA_COLS

HEAD_COLS = 2 * CV_TAPS + 2 + 4 * QK_TAPS + 4 + 2
FF_COLS = 2 * FF_TAPS + 2
_widths = [("c", KT), ("ada_b", 48), ("mix_pre", KT), ("mix_post", KT), ("gate1_b", 1), ("head", H1 * HEAD_COLS),
           ("ln_g", KT), ("ln_b", KT), ("ffn_pre", KT), ("ffn_post", KT), ("ff", FT * FF_COLS), ("fox_b", 1),
           ("lb", 24), ("gnorm", 1), ("gains", 64)]
COL, _at = {}, 0
for _name, _w in _widths:
    COL[_name] = _at
    _at += _w
NPRM = _at
HP_CVW, HP_CVB, HP_QKW, HP_QKB, HP_G = 0, 62, 64, 80, 84


class Steps:

    def __init__(self, ctx, nc, name, steps, credit=0):
        self.sem = ctx.enter_context(nc.semaphore(name))
        self.steps, self.n, self.credit, self.next = steps, len(steps), credit, 0
        assert len(set(steps)) == len(steps), name

    def at(self, step, turn=0):
        return (turn + self.credit) * self.n + self.steps.index(step) + 1

    def open(self, eng):
        if self.credit:
            eng.sem_inc(self.sem, self.credit * self.n)

    def skip(self, eng, turn, *steps):
        eng.wait_ge(self.sem, self.at(steps[0], turn) - 1)
        for step in steps:
            assert self.steps[self.next] == step, (self.steps[self.next], step)
            self.next = (self.next + 1) % self.n
        eng.sem_inc(self.sem, len(steps))

    def did(self, ins, step):
        assert self.steps[self.next] == step, (self.steps[self.next], step)
        self.next = (self.next + 1) % self.n
        ins.then_inc(self.sem, 1)


def build(nc, xT, wstream, ada, params, outT, rows1, rows2):
    f32, f32r, bf16, i32 = mybir.dt.float32, mybir.dt.float32r, mybir.dt.bfloat16, mybir.dt.int32
    ALU, ACT = mybir.AluOpType, mybir.ActivationFunctionType
    ctx = ExitStack()
    ctx.__enter__()

    here = [(nc.sbuf_base + 31) // 32 * 32]

    def place(name, cols, dt=f32, shape=None):
        size = (cols * (2 if dt == bf16 else 4) + 31) // 32 * 32
        t = nc.alloc_sbuf_tensor_at(name, [P] + (shape or [cols]), dt, offset=here[0])
        here[0] += size
        return t

    x = place("x", KT * T, shape=[KT, T])
    raw = [place(f"raw{i}", D) for i in range(RAW)]
    w_hi = [place(f"w_hi{i}", D, f32r) for i in range(SPLIT)]
    w_lo = [place(f"w_lo{i}", D, f32r) for i in range(SPLIT)]
    prm = place("prm", NPRM)
    mod = place("mod", 48)
    cvec = place("cvec", KT)
    col_a = place("col_a", 6 * KT)
    zero_col = place("zero_col", KT)
    eps_col = place("eps_col", 2)
    ones = place("ones", P)
    ident = place("ident", P)
    ident_b = place("ident_b", P, bf16)
    late_b = place("late_b", P, bf16)
    early = place("early", P)
    levels = place("levels", 8 * P, i32, [8, P])
    u_hi = place("u_hi", KT * T, f32r, [KT, T])
    u_lo = place("u_lo", KT * T, f32r, [KT, T])
    sq = [place(f"sq{i}", T) for i in range(2)]
    acc = place("acc", T)
    rms = place("rms", T)
    rstd = place("rstd", T)
    mix_at = here[0]
    m = place("m", KT * T, shape=[KT, T])
    mix_end = here[0]
    phase_at = here[0]

    hm = place("hm", KT * T, shape=[KT, T])
    y = place("y", KT * T, shape=[KT, T])
    tmp_at = here[0]
    qk_raw = place("qk_raw", 4 * (T + 3), shape=[4, T + 3])
    qk = place("qk", 4 * T, shape=[4, T])
    vf = place("vf", 2 * T, shape=[2, T])
    vt = place("vt", 2 * T, shape=[2, NT, P])
    so = place("so", 2 * T, shape=[2, T])
    ypad = [place(f"ypad{i}", T + 30) for i in range(2)]
    sg = [place(f"sg{i}", T) for i in range(2)]
    bc = place("bc", 2 * T, shape=[2, T])
    dg = place("dg", T, shape=[NT, P])
    WOFF = [0, 512, 896, 1152]
    wt = place("wt", 1280)
    sp = place("sp", 1280)
    hp = place("hp", HEAD_COLS)
    dcol = place("dcol", 16, shape=[H1, NT])
    dcur = place("dcur", NT)
    top = here[0]
    here[0] = mix_at
    rz, rlf, rb, rm, rA, rD = [place(n, T) for n in ("rz", "rlf", "rb", "rm", "rA", "rD")]
    cA, cB = [place(n, T) for n in ("cA", "cB")]
    assert here[0] <= mix_end
    here[0] = tmp_at
    y_hi = place("y_hi", KT * T, f32r, [KT, T])
    y_lo = place("y_lo", KT * T, f32r, [KT, T])
    ada_buf = [place(f"ada_buf{i}", KT * ADA_COLS, shape=[KT, ADA_COLS]) for i in range(2)]
    ada_acc = place("ada_acc", 4 * ADA_COLS, shape=[4, ADA_COLS])
    top = max(top, here[0])
    here[0] = phase_at
    ada_start = place("ada_start", ADA_FIRST * KT * ADA_COLS, shape=[ADA_FIRST, KT, ADA_COLS])
    top = max(top, here[0])
    here[0] = phase_at
    f_hi = place("f_hi", FT * T, f32r, [FT, T])
    f_lo = place("f_lo", FT * T, f32r, [FT, T])
    fprm = place("fprm", FF_COLS)
    top = max(top, here[0])
    here[0] = mix_at
    fraw = [place(f"fraw{i}", T + 2) for i in range(2)]
    fcv = [place(f"fcv{i}", T) for i in range(2)]
    fsi = place("fsi", T)
    fval = place("fval", T)
    assert here[0] <= mix_end
    here[0] = phase_at
    a_hi = place("a_hi", KT * T, f32r, [KT, T])
    a_lo = place("a_lo", KT * T, f32r, [KT, T])
    q_hi, q_lo, k_hi, k_lo = [place(n, T, f32r) for n in ("q_hi", "q_lo", "k_hi", "k_lo")]
    fv = place("fv", T)
    va_hi = place("va_hi", 8 * P, f32r, [2, NT, P])
    va_lo = place("va_lo", 8 * P, f32r, [2, NT, P])
    pr = [place(f"pr{i}", T) for i in range(2)]
    pt_hi = [place(f"pt_hi{i}", NT * T, f32r, [NT, T]) for i in range(2)]
    pt_lo = [place(f"pt_lo{i}", NT * T, f32r, [NT, T]) for i in range(2)]
    mx, row_sum, row_inv = place("mx", 2), place("row_sum", 2), place("row_inv", 2)
    top = max(top, here[0])
    here[0] = mix_at
    cbc = [place(f"cbc{i}", 2 * T, shape=[2, T]) for i in range(2)]
    lg = [place(f"lg{i}", T) for i in range(2)]
    assert here[0] <= mix_end
    here[0] = mix_at
    fz, fl, fc, one_row = [place(n, T) for n in ("fz", "fl", "fc", "one_row")]
    here[0] = phase_at
    g_hi = place("g_hi", KT * T, f32r, [KT, T])
    g_lo = place("g_lo", KT * T, f32r, [KT, T])
    hq, hk, hf, hb, hv, hs, hs2 = [place(n, T) for n in ("hq", "hk", "hf", "hb", "hv", "hs", "hs2")]
    hvt = place("hvt", T, shape=[NT, P])
    he = [place(f"he{i}", T) for i in range(2)]
    hl = [place(f"hl{i}", T) for i in range(2)]
    hqd, hkd = place("hqd", T), place("hkd", T)
    hkx = place("hkx", 3 * P, shape=[3, P])
    hsc = place("hsc", NT * T, shape=[NT, T])
    ho, ho2 = place("ho", T), place("ho2", T)
    het = place("het", NT)
    lbcur = place("lbcur", 2)
    top = max(top, here[0])
    assert top <= nc.sbuf_usable_end, (top, nc.sbuf_usable_end)

    ps = [ctx.enter_context(nc.psum_tensor(f"ps{i}", [P, T], f32)) for i in range(8)]

    def sem(name):
        return ctx.enter_context(nc.semaphore(name))

    raw_landed = [sem(f"raw_landed{i}") for i in range(RAW)]
    chunk_hi, chunk_split, gemm_done = sem("chunk_hi"), sem("chunk_split"), sem("gemm_done")
    ff1_pads = sem("ff1_pads")
    ada_landed = [sem(f"ada_landed{i}") for i in range(2)]
    ada_start_landed = [sem(f"ada_start_landed{i}") for i in range(ADA_FIRST)]
    x_landed, prm_landed, const_ready = sem("x_landed"), sem("prm_landed"), sem("const_ready")
    turn_waited = sem("turn_waited")
    rows_out, bc_landed, out_landed = sem("rows_out"), sem("bc_landed"), sem("out_landed")

    ADA_BODY = 4
    s_ada = Steps(ctx, nc, "ada_dve", [f"piece{i}" for i in range(ADA_BODY)] + ["mod"], credit=1)
    p_ada = Steps(ctx, nc, "ada_pe", ["sums"])
    v_set = Steps(ctx, nc, "setup_dve", ["c", "xor", "float", "causal"] + [f"ge{i}" for i in range(7)] + [f"lv{i}" for i in range(8)])
    a_set = Steps(ctx, nc, "setup_act", ["sig_c"])
    v_col = Steps(ctx, nc, "cols_dve", ["a1", "g1", "a2", "g2"])

    class Norm:

        def __init__(self, name, post, pre):
            self.post, self.pre = post, pre
            if post:
                self.pe1 = Steps(ctx, nc, name + "_pe1", ["sum"])
                self.a1 = Steps(ctx, nc, name + "_act1", ["ln", "rstd"])
                self.pt = Steps(ctx, nc, name + "_pool", [f"t{n}" for n in POOL_TILES])
                self.vx = Steps(ctx, nc, name + "_dvex",
                                [s_ for n in range(KT) for s_ in ([] if n in POOL_TILES else [f"t{n}"]) + [f"x{n}"]])
            if pre:
                self.asq = Steps(ctx, nc, name + "_actsq", ["sq"])
                self.pe2 = Steps(ctx, nc, name + "_pe2", ["sum"])
                self.a2 = Steps(ctx, nc, name + "_act2", ["ln", "rstd"])
                self.vt = Steps(ctx, nc, name + "_dvet", ["t"])
                self.ah = Steps(ctx, nc, name + "_acthi", ["hi"])
                self.vl = Steps(ctx, nc, name + "_dvelo", ["lo"])

    norms = [Norm("n0", False, True)] + [Norm(f"n{i}", True, i < 6) for i in range(1, 7)]

    class OutGemm:
        def __init__(self, name):
            self.act = Steps(ctx, nc, name + "_act", ["copy", "sq"], credit=2)
            self.dve = Steps(ctx, nc, name + "_dve", ["acc"], credit=2)

    outs = [OutGemm(f"og{i}") for i in range(6)]

    def matmuls(out, pairs, n_inc=None, start=True, stop=True):
        last = None
        for i, (a, b) in enumerate(pairs):
            last = nc.tensor.matmul(out, a, b, start=(start and i == 0), stop=(stop and i == len(pairs) - 1))
        return last

    def tri(ah, al, bh, bl):
        return [(ah, bh), (ah, bl), (al, bh)]

    def gemm_chunk(pe, chunk, slot, out, hi, lo, k0, nk, start, stop, tile_wait=None, hook=None):
        pe.wait_ge(chunk_split, chunk + 1)
        last = None
        for k in range(nk):
            if tile_wait:
                tile_wait(k0 + k)
            wh, wl = w_hi[slot][:, k * P:(k + 1) * P], w_lo[slot][:, k * P:(k + 1) * P]
            for i, (a, b) in enumerate(tri(wh, wl, hi(k), lo(k))):
                last = nc.tensor.matmul(out, a, b, start=(start and k == 0 and i == 0),
                                        stop=(stop and k == nk - 1 and i == 2))
            if k == nk - 1:
                last.then_inc(gemm_done, 1)
            if hook:
                hook(k)

    def u_tiles(k):
        return u_hi[:, k, :]

    def u_lows(k):
        return u_lo[:, k, :]

    def norm_pe(pe, N, og):
        if N.post:
            pe.wait_ge(og.dve.sem, og.dve.at("acc", KT - 1))
            N.pe1.did(nc.tensor.matmul(ps[5][:], ones[:], acc[:], start=True, stop=True), "sum")
        if N.pre:
            for n in range(KT):
                pe.wait_ge(N.asq.sem, N.asq.at("sq", n))
                N.pe2.did(nc.tensor.matmul(ps[7][:], ones[:], sq[n % 2][:], start=(n == 0), stop=(n == KT - 1)), "sum")

    def inverse_root(act, S, out, total, count):
        S.did(nc.scalar.activation(out[:], total[:], ACT.Ln, scale=1.0 / count, bias=eps_col[:, 0:1]), "ln")
        act.wait_ge(S.sem, S.at("ln"))
        S.did(nc.scalar.activation(out[:], out[:], ACT.Exp, scale=-0.5), "rstd")

    def norm_act(act, N, shift):
        act.preload_act_table_set(LN_EXP)
        if N.post:
            act.wait_ge(N.pe1.sem, N.pe1.at("sum"))
            inverse_root(act, N.a1, rstd, ps[5], D)
        if N.pre:
            for n in range(KT):
                if N.post:
                    act.wait_ge(N.vx.sem, N.vx.at(f"x{n}"))
                elif n == 0:
                    act.wait_ge(x_landed, 16)
                if n >= 2:
                    act.wait_ge(N.pe2.sem, N.pe2.at("sum", n - 2))
                N.asq.did(nc.scalar.activation(sq[n % 2][:], x[:, n, :], ACT.Square), "sq")
            act.wait_ge(N.pe2.sem, N.pe2.at("sum", KT - 1))
            inverse_root(act, N.a2, rms, ps[7], D)
            for n in range(KT):
                act.wait_ge(N.vt.sem, N.vt.at("t", n))
                N.ah.did(nc.scalar.activation(u_hi[:, n, :], sq[n % 2][:], ACT.Identity, bias=shift(n)), "hi")

    def norm_pool(pool, N):
        pool.wait_ge(N.a1.sem, N.a1.at("rstd"))
        for n in POOL_TILES:
            N.pt.did(nc.gpsimd.tensor_tensor(m[:, n, :], m[:, n, :], rstd[:], ALU.mult), f"t{n}")

    def norm_dve(dve, N, gain, scale, shift, wait_cols=None):
        if N.post:
            dve.wait_ge(N.a1.sem, N.a1.at("rstd"))
            for n in range(KT):
                if n in POOL_TILES:
                    dve.wait_ge(N.pt.sem, N.pt.at(f"t{n}"))
                else:
                    N.vx.did(nc.vector.tensor_tensor(m[:, n, :], m[:, n, :], rstd[:], ALU.mult), f"t{n}")
                    dve.wait_ge(N.vx.sem, N.vx.at(f"t{n}"))
                N.vx.did(nc.vector.scalar_tensor_tensor(x[:, n, :], m[:, n, :], gain(n), x[:, n, :],
                                                        ALU.mult, ALU.add), f"x{n}")
        if N.pre:
            if wait_cols:
                wait_cols()
            dve.wait_ge(N.a2.sem, N.a2.at("rstd"))

            def low(n):
                dve.wait_ge(N.ah.sem, N.ah.at("hi", n))
                N.vl.did(nc.vector.scalar_tensor_tensor(u_lo[:, n, :], sq[n % 2][:], shift(n),
                                                        u_hi[:, n, :].bitcast(f32), ALU.add, ALU.subtract), "lo")

            for n in range(KT):
                if n >= 2:
                    low(n - 2)
                    dve.wait_ge(N.vl.sem, N.vl.at("lo", n - 2))
                N.vt.did(nc.vector.scalar_tensor_tensor(sq[n % 2][:], x[:, n, :], scale(n), rms[:],
                                                        ALU.mult, ALU.mult), "t")
            low(KT - 2)
            low(KT - 1)

    def out_pe(pe, og, base, ks, hi, lo, ready=None, extra=None):
        nch = len(ks)
        og_body = 2
        with pe.Fori(0, KT // og_body) as it:
            for s in range(og_body):
                pe.wait_ge(og.act.sem, og.act.at("sq", og_body * it + s - 2))
                for j, nk in enumerate(ks):
                    c = s * nch + j
                    gemm_chunk(pe, base + og_body * nch * it + c, (base + c) % SPLIT, ps[s][:],
                               lambda k, o=sum(ks[:j]): hi(o + k), lambda k, o=sum(ks[:j]): lo(o + k), 0, nk,
                               j == 0, j == nch - 1,
                               tile_wait=(lambda k, o=sum(ks[:j]): ready(o + k)) if ready and s == 0 else None)
            if extra:
                extra(it)

    def out_act(act, og, base, ks):
        nch = len(ks)
        og.act.open(act)
        with act.Fori(0, KT // 2) as it:
            for s in range(2):
                act.wait_ge(gemm_done, base + 2 * nch * it + (s + 1) * nch)
                og.act.did(nc.scalar.activation(m[:, bass.ds(2 * it + s, 1), :], ps[s][:], ACT.Identity), "copy")
                act.wait_ge(og.dve.sem, og.dve.at("acc", 2 * it + s - 2))
                og.act.did(nc.scalar.activation(sq[s][:], ps[s][:], ACT.Square), "sq")

    def out_dve(dve, og, before=None, after=None):
        nc.vector.memset(acc[:], 0.0).then_inc(og.dve.sem, og.dve.credit * og.dve.n)
        with dve.Fori(0, KT // 2) as it:
            if before:
                before(it)
            for s in range(2):
                dve.wait_ge(og.act.sem, og.act.at("sq", 2 * it + s))
                dve.wait_ge(og.dve.sem, og.dve.at("acc", 2 * it + s - 1))
                og.dve.did(nc.vector.tensor_tensor(acc[:], acc[:], sq[s][:], ALU.add), "acc")
            if after:
                after(it)

    def prm_col(name, i=0):
        return prm[:, COL[name] + i:COL[name] + i + 1]

    def ada_dve_pieces(dve, turn, start=False):
        for s in range(ADA_BODY):
            b = s % 2
            if start:
                piece = ada_start[:, ADA_BODY * turn + s]
                dve.wait_ge(ada_start_landed[ADA_BODY * turn + s], 16)
            else:
                piece = ada_buf[b]
                dve.wait_ge(ada_landed[b], 32 * (turn - ADA_FIRST // ADA_BODY) + 16 * (s // 2) + 16)
            for k in range(KT):
                if k == 0:
                    ins = nc.vector.tensor_scalar(ada_acc[:, s, :], piece[:, 0, :], cvec[:, 0:1], None, ALU.mult)
                else:
                    dve.wait_ge(ada_link.sem, ada_link.at(f"l{s}{k - 1}", turn))
                    ins = nc.vector.scalar_tensor_tensor(ada_acc[:, s, :], piece[:, k, :], cvec[:, k:k + 1],
                                                         ada_acc[:, s, :], ALU.mult, ALU.add)
                if k < KT - 1:
                    ada_link.did(ins, f"l{s}{k}")
                else:
                    s_ada.did(ins, f"piece{s}")

    ada_link = Steps(ctx, nc, "ada_link", [f"l{s}{k}" for s in range(ADA_BODY) for k in range(KT - 1)])

    def ada_dve_mod(dve, turn):
        dve.wait_ge(p_ada.sem, p_ada.at("sums", turn))
        n = ADA_BODY * ADA_COLS // P
        s_ada.did(nc.vector.tensor_tensor(mod[:, bass.ds(n * turn, n)], ps[6][:, 0:n],
                                          prm[:, bass.ds(COL["ada_b"] + n * turn, n)], ALU.add), "mod")

    def ada_pe(pe, turn):
        pe.wait_ge(s_ada.sem, s_ada.at("mod", turn - 1))
        pe.wait_ge(s_ada.sem, s_ada.at(f"piece{ADA_BODY - 1}", turn))
        last = None
        for s in range(ADA_BODY):
            for h in range(ADA_COLS // P):
                j = s * (ADA_COLS // P) + h
                last = nc.tensor.matmul(ps[6][:, j:j + 1], ada_acc[:, s, h * P:(h + 1) * P], ones[:, 0:1],
                                        start=True, stop=True)
        p_ada.did(last, "sums")

    v_gate = Steps(ctx, nc, "gate_dve", ["one", "zi", "zf", "lf", "b", "m", "A", "D", "dcol", "pad", "ysum0"])
    a_gate = Steps(ctx, nc, "gate_act", ["abs", "exp", "ln", "E"])
    p_gate = Steps(ctx, nc, "gate_pe", ["dT"])
    cv = lambda i: [f"cv{i}_{j}" for j in range(CV_TAPS)] + [f"y{i}", f"ys{i}"]
    c4 = [f"c{pr_}{j}_{t}" for pr_ in "qk" for t in range(QK_TAPS) for j in range(2)]
    v_mix = Steps(ctx, nc, "mix_dve", ["hp", "dc", "diag", "gt0"] + cv(0) + ["gt1"] + cv(1) + c4
                  + [f"sp{i}" for i in range(NT)]
                  + ["dm", "dn", "d2", "vr", "h0", "h1", "hg0", "hg1"], credit=1)
    a_mix = Steps(ctx, nc, "mix_act", ["sg0", "sg1"] + [f"dg{i}" for i in range(NT)] + [f"off{i}" for i in range(NT - 1)]
                  + ["rq0", "rq1", "rk0", "rk1", "v0", "v1", "sq0", "sq1", "sk0", "sk1", "so0", "so1",
                     "vt0", "vt1", "n0", "n1", "ln", "rstd"], credit=1)
    p_mix = Steps(ctx, nc, "mix_pe", ["vt0", "vt1", "qk0", "qk1", "qk2", "qk3", "den", "num0", "num1", "hs"], credit=1)
    p_ln = Steps(ctx, nc, "ln_pe", ["mu"] + [f"s{n}" for n in range(KT)])
    a_ln = Steps(ctx, nc, "ln_act", [f"hh{n}" for n in range(KT)] + [f"sq{n}" for n in range(KT)] + ["ln", "rstd"]
                 + [x_ for n in range(KT) for x_ in (f"silu{n}", f"hi{n}")])
    v_ln = Steps(ctx, nc, "ln_dve", [f"hl{n}" for n in range(KT)] + ["mu"] + [f"yc{n}" for n in range(KT)]
                 + [f"t{n}" for n in range(KT)] + [f"lo{n}" for n in range(KT)])

    a_ff1 = Steps(ctx, nc, "ff1_act", ["g", "a", "silu", "hi"], credit=2)
    ff_c = [f"{n}{t}" for t in range(FF_TAPS) for n in "ga"]
    v_ff1 = Steps(ctx, nc, "ff1_dve", ["prm"] + ff_c + ["f", "lo"], credit=2)
    a_ff = [Steps(ctx, nc, f"ff{i}_act", ["silu", "hi"], credit=2) for i in (2, 3)]
    v_ff = [Steps(ctx, nc, f"ff{i}_dve", ["f", "lo"], credit=2) for i in (2, 3)]

    v_fg = Steps(ctx, nc, "fg_dve", ["one", "z", "lf", "c", "zero_hi", "zero_lo"])
    a_fg = Steps(ctx, nc, "fg_act", ["abs", "exp", "ln"])
    U = 2 * NT
    v_fox0 = Steps(ctx, nc, "fox0_dve", ["ql", "kl"])
    a_fox0 = Steps(ctx, nc, "fox0_act", ["q", "k", "v"])
    dve_steps, act_steps, pe_steps = ["N0", "r0", "s0", "lo"], ["e0", "hi"], ["L0", "pv1"]
    for n in range(U):
        if n + 1 < U:
            dve_steps += [f"N{n + 1}", f"pl{n}", f"r{n + 1}", f"s{n + 1}"]
            act_steps += [f"e{n + 1}", f"ph{n}"]
            pe_steps += [f"L{n + 1}"]
        pe_steps += [f"T{n}"]
        if n == 0:
            dve_steps += ["vl0", "vl1"]
            act_steps += ["vh0", "vh1"]
            pe_steps += ["vT"]
        if n == NT + 1:
            pe_steps += ["pv0"]
    v_fox = Steps(ctx, nc, "fox_dve", dve_steps + ["ql", "kl", f"pl{U - 1}"], credit=1)
    a_fox = Steps(ctx, nc, "fox_act", act_steps + ["q", "k", f"ph{U - 1}", "v"], credit=1)
    p_fox = Steps(ctx, nc, "fox_pe", pe_steps, credit=1)

    LEVELS = [64, 32, 16, 8, 4, 2, 1]
    v_hg0 = Steps(ctx, nc, "hgs_dve", ["mx", "mx2", "d0", "d1", "d2", "s", "s2", "r", "lb", "oml", "zero"])
    a_hg0 = Steps(ctx, nc, "hgs_act", ["e0", "e1", "e2", "q", "sig", "v"])
    hg_steps = ["cur", "f", "k", "gs"] + [f"b{j}" for j in range(NT)] + ["dl64", "dr64"]
    for i, w in enumerate(LEVELS):
        if i + 1 < len(LEVELS):
            hg_steps += [f"dl{LEVELS[i + 1]}", f"dr{LEVELS[i + 1]}"]
        hg_steps += [f"ml{w}", f"mr{w}"]
        if i:
            hg_steps += [f"pc{LEVELS[i - 1]}"]
        hg_steps += {0: ["o1", "o2"], 1: ["lo"]}.get(i, [])
    v_hg = Steps(ctx, nc, "hg_dve", hg_steps + ["qd", "kd", "x20", "x31", "x30", "pc1", "pc0"], credit=1)
    a_hg = Steps(ctx, nc, "hg_act", ["ln", "osq", "vt", "e64", "lnv", "rstd", "e32", "hi", "g"]
                 + [f"e{w}" for w in LEVELS[2:]] + ["et", "eb"]
                 + [f"ek{j}" for j in range(NT - 1)] + ["offA", "offB0", "offB1", "q", "sig", "sg", "v"], credit=1)
    p_hg = Steps(ctx, nc, "hg_pe", ["pv", "vT", "ss"] + [f"S{w}" for w in LEVELS] + ["S0", "offA", "offB"], credit=1)

    block = ctx.enter_context(nc.Block())

    @block.sync
    def _(sp_):
        sp_.dma_start(prm[:], params).then_inc(prm_landed, 16)
        sp_.dma_start(x[:], xT).then_inc(x_landed, 16)

        def load_ada(piece, s):
            src = ada[piece] if isinstance(piece, int) else ada[bass.ds(piece, 1), :, :].rearrange("o p c -> (o p) c")
            sp_.dma_start(ada_buf[s][:].rearrange("p k c -> p (k c)"), src).then_inc(ada_landed[s], 16)

        for p in range(ADA_FIRST):
            sp_.dma_start(ada_start[:, p].rearrange("p k c -> p (k c)"), ada[p]).then_inc(ada_start_landed[p], 16)

        def load_chunk(c, slot, wait=True):
            if wait:
                sp_.wait_ge(chunk_split, c - RAW + 1)
            src = wstream[c] if isinstance(c, int) else wstream[bass.ds(c, 1), :, :].rearrange("o p c -> (o p) c")
            sp_.dma_start(raw[slot][:], src).then_inc(raw_landed[slot], 16)

        for c in range(RAW):
            load_chunk(c, c, wait=False)
        with sp_.Fori(1, C_WOUT1 // RAW) as it:
            for s in range(RAW):
                load_chunk(RAW * it + s, s)
        for c in range(C_WOUT1 // RAW * RAW, C_WOUT1):
            load_chunk(c, c % RAW)
        with sp_.Fori(0, 2 * KT // RAW) as it:
            for s in range(RAW):
                load_chunk(C_WOUT1 + RAW * it + s, (C_WOUT1 + s) % RAW)
                turn = ADA_FIRST // ADA_BODY + it
                if s >= 2:
                    sp_.wait_ge(s_ada.sem, s_ada.at(f"piece{s - 2}", turn))
                else:
                    sp_.wait_ge(s_ada.sem, s_ada.at(f"piece{s + 2}", turn - 1))
                    if s == 0 or s == 1:
                        sp_.wait_ge(v_ln.sem, v_ln.at("mu"))
                load_ada(ADA_FIRST + ADA_BODY * it + s, s % 2)
        rest = C_WOUT1 + 2 * KT
        with sp_.Fori(0, (C_END - rest) // RAW) as it:
            for s in range(RAW):
                load_chunk(rest + RAW * it + s, (rest + s) % RAW)
        for c in range(rest + (C_END - rest) // RAW * RAW, C_END):
            load_chunk(c, c % RAW)

    @block.gpsimd
    def _(pool):
        g = nc.gpsimd
        g.memset(ones[:], 1.0).then_inc(const_ready, 1)
        g.memset(ident[:], 0.0).then_inc(const_ready, 1)
        g.memset(early[:], 0.0).then_inc(const_ready, 1)
        g.memset(late_b[:], 0.0).then_inc(const_ready, 1)
        g.memset(ident_b[:], 0.0).then_inc(const_ready, 1)
        g.memset(zero_col[:], 0.0).then_inc(const_ready, 1)
        g.memset(eps_col[:, 0:1], EPS)
        g.memset(eps_col[:, 1:2], 1e-37).then_inc(const_ready, 1)
        pool.wait_ge(const_ready, 7)
        for t in (ident, ident_b):
            g.affine_select(out=t[:], in_=t[:], compare_op=ALU.not_equal, fill=1.0, base=0, pattern=[[-1, P]],
                            channel_multiplier=1).then_inc(const_ready, 1)
        g.affine_select(out=early[:], in_=early[:], compare_op=ALU.is_ge, fill=-BIG, base=0, pattern=[[1, P]],
                        channel_multiplier=-1).then_inc(const_ready, 1)
        g.affine_select(out=late_b[:], in_=late_b[:], compare_op=ALU.is_ge, fill=BIG, base=0, pattern=[[-1, P]],
                        channel_multiplier=1).then_inc(const_ready, 1)
        g.iota(levels[:, 0, :], pattern=[[0, P]], base=0, channel_multiplier=1).then_inc(const_ready, 1)
        g.iota(levels[:, 1, :], pattern=[[1, P]], base=0, channel_multiplier=0).then_inc(const_ready, 1)

        def split(c, rslot, slot, landed, wait=True):
            pool.wait_ge(raw_landed[rslot], landed)
            if wait:
                pool.wait_ge(gemm_done, c - SPLIT + 1)
            g.tensor_tensor(w_hi[slot][:], raw[rslot][:], ones[:, 0:1].to_broadcast([P, D]),
                            ALU.mult).then_inc(chunk_hi, 1)
            pool.wait_ge(chunk_hi, c + 1)
            g.tensor_tensor(w_lo[slot][:], raw[rslot][:], w_hi[slot][:].bitcast(f32),
                            ALU.subtract).then_inc(chunk_split, 1)

        def split_range(first, end):
            with pool.Fori(0, (end - first) // RAW) as it:
                for s in range(RAW):
                    c = first + s
                    split(c + RAW * it, c % RAW, c % SPLIT, 16 * it + 16 * (c // RAW) + 16)
            for c in range(end - (end - first) % RAW, end):
                split(c, c % RAW, c % SPLIT, 16 * (c // RAW) + 16)

        for c in range(SPLIT):
            split(c, c, c, 16, wait=False)
        at = SPLIT
        for N, base in zip(norms[1:], (C_UP1, C_GATE2, C_UP2, C_HG, C_UP3, C_END)):
            end = min(base + SPLIT, C_END)
            split_range(at, end)
            norm_pool(pool, N)
            at = end

    @block.tensor
    def _(pe):
        pe.wait_ge(const_ready, 13)
        pe.wait_ge(v_set.sem, v_set.at("c"))
        norm_pe(pe, norms[0], None)
        for turn in range(ADA_FIRST // ADA_BODY):
            ada_pe(pe, turn)

        N0 = norms[0]
        gemm_chunk(pe, C_GATE1, 0, ps[5][:], u_tiles, u_lows, 0, KT, True, True,
                   tile_wait=lambda k: pe.wait_ge(N0.vl.sem, N0.vl.at("lo", k)))
        pe.wait_ge(v_gate.sem, v_gate.at("D"))
        for st in range(NT):
            last = nc.tensor.matmul(ps[4][:, st * H1:(st + 1) * H1], rD[0:H1, st * P:(st + 1) * P],
                                    ident[0:H1, 0:H1], start=True, stop=True)
        p_gate.did(last, "dT")

        p_mix.open(pe)
        with pe.Fori(0, H1) as h:
            before = {0: (a_mix, "v0", -1), 1: (a_mix, "v1", -1), 2: (a_mix, "so0", -1), 3: (a_mix, "so1", -1),
                      4: (a_mix, "sg0", 0), 5: (v_mix, "gt0", 0), 6: (a_mix, "sg1", 0), 7: (v_mix, "gt1", 0),
                      8: (a_mix, "rq0", 0), 9: (a_mix, "rq1", 0), 10: (a_mix, "rk0", 0), 11: (a_mix, "rk1", 0)}
            for j in range(12):
                S, step, back = before[j]
                pe.wait_ge(S.sem, S.at(step, h + back))
                gemm_chunk(pe, C_MIX + 12 * h + j, (C_MIX + j) % SPLIT, ps[j % 4][:], u_tiles, u_lows, 0, KT, True, True)
            pe.wait_ge(v_mix.sem, v_mix.at("hg1", h - 1))
            for e in range(2):
                pe.wait_ge(a_mix.sem, a_mix.at(f"v{e}", h))
                for st in range(NT):
                    last = nc.tensor.transpose(ps[4 + e][:, st * P:(st + 1) * P], vf[:, e, st * P:(st + 1) * P], ident[:])
                p_mix.did(last, f"vt{e}")
            bank = [6, 7, 4, 5]
            pe.wait_ge(a_mix.sem, a_mix.at("sk1", h))
            for st in range(NT):
                if st >= 2:
                    pe.wait_ge(a_mix.sem, a_mix.at(f"vt{st - 2}", h))
                p_mix.did(matmuls(ps[bank[st]][:, 0:T - st * P],
                                  [(qk[:, 2 + e, st * P:(st + 1) * P], qk[:, e, st * P:T]) for e in range(2)]), f"qk{st}")
            pe.wait_ge(v_mix.sem, v_mix.at(f"sp{NT - 1}", h))
            for name, b, w in (("den", 7, None), ("num0", 6, 0), ("num1", 4, 1)):
                for st in range(NT):
                    last = nc.tensor.matmul(ps[b][:, st * P:T], ones[:] if w is None else vt[:, w, st, :],
                                            sp[:, WOFF[st]:WOFF[st] + T - st * P], start=(st == 0), stop=(st == NT - 1))
                p_mix.did(last, name)
            for e in range(2):
                pe.wait_ge(a_mix.sem, a_mix.at(f"n{e}", h))
                last = nc.tensor.matmul(ps[5][:], ones[:], sq[e][:], start=(e == 0), stop=(e == 1))
            p_mix.did(last, "hs")

        pe.wait_ge(v_mix.sem, v_mix.at("hg1", H1 - 1))
        p_ln.did(nc.tensor.matmul(ps[4][:], ones[:], acc[:], start=True, stop=True), "mu")
        for n in range(KT):
            pe.wait_ge(a_ln.sem, a_ln.at(f"sq{n}"))
            p_ln.did(nc.tensor.matmul(ps[5][:], ones[:], sq[n % 2][:], start=(n == 0), stop=(n == KT - 1)), f"s{n}")
        out_pe(pe, outs[0], C_WOUT1, (8, 8), lambda k: (u_hi if k < KT else y_hi)[:, k % KT, :],
               lambda k: (u_lo if k < KT else y_lo)[:, k % KT, :],
               ready=lambda k: pe.wait_ge(v_ln.sem, v_ln.at(f"hl{k}" if k < KT else f"lo{k - KT}")),
               extra=lambda it: ada_pe(pe, ADA_FIRST // ADA_BODY + it))

        def ffn_pe(N, base, dbase, read, og, prev):
            def read_wait(j, name, s):
                S, step = read[name]
                pe.wait_ge(S.sem, S.at(step, 2 * j + s - 2))
            with pe.Fori(0, FT // 2) as it:
                for s in range(2):
                    for j, name in enumerate("ga"):
                        read_wait(it, name, s)
                        c = 2 * s + j
                        gemm_chunk(pe, base + 4 * it + c, (base + c) % SPLIT, ps[c][:], u_tiles, u_lows, 0, KT, True, True,
                                   tile_wait=(lambda k: pe.wait_ge(N.vl.sem, N.vl.at("lo", k))) if c == 0 else None)
            S, step = prev
            out_pe(pe, og, dbase, DOWN_K, lambda k: f_hi[:, k, :], lambda k: f_lo[:, k, :],
                   ready=lambda k: pe.wait_ge(S.sem, S.at(step, k)))

        norm_pe(pe, norms[1], outs[0])
        ffn_pe(norms[1], C_UP1, C_DOWN1, {"g": (a_ff1, "g"), "a": (a_ff1, "a")}, outs[1], (v_ff1, "lo"))
        norm_pe(pe, norms[2], outs[1])

        N = norms[2]
        gemm_chunk(pe, C_GATE2, C_GATE2 % SPLIT, ps[3][:], u_tiles, u_lows, 0, KT, True, True,
                   tile_wait=lambda k: pe.wait_ge(N.vl.sem, N.vl.at("lo", k)))

        FOX_PAIRS = FOX_H // 2

        def fox_gemm(i, par, hook=lambda kk: None):
            for j, (S, step) in enumerate(((v_fox, "ql"), (v_fox, "kl"), (a_fox, "v"))):
                if not (isinstance(i, int) and i == 0):
                    pe.wait_ge(S.sem, S.at(step, i - 2))
                gemm_chunk(pe, C_FOX + 3 * i + j, (C_FOX + 3 * par + j) % SPLIT, ps[j][:], u_tiles, u_lows, 0, KT,
                           True, True, hook=lambda k, j=j: hook(KT * j + k))

        def fox_values(i):
            pe.wait_ge(a_fox.sem, a_fox.at("v", i - 1))
            pe.wait_ge(v_fox.sem, v_fox.at("lo", i))
            for st in range(NT):
                last = nc.tensor.transpose(ps[3][:, st * P:(st + 1) * P], fv[:, st * P:(st + 1) * P], ident[:])
            p_fox.did(last, "vT")

        def fox_logits(i, n):
            a, r = divmod(n, NT)
            rows, qs, ks = slice(a * FOX_D, (a + 1) * FOX_D), slice(r * P, (r + 1) * P), slice(0, (r + 1) * P)
            if n == 0:
                pe.wait_ge(v_fox.sem, v_fox.at("kl", i - 1))
            if n >= 2:
                pe.wait_ge(v_fox.sem, v_fox.at(f"N{n - 2}", i))
            for j, (l_, r_) in enumerate(tri(q_hi[rows, qs], q_lo[rows, qs], k_hi[rows, ks], k_lo[rows, ks])):
                nc.tensor.matmul(ps[4 + n % 2][:, ks], l_, r_, start=(j == 0), stop=False)
            p_fox.did(nc.tensor.matmul(ps[4 + n % 2][:, qs], ident_b[:], late_b[:], start=False, stop=True), f"L{n}")

        def fox_turn(i, n):
            r = n % NT
            pe.wait_ge(v_fox.sem, v_fox.at(f"s{n}", i))
            if n >= 2:
                pe.wait_ge(v_fox.sem, v_fox.at(f"pl{n - 2}", i))
            for st in range(r + 1):
                last = nc.tensor.transpose(ps[6 + n % 2][:, st * P:(st + 1) * P], pr[n % 2][:, st * P:(st + 1) * P],
                                           ident[:])
            p_fox.did(last, f"T{n}")

        def fox_weigh(i, a):
            pe.wait_ge(v_fox.sem, v_fox.at(f"pl{NT * a + NT - 1}", i))
            for st in range(NT):
                ts = slice(st * P, T)
                for j, (l_, r_) in enumerate(tri(va_hi[:, a, st, :], va_lo[:, a, st, :], pt_hi[a][:, st, ts],
                                                 pt_lo[a][:, st, ts])):
                    last = nc.tensor.matmul(ps[3][:, ts], l_, r_, start=(a == 0 and st == 0 and j == 0),
                                            stop=(a == 1 and st == NT - 1 and j == 2))
            p_fox.did(last, f"pv{a}")

        def fox_turn_pe(i, par, lag=True, gemm=True):
            def hook(kk):
                if kk == 1:
                    if lag:
                        fox_weigh(i - 1, 1)
                    else:
                        p_fox.skip(pe, i, "pv1")
                elif kk == 4:
                    fox_values(i)
                elif kk % 3 == 2:
                    n = kk // 3
                    if n + 1 < U:
                        fox_logits(i, n + 1)
                    fox_turn(i, n)
                    if n == NT + 1:
                        fox_weigh(i, 0)
            fox_logits(i, 0)
            if gemm:
                fox_gemm(i + 1, par, hook)
            else:
                for kk in range(3 * KT):
                    hook(kk)

        p_fox.open(pe)
        fox_gemm(0, 0)
        pe.wait_ge(v_fg.sem, v_fg.at("zero_lo"))
        pe.wait_ge(v_fox0.sem, v_fox0.at("kl"))
        pe.wait_ge(a_fox0.sem, a_fox0.at("v"))
        fox_turn_pe(0, 1, lag=False)
        with pe.Fori(0, FOX_PAIRS // 2 - 1) as it:
            for sub in range(2):
                fox_turn_pe(2 * it + sub + 1, sub)
        fox_turn_pe(FOX_PAIRS - 1, 0, gemm=False)
        p_fox.skip(pe, FOX_PAIRS, "L0")
        fox_weigh(FOX_PAIRS - 1, 1)
        out_pe(pe, outs[2], C_FOXOUT, (KT,), lambda k: a_hi[:, k, :], lambda k: a_lo[:, k, :],
               ready=lambda k: pe.wait_ge(v_fox.sem, v_fox.at("lo", k + 1)))
        norm_pe(pe, norms[3], outs[2])
        ffn_pe(norms[3], C_UP2, C_DOWN2, {"g": (a_ff[0], "silu"), "a": (v_ff[0], "f")}, outs[3], (v_ff[0], "lo"))
        norm_pe(pe, norms[4], outs[3])

        N4 = norms[4]

        def hg_gemm(i, hook=lambda kk: None, wait=None):
            for j, step in enumerate(("q", "sig", "v", "g")):
                if not (isinstance(i, int) and i == 0):
                    pe.wait_ge(a_hg.sem, a_hg.at(step, i - 1 if step == "g" else i - 2))
                gemm_chunk(pe, C_HG + 4 * i + j, (C_HG + j) % SPLIT, ps[j][:], u_tiles, u_lows, 0, KT, True, True,
                           tile_wait=wait if j == 0 else None, hook=lambda k, j=j: hook(KT * j + k))

        def hg_level(i, n):
            src = hl[n % 2] if n < len(LEVELS) else None
            b = 5 + n % 2
            if n >= 2:
                pe.wait_ge(v_hg.sem, v_hg.at(f"pc{LEVELS[n - 2]}", i))
            if src is not None:
                pe.wait_ge(v_hg.sem, v_hg.at(f"mr{LEVELS[n]}", i))
            for t in range(NT):
                ts = slice(t * P, (t + 1) * P)
                last = nc.tensor.matmul(ps[b][:, ts], (hk if src is None else src)[:, ts],
                                        (hq if src is None else src)[:, ts], start=True, stop=True)
            p_hg.did(last, f"S{LEVELS[n]}" if src is not None else "S0")

        def hg_off(i, which):
            tile_ = lambda t_, j: t_[:, j * P:(j + 1) * P]
            if which == "offA":
                pe.wait_ge(v_hg.sem, v_hg.at("x30", i))
                blocks_ = [(tile_(hkd, 0), 1), (hkx[:, 0, :], 2), (hkx[:, 2, :], 3)]
                bank_ = 7
            else:
                pe.wait_ge(a_hg.sem, a_hg.at("lnv", i))
                blocks_ = [(tile_(hkd, 1), 2), (hkx[:, 1, :], 3), (tile_(hkd, 2), 3)]
                bank_ = 4
            for n, (l_, t) in enumerate(blocks_):
                last = nc.tensor.matmul(ps[bank_][:, n * P:(n + 1) * P], l_, tile_(hqd, t), start=True, stop=True)
            p_hg.did(last, which)

        def hg_weigh(i):
            pe.wait_ge(v_hg.sem, v_hg.at("pc0", i - 1))
            pe.wait_ge(a_hg.sem, a_hg.at("offB1", i - 1))
            for c in range(NT):
                last = nc.tensor.matmul(ps[7][:, c * P:T], hvt[:, c, :], hsc[:, c, c * P:T], start=(c == 0),
                                        stop=(c == NT - 1))
            p_hg.did(last, "pv")

        def hg_squares(i):
            pe.wait_ge(a_hg.sem, a_hg.at("vt", i))
            p_hg.did(nc.tensor.matmul(ps[4][:], ones[:], ho2[:], start=True, stop=True), "ss")

        def hg_turn_pe(i, lag=True, gemm=True):
            def hook(kk):
                n, rest_ = divmod(kk - 4, 3)
                if kk == 0:
                    if lag:
                        hg_weigh(i)
                    else:
                        p_hg.skip(pe, i, "pv")
                elif kk == 1:
                    pe.wait_ge(a_hg.sem, a_hg.at("v", i - 1))
                    for st in range(NT):
                        last = nc.tensor.transpose(ps[4][:, st * P:(st + 1) * P], hv[:, st * P:(st + 1) * P], ident[:])
                    p_hg.did(last, "vT")
                elif kk == 3:
                    if lag:
                        hg_squares(i)
                    else:
                        p_hg.skip(pe, i, "ss")
                elif rest_ == 0 and n < len(LEVELS) + 1:
                    hg_level(i, n)
                elif kk == 4 + 3 * (len(LEVELS) + 1):
                    hg_off(i, "offA")
                    hg_off(i, "offB")
            if gemm:
                hg_gemm(i + 1, hook)
            else:
                for kk in range(4 * KT):
                    hook(kk)

        p_hg.open(pe)
        hg_gemm(0, wait=lambda k: pe.wait_ge(N4.vl.sem, N4.vl.at("lo", k)))
        pe.wait_ge(a_hg0.sem, a_hg0.at("v"))
        hg_turn_pe(0, lag=False)
        with pe.Fori(1, HG_H - 1) as i:
            hg_turn_pe(i)
        hg_turn_pe(HG_H - 1, gemm=False)
        hg_weigh(HG_H)
        p_hg.skip(pe, HG_H, "vT")
        hg_squares(HG_H)
        out_pe(pe, outs[4], C_HGOUT, (KT,), lambda k: g_hi[:, k, :], lambda k: g_lo[:, k, :],
               ready=lambda k: pe.wait_ge(v_hg.sem, v_hg.at("lo", k + 1)))
        norm_pe(pe, norms[5], outs[4])
        ffn_pe(norms[5], C_UP3, C_DOWN3, {"g": (a_ff[1], "silu"), "a": (v_ff[1], "f")}, outs[5], (v_ff[1], "lo"))
        norm_pe(pe, norms[6], outs[5])

    @block.scalar
    def _(act):
        A = nc.scalar.activation
        act.wait_ge(prm_landed, 16)
        a_set.did(A(cvec[:], prm[:, COL["c"]:COL["c"] + KT], ACT.Sigmoid), "sig_c")
        act.wait_ge(const_ready, 13)
        norm_act(act, norms[0], lambda n: mod[:, n:n + 1])

        act.wait_ge(v_gate.sem, v_gate.at("zf"))
        a_gate.did(A(rb[0:H1, :], rlf[0:H1, :], ACT.Abs), "abs")
        act.wait_ge(a_gate.sem, a_gate.at("abs"))
        a_gate.did(A(rb[0:H1, :], rb[0:H1, :], ACT.Exp, scale=-1.0), "exp")
        act.wait_ge(a_gate.sem, a_gate.at("exp"))
        a_gate.did(A(rb[0:H1, :], rb[0:H1, :], ACT.Ln, bias=1.0), "ln")
        act.wait_ge(v_gate.sem, v_gate.at("A"))
        a_gate.did(A(rm[0:H1, :], rm[0:H1, :], ACT.Exp, scale=-1.0), "E")
        act.dma_start(rows1[0], rA[0:H1, :]).then_inc(rows_out, 16)
        act.wait_ge(a_gate.sem, a_gate.at("E"))
        act.dma_start(rows1[1], rm[0:H1, :]).then_inc(rows_out, 16)
        act.wait_ge(rows_out, 32)

        act.wait_ge(v_gate.sem, v_gate.at("ysum0"))
        a_mix.open(act)
        with act.Fori(0, H1) as h:
            act.wait_ge(v_mix.sem, v_mix.at("dn", h - 1))
            act.dma_start(bc[:], rows1[:, bass.ds(h, 1), :].rearrange("a h t -> h a t").to_broadcast([P, 2, T]))\
               .then_inc(bc_landed, 16)
            for j in range(2):
                act.wait_ge(gemm_done, C_MIX + 12 * h + 2 * j + 1)
                act.wait_ge(v_mix.sem, v_mix.at(f"gt{j}", h - 1))
                a_mix.did(A(sg[j][:], ps[2 * j][:], ACT.Sigmoid), f"sg{j}")
            act.wait_ge(v_mix.sem, v_mix.at("diag", h))
            act.wait_ge(bc_landed, 16 * h + 16)
            for st in range(NT):
                a_mix.did(A(wt[:, WOFF[st]:WOFF[st] + P], dg[:, st, :], ACT.Exp, bias=dcur[:, st:st + 1]), f"dg{st}")
            for st in range(NT - 1):
                a_mix.did(A(wt[:, WOFF[st] + P:WOFF[st] + T - st * P], bc[:, 0, (st + 1) * P:T], ACT.Exp,
                            bias=dcur[:, st:st + 1]), f"off{st}")
            for j, name in enumerate(("rq0", "rq1", "rk0", "rk1")):
                act.wait_ge(gemm_done, C_MIX + 12 * h + 4 + j + 1)
                if j == 0:
                    act.wait_ge(v_mix.sem, v_mix.at(f"ck1_{QK_TAPS - 1}", h - 1))
                a_mix.did(A(qk_raw[:, j, 3:], ps[j][:], ACT.Identity), name)
            for j in range(2):
                act.wait_ge(gemm_done, C_MIX + 12 * h + 8 + j + 1)
                if j == 0:
                    act.wait_ge(p_mix.sem, p_mix.at("vt1", h - 1))
                a_mix.did(A(vf[:, j, :], ps[j][:], ACT.Identity), f"v{j}")
            for j, name in enumerate(("sq0", "sq1", "sk0", "sk1")):
                act.wait_ge(v_mix.sem, v_mix.at(f"c{'qk'[j // 2]}{j % 2}_{QK_TAPS - 1}", h))
                a_mix.did(A(qk[:, j, :], qk[:, j, :], ACT.Silu, bias=hp[:, HP_QKB + j:HP_QKB + j + 1]), name)
            for j in range(2):
                act.wait_ge(gemm_done, C_MIX + 12 * h + 10 + j + 1)
                if j == 0:
                    act.wait_ge(v_mix.sem, v_mix.at("hg1", h - 1))
                a_mix.did(A(so[:, j, :], ps[2 + j][:], ACT.Sigmoid), f"so{j}")
            act.preload_act_table_set(LN_EXP)
            for e in range(2):
                act.wait_ge(p_mix.sem, p_mix.at(f"vt{e}", h))
                a_mix.did(A(vt[:, e, :, :], ps[4 + e][:], ACT.Identity), f"vt{e}")
            for e in range(2):
                act.wait_ge(p_mix.sem, p_mix.at(f"num{e}", h))
                a_mix.did(A(sq[e][:], ps[6 if e == 0 else 4][:], ACT.Square), f"n{e}")
            act.wait_ge(v_mix.sem, v_mix.at("vr", h))
            a_mix.did(A(cB[:], cA[:], ACT.Ln, bias=eps_col[:, 1:2]), "ln")
            act.wait_ge(a_mix.sem, a_mix.at("ln", h))
            a_mix.did(A(rstd[:], cB[:], ACT.Exp, scale=-0.5), "rstd")

        act.wait_ge(v_mix.sem, v_mix.at("hg1", H1 - 1))
        for n in range(KT):
            a_ln.did(A(u_hi[:, n, :], hm[:, n, :], ACT.Identity), f"hh{n}")
        for n in range(KT):
            act.wait_ge(v_ln.sem, v_ln.at(f"yc{n}"))
            if n >= 2:
                act.wait_ge(p_ln.sem, p_ln.at(f"s{n - 2}"))
            a_ln.did(A(sq[n % 2][:], y[:, n, :], ACT.Square), f"sq{n}")
        act.wait_ge(p_ln.sem, p_ln.at(f"s{KT - 1}"))
        inverse_root(act, a_ln, rstd, ps[5], D)
        for n in range(KT):
            act.wait_ge(v_ln.sem, v_ln.at(f"t{n}"))
            a_ln.did(A(y[:, n, :], y[:, n, :], ACT.Silu, bias=prm_col("ln_b", n), scale=prm_col("ln_g", n)), f"silu{n}")
            act.wait_ge(a_ln.sem, a_ln.at(f"silu{n}"))
            a_ln.did(A(y_hi[:, n, :], y[:, n, :], ACT.Identity), f"hi{n}")
        out_act(act, outs[0], C_WOUT1, (8, 8))
        norm_act(act, norms[1], lambda n: mod[:, 24 + n:25 + n])

        act.wait_ge(ff1_pads, 2)
        a_ff1.open(act)
        with act.Fori(0, FT // 2) as it:
            for s in range(2):
                j = 2 * it + s
                for n, name in enumerate("ga"):
                    act.wait_ge(gemm_done, C_UP1 + 4 * it + 2 * s + n + 1)
                    act.wait_ge(v_ff1.sem, v_ff1.at(f"{name}{FF_TAPS - 1}", j - 1))
                    a_ff1.did(A(fraw[n][:, 2:], ps[2 * s + n][:], ACT.Identity), name)
                act.wait_ge(v_ff1.sem, v_ff1.at(f"g{FF_TAPS - 1}", j))
                a_ff1.did(A(fsi[:], fcv[0][:], ACT.Silu, bias=fprm[:, 6:7]), "silu")
                act.wait_ge(v_ff1.sem, v_ff1.at("f", j))
                a_ff1.did(A(f_hi[:, bass.ds(j, 1), :], fval[:], ACT.Identity), "hi")
        out_act(act, outs[1], C_DOWN1, DOWN_K)
        norm_act(act, norms[2], lambda n: zero_col[:, n:n + 1])

        act.wait_ge(v_fg.sem, v_fg.at("z"))
        a_fg.did(A(fl[0:FOX_H, :], fz[0:FOX_H, :], ACT.Abs), "abs")
        act.wait_ge(a_fg.sem, a_fg.at("abs"))
        a_fg.did(A(fl[0:FOX_H, :], fl[0:FOX_H, :], ACT.Exp, scale=-1.0), "exp")
        act.wait_ge(a_fg.sem, a_fg.at("exp"))
        a_fg.did(A(fl[0:FOX_H, :], fl[0:FOX_H, :], ACT.Ln, bias=1.0), "ln")
        act.wait_ge(v_fg.sem, v_fg.at("c"))
        act.dma_start(rows2, fc[0:FOX_H, :]).then_inc(rows_out, 16)
        act.wait_ge(rows_out, 48)

        def fox_round(S, i, what):
            j = "qkv".index(what)
            act.wait_ge(gemm_done, C_FOX + 3 * i + j + 1)
            if S is a_fox and what in "qk":
                act.wait_ge(p_fox.sem, p_fox.at(f"L{U - 1}", i - 1))
            if S is a_fox and what == "v":
                act.wait_ge(p_fox.sem, p_fox.at("vT", i - 1))
            if what == "q":
                ins = A(q_hi[:], ps[0][:], ACT.Identity, scale=-float(FOX_D) ** -0.5)
            else:
                ins = A({"k": k_hi, "v": fv}[what][:], ps[j][:], ACT.Identity)
            S.did(ins, what)

        def fox_cbc(i, b):
            rows = rows2[2 * i:2 * i + 2, :] if isinstance(i, int) else rows2[bass.ds(2 * i, 2), :]
            act.dma_start(cbc[b][:], rows.unsqueeze(0).to_broadcast([P, 2, T])).then_inc(bc_landed, 16)

        fox_cbc(0, 0)
        for what in "qkv":
            fox_round(a_fox0, 0, what)

        def fox_act_turn(i, b, lag=True, nxt=True):
            def expo(n):
                r = n % NT
                act.wait_ge(v_fox.sem, v_fox.at(f"N{n}", i))
                if n >= 2:
                    act.wait_ge(p_fox.sem, p_fox.at(f"T{n - 2}", i))
                a_fox.did(A(pr[n % 2][:, 0:(r + 1) * P], lg[n % 2][:, 0:(r + 1) * P], ACT.Exp, scale=-1.0,
                            bias=mx[:, n % 2:n % 2 + 1], accum_out=row_sum[:, n % 2:n % 2 + 1]), f"e{n}")

            def high(n):
                a, r = divmod(n, NT)
                act.wait_ge(p_fox.sem, p_fox.at(f"T{n}", i))
                a_fox.did(A(pt_hi[a][:, 0:r + 1, r * P:(r + 1) * P],
                            ps[6 + n % 2][:, 0:(r + 1) * P].rearrange("p (s c) -> p s c", c=P), ACT.Identity), f"ph{n}")

            expo(0)
            if lag:
                fox_result(i)
            else:
                a_fox.skip(act, i, "hi")
            if nxt:
                act.wait_ge(v_fox.sem, v_fox.at("N0", i))
                fox_cbc(i + 1, 1 - b)
            for n in range(U - 1):
                expo(n + 1)
                high(n)
                if n == 0:
                    act.wait_ge(p_fox.sem, p_fox.at("vT", i))
                    for a in range(2):
                        cols = slice(a * FOX_D, (a + 1) * FOX_D)
                        a_fox.did(A(va_hi[:, a, :, cols], ps[3][:].rearrange("p (s c) -> p s c", c=P)[:, :, cols],
                                    ACT.Identity), f"vh{a}")
            if nxt:
                for what in "qk":
                    fox_round(a_fox, i + 1, what)
            else:
                a_fox.skip(act, i, "q", "k")
            high(U - 1)
            if nxt:
                fox_round(a_fox, i + 1, "v")
            else:
                a_fox.skip(act, i, "v")

        def fox_result(i):
            act.wait_ge(p_fox.sem, p_fox.at("pv1", i))
            dst = a_hi[:, i - 1, :] if isinstance(i, int) else a_hi[:, bass.ds(i - 1, 1), :]
            a_fox.did(A(dst, ps[3][:], ACT.Identity), "hi")

        a_fox.open(act)
        act.wait_ge(v_fg.sem, v_fg.at("zero_lo"))
        PAIRS = FOX_H // 2
        fox_act_turn(0, 0, lag=False)
        with act.Fori(0, PAIRS // 2 - 1) as it:
            for sub in range(2):
                fox_act_turn(2 * it + sub + 1, 1 - sub)
        fox_act_turn(PAIRS - 1, 1, nxt=False)
        a_fox.skip(act, PAIRS, "e0")
        fox_result(PAIRS)
        out_act(act, outs[2], C_FOXOUT, (KT,))
        norm_act(act, norms[3], lambda n: zero_col[:, n:n + 1])

        def ffn_act(aS, vS, base):
            aS.open(act)
            with act.Fori(0, FT // 2) as it:
                for s in range(2):
                    j = 2 * it + s
                    act.wait_ge(gemm_done, base + 4 * it + 2 * s + 1)
                    act.wait_ge(vS.sem, vS.at("f", j - 2))
                    aS.did(A(fcv[s][:], ps[2 * s][:], ACT.Silu), "silu")
                    act.wait_ge(vS.sem, vS.at("f", j))
                    aS.did(A(f_hi[:, bass.ds(j, 1), :], fraw[s][:, 0:T], ACT.Identity), "hi")

        ffn_act(a_ff[0], v_ff[0], C_UP2)
        out_act(act, outs[3], C_DOWN2, DOWN_K)
        norm_act(act, norms[4], lambda n: zero_col[:, n:n + 1])

        for r in range(3):
            act.wait_ge(v_hg0.sem, v_hg0.at(f"d{r}"))
            a_hg0.did(A(col_a[:, 8 * r:8 * r + 8], col_a[:, 8 * r:8 * r + 8], ACT.Exp), f"e{r}")
        HGF = {"q": (0, hq, ACT.Identity), "sig": (1, hf, ACT.Sigmoid), "v": (2, hv, ACT.Identity), "g": (3, hs, ACT.Identity)}

        def hg_read(S, i, what):
            j, dst, func = HGF[what]
            act.wait_ge(gemm_done, C_HG + 4 * i + j + 1)
            S.did(A(dst[:], ps[j][:], func), what)

        for what in ("q", "sig", "v"):
            hg_read(a_hg0, 0, what)

        def hg_squares_act(i):
            act.wait_ge(p_hg.sem, p_hg.at("pv", i))
            a_hg.did(A(ho2[:], ps[7][:], ACT.Square), "osq")

        def hg_inverse_act(i):
            act.wait_ge(p_hg.sem, p_hg.at("ss", i))
            a_hg.did(A(ho[:], ps[4][:], ACT.Ln, scale=1.0 / P, bias=eps_col[:, 0:1]), "lnv")
            act.wait_ge(a_hg.sem, a_hg.at("lnv", i))
            a_hg.did(A(ho2[:], ho[:], ACT.Exp, scale=-0.5), "rstd")

        def hg_round_act(i):
            act.wait_ge(v_hg.sem, v_hg.at("o2", i))
            dst = g_hi[:, i - 1, :] if isinstance(i, int) else g_hi[:, bass.ds(i - 1, 1), :]
            a_hg.did(A(dst, ho[:], ACT.Identity), "hi")

        def hg_act_turn(i, lag=True, nxt=True):
            def decays(w):
                act.wait_ge(v_hg.sem, v_hg.at(f"dr{w}", i))
                b = LEVELS.index(w) % 2
                a_hg.did(A(he[b][:], he[b][:], ACT.Exp), f"e{w}")

            act.preload_act_table_set(LN_EXP)
            act.wait_ge(v_hg.sem, v_hg.at("k", i))
            a_hg.did(A(hf[:], hf[:], ACT.Ln), "ln")
            if lag:
                hg_squares_act(i)
            else:
                a_hg.skip(act, i, "osq")
            act.wait_ge(p_hg.sem, p_hg.at("vT", i))
            a_hg.did(A(hvt[:], ps[4][:], ACT.Identity), "vt")
            decays(64)
            if lag:
                hg_inverse_act(i)
            else:
                a_hg.skip(act, i, "lnv", "rstd")
            decays(32)
            if lag:
                hg_round_act(i)
            else:
                a_hg.skip(act, i, "hi")
            hg_read(a_hg, i, "g")
            for w in LEVELS[2:]:
                decays(w)
            last_cols = hb[:].rearrange("p (j c) -> p j c", c=P)[:, :, P - 1:P]
            a_hg.did(A(het[:], last_cols, ACT.Exp), "et")
            act.wait_ge(v_hg.sem, v_hg.at("mr2", i))
            a_hg.did(A(he[1][:], hb[:], ACT.Exp), "eb")
            act.wait_ge(v_hg.sem, v_hg.at("mr1", i))
            for j in range(NT - 1):
                a_hg.did(A(he[0][:, j * P:(j + 1) * P], hb[:, j * P:(j + 1) * P], ACT.Exp, scale=-1.0,
                           bias=hb[:, (j + 1) * P - 1:(j + 1) * P]), f"ek{j}")
            act.wait_ge(p_hg.sem, p_hg.at("offA", i))
            a_hg.did(A(hsc[:, 0, P:T], ps[7][:, 0:3 * P], ACT.Identity), "offA")
            act.wait_ge(p_hg.sem, p_hg.at("offB", i))
            a_hg.did(A(hsc[:, 1, 2 * P:T], ps[4][:, 0:2 * P], ACT.Identity), "offB0")
            a_hg.did(A(hsc[:, 2, 3 * P:T], ps[4][:, 2 * P:3 * P], ACT.Identity), "offB1")
            if nxt:
                act.wait_ge(v_hg.sem, v_hg.at("x30", i))
                act.wait_ge(p_hg.sem, p_hg.at("S0", i))
                hg_read(a_hg, i + 1, "q")
                hg_read(a_hg, i + 1, "sig")
            else:
                a_hg.skip(act, i, "q", "sig")
            act.wait_ge(a_hg.sem, a_hg.at("g", i))
            a_hg.did(A(hs2[:], hs[:], ACT.Sigmoid), "sg")
            if nxt:
                hg_read(a_hg, i + 1, "v")
            else:
                a_hg.skip(act, i, "v")

        a_hg.open(act)
        hg_act_turn(0, lag=False)
        with act.Fori(1, HG_H - 1) as i:
            hg_act_turn(i)
        hg_act_turn(HG_H - 1, nxt=False)
        a_hg.skip(act, HG_H, "ln")
        hg_squares_act(HG_H)
        a_hg.skip(act, HG_H, "vt", "e64")
        hg_inverse_act(HG_H)
        a_hg.skip(act, HG_H, "e32")
        hg_round_act(HG_H)
        out_act(act, outs[4], C_HGOUT, (KT,))
        norm_act(act, norms[5], lambda n: zero_col[:, n:n + 1])
        ffn_act(a_ff[1], v_ff[1], C_UP3)
        out_act(act, outs[5], C_DOWN3, DOWN_K)
        norm_act(act, norms[6], None)
        for n in range(KT):
            act.wait_ge(norms[6].vx.sem, norms[6].vx.at(f"x{n}"))
            act.dma_start(outT[:, n, :], x[:, n, :]).then_inc(out_landed, 16)
        act.wait_ge(out_landed, 16 * KT)

    @block.vector
    def _(dve):
        V = nc.vector

        dve.wait_ge(a_set.sem, a_set.at("sig_c"))
        v_set.did(V.tensor_tensor(cvec[:], cvec[:], prm[:, COL["c"]:COL["c"] + KT], ALU.mult), "c")
        dve.wait_ge(const_ready, 13)
        v_set.did(V.tensor_tensor(levels[:, 2, :], levels[:, 0, :], levels[:, 1, :], ALU.bitwise_xor), "xor")
        dve.wait_ge(v_set.sem, v_set.at("xor"))
        v_set.did(V.tensor_copy(m[:, 7, 0:P], levels[:, 2, :]), "float")
        dve.wait_ge(v_set.sem, v_set.at("float"))
        v_set.did(V.tensor_tensor(m[:, 7, 0:P], m[:, 7, 0:P], early[:], ALU.add), "causal")
        dve.wait_ge(v_set.sem, v_set.at("causal"))
        for n, w in enumerate(LEVELS):
            v_set.did(V.tensor_scalar(m[:, n, 0:P], m[:, 7, 0:P], float(w), None, ALU.is_ge), f"ge{n}")
        dve.wait_ge(v_set.sem, v_set.at("ge6"))
        v_set.did(V.tensor_copy(levels[:, 0, :], m[:, 0, 0:P]), "lv0")
        for n in range(1, len(LEVELS)):
            v_set.did(V.tensor_tensor(levels[:, n, :], m[:, n, 0:P], m[:, n - 1, 0:P], ALU.subtract), f"lv{n}")
        v_set.did(V.tensor_scalar(levels[:, 7, :], m[:, 7, 0:P], 0.0, None, ALU.is_equal), "lv7")

        def first_mod():
            s_ada.open(dve)
            for turn in range(ADA_FIRST // ADA_BODY):
                ada_dve_pieces(dve, turn, start=True)
                ada_dve_mod(dve, turn)
            dve.wait_ge(s_ada.sem, s_ada.at("mod", ADA_FIRST // ADA_BODY - 1))
            v_col.did(V.scalar_tensor_tensor(col_a[:, 0:KT], mod[:, 8:16], 1.0, prm[:, COL["mix_pre"]:COL["mix_pre"] + KT],
                                             ALU.add, ALU.mult), "a1")
            dve.wait_ge(v_col.sem, v_col.at("a1"))

        dve.wait_ge(x_landed, 16)
        norm_dve(dve, norms[0], None, lambda n: col_a[:, n:n + 1], lambda n: mod[:, n:n + 1], first_mod)

        H = slice(0, H1)
        v_gate.did(V.memset(cA[0:H1, :], 1.0), "one")
        dve.wait_ge(gemm_done, C_GATE1 + 1)
        v_gate.did(V.tensor_scalar(rz[H, :], ps[5][0:H1, :], prm[0:H1, COL["gate1_b"]:COL["gate1_b"] + 1], None, ALU.add), "zi")
        v_gate.did(V.tensor_scalar(rlf[H, :], ps[5][32:32 + H1, :], prm[32:32 + H1, COL["gate1_b"]:COL["gate1_b"] + 1],
                                   None, ALU.add), "zf")
        dve.wait_ge(a_gate.sem, a_gate.at("ln"))
        dve.wait_ge(v_gate.sem, v_gate.at("zf"))
        v_gate.did(V.scalar_tensor_tensor(rlf[H, :], rlf[H, :], 0.0, rb[H, :], ALU.min, ALU.subtract), "lf")
        dve.wait_ge(v_gate.sem, v_gate.at("lf"))
        v_gate.did(V.tensor_tensor_scan(rb[H, :], cA[H, :], rlf[H, :], 0.0, ALU.mult, ALU.add), "b")
        v_gate.did(V.tensor_tensor_scan(rm[H, :], rlf[H, :], rz[H, :], 0.0, ALU.add, ALU.max), "m")
        dve.wait_ge(v_gate.sem, v_gate.at("m"))
        v_gate.did(V.tensor_tensor(rA[H, :], rb[H, :], rm[H, :], ALU.subtract), "A")
        v_gate.did(V.tensor_tensor(rD[H, :], rz[H, :], rb[H, :], ALU.subtract), "D")
        dve.wait_ge(p_gate.sem, p_gate.at("dT"))
        v_gate.did(V.tensor_copy(dcol[:], ps[4][:, 0:NT * H1].rearrange("p (s h) -> p h s", h=H1)), "dcol")
        V.memset(ypad[0][:, 0:30], 0.0)
        V.memset(ypad[1][:, 0:30], 0.0)
        v_gate.did(V.memset(qk_raw[:, :, 0:3], 0.0), "pad")
        v_gate.did(V.memset(acc[:], 0.0), "ysum0")

        v_mix.open(dve)
        with dve.Fori(0, H1) as h:
            dve.wait_ge(v_gate.sem, v_gate.at("ysum0"))
            dve.wait_ge(v_mix.sem, v_mix.at("hg1", h - 1))
            v_mix.did(V.tensor_copy(hp[:], prm[:, bass.ds(COL["head"] + HEAD_COLS * h, HEAD_COLS)]), "hp")
            v_mix.did(V.tensor_copy(dcur[:], dcol[:, bass.ds(h, 1), :]), "dc")
            dve.wait_ge(bc_landed, 16 * h + 16)
            v_mix.did(V.tensor_tensor(dg[:], bc[:, 0, :].rearrange("p (s c) -> p s c", c=P),
                                      early[:].unsqueeze(1).to_broadcast([P, NT, P]), ALU.add), "diag")

            def gated(j):
                dve.wait_ge(gemm_done, C_MIX + 12 * h + 2 * j + 2)
                dve.wait_ge(a_mix.sem, a_mix.at(f"sg{j}", h))
                v_mix.did(V.tensor_tensor(ypad[j][:, 30:], ps[2 * j + 1][:], sg[j][:], ALU.mult), f"gt{j}")

            def conv31(i):
                for j in range(CV_TAPS):
                    ch = (cA, cB)[j % 2]
                    wj = hp[:, HP_CVW + CV_TAPS * i + j:HP_CVW + CV_TAPS * i + j + 1]
                    src = ypad[i][:, j:j + T]
                    if j == 0:
                        dve.wait_ge(v_mix.sem, v_mix.at(f"gt{i}", h))
                    if j >= 2:
                        dve.wait_ge(v_mix.sem, v_mix.at(f"cv{i}_{j - 2}", h))
                        v_mix.did(V.scalar_tensor_tensor(ch[:], src, wj, ch[:], ALU.mult, ALU.add), f"cv{i}_{j}")
                    else:
                        v_mix.did(V.tensor_scalar(ch[:], src, wj, None, ALU.mult), f"cv{i}_{j}")
                dve.wait_ge(v_mix.sem, v_mix.at(f"cv{i}_{CV_TAPS - 1}", h))
                dst = y[:, bass.ds(2 * h + i, 1), :]
                v_mix.did(V.scalar_tensor_tensor(dst, cA[:], hp[:, HP_CVB + i:HP_CVB + i + 1], cB[:], ALU.add, ALU.add), f"y{i}")
                dve.wait_ge(v_mix.sem, v_mix.at(f"y{i}", h))
                v_mix.did(V.tensor_tensor(acc[:], acc[:], dst, ALU.add), f"ys{i}")

            gated(0)
            conv31(0)
            gated(1)
            conv31(1)
            for p_, part in enumerate("qk"):
                dve.wait_ge(a_mix.sem, a_mix.at(f"r{part}1", h))
                for t in range(QK_TAPS):
                    for j in range(2):
                        n = 2 * p_ + j
                        wj = hp[:, HP_QKW + QK_TAPS * n + t:HP_QKW + QK_TAPS * n + t + 1]
                        src = qk_raw[:, n, t:t + T]
                        if t == 0:
                            ins = V.tensor_scalar(qk[:, n, :], src, wj, None, ALU.mult)
                        else:
                            dve.wait_ge(v_mix.sem, v_mix.at(f"c{part}{j}_{t - 1}", h))
                            ins = V.scalar_tensor_tensor(qk[:, n, :], src, wj, qk[:, n, :], ALU.mult, ALU.add)
                        v_mix.did(ins, f"c{part}{j}_{t}")
            bank = [6, 7, 4, 5]
            dve.wait_ge(a_mix.sem, a_mix.at(f"off{NT - 2}", h))
            for st in range(NT):
                w = T - st * P
                dve.wait_ge(p_mix.sem, p_mix.at(f"qk{st}", h))
                v_mix.did(V.scalar_tensor_tensor(sp[:, WOFF[st]:WOFF[st] + w], ps[bank[st]][:, 0:w], float(DH1) ** -0.5,
                                                 wt[:, WOFF[st]:WOFF[st] + w], ALU.mult, ALU.mult), f"sp{st}")
            dve.wait_ge(p_mix.sem, p_mix.at("den", h))
            v_mix.did(V.scalar_tensor_tensor(rms[:], ps[7][:], -1.0, bc[:, 1, :], ALU.mult, ALU.max), "dm")
            dve.wait_ge(v_mix.sem, v_mix.at("dm", h))
            v_mix.did(V.tensor_tensor(rms[:], ps[7][:], rms[:], ALU.max), "dn")
            dve.wait_ge(v_mix.sem, v_mix.at("dn", h))
            v_mix.did(V.scalar_tensor_tensor(cA[:], rms[:], EPS, rms[:], ALU.mult, ALU.mult), "d2")
            dve.wait_ge(v_mix.sem, v_mix.at("d2", h))
            dve.wait_ge(p_mix.sem, p_mix.at("hs", h))
            v_mix.did(V.scalar_tensor_tensor(cA[:], ps[5][:], 1.0 / DH1, cA[:], ALU.mult, ALU.add), "vr")
            dve.wait_ge(a_mix.sem, a_mix.at("rstd", h))
            for e in range(2):
                v_mix.did(V.tensor_tensor((cA, cB)[e][:], ps[6 if e == 0 else 4][:], rstd[:], ALU.mult), f"h{e}")
            for e in range(2):
                dve.wait_ge(v_mix.sem, v_mix.at(f"h{e}", h))
                v_mix.did(V.scalar_tensor_tensor(hm[:, bass.ds(2 * h + e, 1), :], (cA, cB)[e][:],
                                                 hp[:, HP_G + e:HP_G + e + 1], so[:, e, :], ALU.mult, ALU.mult), f"hg{e}")

        for n in range(KT):
            dve.wait_ge(a_ln.sem, a_ln.at(f"hh{n}"))
            v_ln.did(V.tensor_tensor(u_lo[:, n, :], hm[:, n, :], u_hi[:, n, :].bitcast(f32), ALU.subtract), f"hl{n}")
        dve.wait_ge(p_ln.sem, p_ln.at("mu"))
        v_ln.did(V.tensor_scalar(rms[:], ps[4][:], 1.0 / D, None, ALU.mult), "mu")
        dve.wait_ge(v_ln.sem, v_ln.at("mu"))
        for n in range(KT):
            v_ln.did(V.tensor_tensor(y[:, n, :], y[:, n, :], rms[:], ALU.subtract), f"yc{n}")
        dve.wait_ge(v_ln.sem, v_ln.at(f"yc{KT - 1}"))
        dve.wait_ge(a_ln.sem, a_ln.at("rstd"))
        for n in range(KT):
            v_ln.did(V.tensor_tensor(y[:, n, :], y[:, n, :], rstd[:], ALU.mult), f"t{n}")
        for n in range(KT):
            dve.wait_ge(a_ln.sem, a_ln.at(f"hi{n}"))
            v_ln.did(V.tensor_tensor(y_lo[:, n, :], y[:, n, :], y_hi[:, n, :].bitcast(f32), ALU.subtract), f"lo{n}")

        first = ADA_FIRST // ADA_BODY
        out_dve(dve, outs[0], lambda it: ada_dve_pieces(dve, first + it), lambda it: ada_dve_mod(dve, first + it))
        dve.wait_ge(s_ada.sem, s_ada.at("mod", ADA_ALL // ADA_BODY - 1))
        for name, o, src, gain in (("g1", 8, 16, "mix_post"), ("a2", 16, 32, "ffn_pre"), ("g2", 24, 40, "ffn_post")):
            g_ = prm[:, COL[gain]:COL[gain] + KT]
            if name == "a2":
                ins = V.scalar_tensor_tensor(col_a[:, o:o + KT], mod[:, src:src + KT], 1.0, g_, ALU.add, ALU.mult)
            else:
                ins = V.tensor_tensor(col_a[:, o:o + KT], mod[:, src:src + KT], g_, ALU.mult)
            v_col.did(ins, name)
        dve.wait_ge(v_col.sem, v_col.at("g2"))
        norm_dve(dve, norms[1], lambda n: col_a[:, 8 + n:9 + n], lambda n: col_a[:, 16 + n:17 + n],
                 lambda n: mod[:, 24 + n:25 + n])

        V.memset(fraw[0][:, 0:2], 0.0).then_inc(ff1_pads, 1)
        V.memset(fraw[1][:, 0:2], 0.0).then_inc(ff1_pads, 1)
        v_ff1.open(dve)
        with dve.Fori(0, FT // 2) as it:
            for s in range(2):
                j = 2 * it + s
                dve.wait_ge(a_ff1.sem, a_ff1.at("silu", j - 1))
                v_ff1.did(V.tensor_copy(fprm[:], prm[:, bass.ds(COL["ff"] + FF_COLS * j, FF_COLS)]), "prm")
                dve.wait_ge(v_ff1.sem, v_ff1.at("prm", j))
                for t in range(FF_TAPS):
                    for n, name in enumerate("ga"):
                        if t == 0:
                            dve.wait_ge(a_ff1.sem, a_ff1.at(name, j))
                        wj = fprm[:, FF_TAPS * n + t:FF_TAPS * n + t + 1]
                        src = fraw[n][:, t:t + T]
                        if t == 0:
                            ins = V.tensor_scalar(fcv[n][:], src, wj, None, ALU.mult)
                        else:
                            dve.wait_ge(v_ff1.sem, v_ff1.at(f"{name}{t - 1}", j))
                            ins = V.scalar_tensor_tensor(fcv[n][:], src, wj, fcv[n][:], ALU.mult, ALU.add)
                        v_ff1.did(ins, f"{name}{t}")
                dve.wait_ge(a_ff1.sem, a_ff1.at("silu", j))
                dve.wait_ge(v_ff1.sem, v_ff1.at(f"a{FF_TAPS - 1}", j))
                v_ff1.did(V.scalar_tensor_tensor(fval[:], fcv[1][:], fprm[:, 7:8], fsi[:], ALU.add, ALU.mult), "f")
                dve.wait_ge(a_ff1.sem, a_ff1.at("hi", j))
                dve.wait_ge(v_ff1.sem, v_ff1.at("f", j))
                v_ff1.did(V.tensor_tensor(f_lo[:, bass.ds(j, 1), :], fval[:], f_hi[:, bass.ds(j, 1), :].bitcast(f32),
                                          ALU.subtract), "lo")
        out_dve(dve, outs[1])
        gains = lambda layer, which: (lambda n: prm_col("gains", 32 * layer + 8 * which + n))
        zero = lambda n: zero_col[:, n:n + 1]
        norm_dve(dve, norms[2], lambda n: col_a[:, 24 + n:25 + n], gains(0, 0), zero)

        R = slice(0, FOX_H)
        v_fg.did(V.memset(one_row[R, :], 1.0), "one")
        dve.wait_ge(gemm_done, C_GATE2 + 1)
        v_fg.did(V.tensor_scalar(fz[R, :], ps[3][R, :], prm[R, COL["fox_b"]:COL["fox_b"] + 1], None, ALU.add), "z")
        dve.wait_ge(a_fg.sem, a_fg.at("ln"))
        dve.wait_ge(v_fg.sem, v_fg.at("z"))
        v_fg.did(V.scalar_tensor_tensor(fl[R, :], fz[R, :], 0.0, fl[R, :], ALU.min, ALU.subtract), "lf")
        dve.wait_ge(v_fg.sem, v_fg.at("lf"))
        v_fg.did(V.tensor_tensor_scan(fc[R, :], one_row[R, :], fl[R, :], 0.0, ALU.mult, ALU.add), "c")
        for t, step in ((va_hi, "zero_hi"), (va_lo, "zero_lo")):
            for a in range(2):
                o = (1 - a) * FOX_D
                ins = V.memset(t[:, a, :, o:o + FOX_D].bitcast(f32), 0.0)
            v_fg.did(ins, step)

        def fox_low(S, aS, i, what, at=None):
            dve.wait_ge(aS.sem, aS.at(what[0], *at))
            if what == "ql":
                S.did(V.scalar_tensor_tensor(q_lo[:], ps[0][:], -float(FOX_D) ** -0.5, q_hi[:].bitcast(f32),
                                             ALU.mult, ALU.subtract), "ql")
            else:
                S.did(V.tensor_tensor(k_lo[:], ps[1][:], k_hi[:].bitcast(f32), ALU.subtract), "kl")

        for what in ("ql", "kl"):
            fox_low(v_fox0, a_fox0, 0, what, (0,))

        def fox_dve_turn(i, b, lag=True, nxt=True):
            dve.wait_ge(bc_landed, 16 * H1 + 16 * (i + 1))

            def negated(n):
                a, r = divmod(n, NT)
                w = (r + 1) * P
                dve.wait_ge(p_fox.sem, p_fox.at(f"L{n}", i))
                if n >= 2:
                    dve.wait_ge(a_fox.sem, a_fox.at(f"e{n - 2}", i))
                dve.sem_inc(turn_waited, 1)
                v_fox.did(V.tensor_tensor_reduce(out=lg[n % 2][:, 0:w], in0=ps[4 + n % 2][:, 0:w], in1=cbc[b][:, a, 0:w],
                                                 scale=1.0, scalar=BIG, op0=ALU.add, op1=ALU.min,
                                                 accum_out=mx[:, n % 2:n % 2 + 1]), f"N{n}")

            def divided(n):
                w = (n % NT + 1) * P
                dve.wait_ge(a_fox.sem, a_fox.at(f"e{n}", i))
                v_fox.did(V.reciprocal(row_inv[:, n % 2:n % 2 + 1], row_sum[:, n % 2:n % 2 + 1]), f"r{n}")
                dve.wait_ge(v_fox.sem, v_fox.at(f"r{n}", i))
                v_fox.did(V.tensor_scalar(pr[n % 2][:, 0:w], pr[n % 2][:, 0:w], row_inv[:, n % 2:n % 2 + 1], None,
                                          ALU.mult), f"s{n}")

            def low(n):
                a, r = divmod(n, NT)
                dve.wait_ge(a_fox.sem, a_fox.at(f"ph{n}", i))
                cols = slice(r * P, (r + 1) * P)
                v_fox.did(V.tensor_tensor(pt_lo[a][:, 0:r + 1, cols],
                                          ps[6 + n % 2][:, 0:(r + 1) * P].rearrange("p (s c) -> p s c", c=P),
                                          pt_hi[a][:, 0:r + 1, cols].bitcast(f32), ALU.subtract), f"pl{n}")

            negated(0)
            divided(0)
            if lag:
                fox_rest(i)
            else:
                v_fox.skip(dve, i, "lo")
            for n in range(U - 1):
                negated(n + 1)
                low(n)
                divided(n + 1)
                if n == 0:
                    dve.wait_ge(a_fox.sem, a_fox.at("vh1", i))
                    for a in range(2):
                        cols = slice(a * FOX_D, (a + 1) * FOX_D)
                        v_fox.did(V.tensor_tensor(va_lo[:, a, :, cols],
                                                  ps[3][:].rearrange("p (s c) -> p s c", c=P)[:, :, cols],
                                                  va_hi[:, a, :, cols].bitcast(f32), ALU.subtract), f"vl{a}")
            if nxt:
                for what in ("ql", "kl"):
                    fox_low(v_fox, a_fox, i + 1, what, (i,))
            else:
                v_fox.skip(dve, i, "ql", "kl")
            low(U - 1)

        def fox_rest(i):
            at_ = (lambda t: t[:, i - 1, :]) if isinstance(i, int) else (lambda t: t[:, bass.ds(i - 1, 1), :])
            dve.wait_ge(a_fox.sem, a_fox.at("hi", i))
            v_fox.did(V.tensor_tensor(at_(a_lo), ps[3][:], at_(a_hi).bitcast(f32), ALU.subtract), "lo")

        v_fox.open(dve)
        PAIRS = FOX_H // 2
        fox_dve_turn(0, 0, lag=False)
        with dve.Fori(0, PAIRS // 2 - 1) as it:
            for sub in range(2):
                fox_dve_turn(2 * it + sub + 1, 1 - sub)
        fox_dve_turn(PAIRS - 1, 1, nxt=False)
        v_fox.skip(dve, PAIRS, "N0", "r0", "s0")
        fox_rest(PAIRS)
        out_dve(dve, outs[2])
        norm_dve(dve, norms[3], gains(0, 1), gains(0, 2), zero)

        def ffn_dve(vS, aS, base):
            vS.open(dve)
            with dve.Fori(0, FT // 2) as it:
                for s in range(2):
                    j = 2 * it + s
                    dve.wait_ge(gemm_done, base + 4 * it + 2 * s + 2)
                    dve.wait_ge(aS.sem, aS.at("silu", j))
                    dve.wait_ge(aS.sem, aS.at("hi", j - 2))
                    vS.did(V.tensor_tensor(fraw[s][:, 0:T], ps[2 * s + 1][:], fcv[s][:], ALU.mult), "f")
                    dve.wait_ge(aS.sem, aS.at("hi", j))
                    dve.wait_ge(vS.sem, vS.at("f", j))
                    vS.did(V.tensor_tensor(f_lo[:, bass.ds(j, 1), :], fraw[s][:, 0:T],
                                           f_hi[:, bass.ds(j, 1), :].bitcast(f32), ALU.subtract), "lo")

        ffn_dve(v_ff[0], a_ff[0], C_UP2)
        out_dve(dve, outs[3])
        norm_dve(dve, norms[4], gains(0, 3), gains(1, 0), zero)

        lb_row = lambda r: prm[:, COL["lb"] + 8 * r:COL["lb"] + 8 * r + 8]
        ca = lambda r: col_a[:, 8 * r:8 * r + 8]
        v_hg0.did(V.tensor_tensor(ca(3), lb_row(0), lb_row(1), ALU.max), "mx")
        dve.wait_ge(v_hg0.sem, v_hg0.at("mx"))
        v_hg0.did(V.tensor_tensor(ca(3), ca(3), lb_row(2), ALU.max), "mx2")
        dve.wait_ge(v_hg0.sem, v_hg0.at("mx2"))
        for r in range(3):
            v_hg0.did(V.tensor_tensor(ca(r), lb_row(r), ca(3), ALU.subtract), f"d{r}")
        dve.wait_ge(a_hg0.sem, a_hg0.at("e2"))
        v_hg0.did(V.tensor_tensor(ca(3), ca(0), ca(1), ALU.add), "s")
        dve.wait_ge(v_hg0.sem, v_hg0.at("s"))
        v_hg0.did(V.tensor_tensor(ca(4), ca(3), ca(2), ALU.add), "s2")
        dve.wait_ge(v_hg0.sem, v_hg0.at("s2"))
        v_hg0.did(V.reciprocal(ca(4), ca(4)), "r")
        dve.wait_ge(v_hg0.sem, v_hg0.at("r"))
        v_hg0.did(V.tensor_tensor(ca(4), ca(3), ca(4), ALU.mult), "lb")
        dve.wait_ge(v_hg0.sem, v_hg0.at("lb"))
        v_hg0.did(V.tensor_scalar(ca(5), ca(4), -1.0, 1.0, ALU.mult, ALU.add), "oml")
        v_hg0.did(V.memset(hsc[:], 0.0), "zero")
        dve.wait_ge(v_hg0.sem, v_hg0.at("zero"))

        diag = hsc[:].rearrange("p c t -> p (c t)")

        def hg_gate_dve(i):
            dve.wait_ge(a_hg.sem, a_hg.at("sg", i - 1))
            v_hg.did(V.tensor_tensor(hs[:], hs[:], hs2[:], ALU.mult), "gs")

        def hg_norm_dve(i):
            dve.wait_ge(a_hg.sem, a_hg.at("rstd", i))
            v_hg.did(V.tensor_tensor(ho[:], ps[7][:], ho2[:], ALU.mult), "o1")
            dve.wait_ge(v_hg.sem, v_hg.at("o1", i))
            v_hg.did(V.scalar_tensor_tensor(ho[:], ho[:], prm_col("gnorm"), hs[:], ALU.mult, ALU.mult), "o2")

        def hg_rest_dve(i):
            at_ = (lambda t: t[:, i - 1, :]) if isinstance(i, int) else (lambda t: t[:, bass.ds(i - 1, 1), :])
            dve.wait_ge(a_hg.sem, a_hg.at("hi", i))
            v_hg.did(V.tensor_tensor(at_(g_lo), ho[:], at_(g_hi).bitcast(f32), ALU.subtract), "lo")

        def hg_dve_turn(i, lag=True):
            w_ = lambda step: dve.wait_ge(v_hg.sem, v_hg.at(step, i))
            one_ = lambda o: col_a[:, bass.ds(o + i, 1)] if not isinstance(i, int) else col_a[:, o + i:o + i + 1]
            dve.wait_ge(v_hg.sem, v_hg.at("pc0", i - 1))
            V.tensor_copy(lbcur[:, 1:2], one_(40))
            v_hg.did(V.tensor_copy(lbcur[:, 0:1], one_(32)), "cur")
            w_("cur")
            dve.wait_ge(a_hg0.sem, a_hg0.at("sig"))
            dve.wait_ge(a_hg.sem, a_hg.at("sig", i - 1))
            v_hg.did(V.tensor_scalar(hf[:], hf[:], lbcur[:, 1:2], lbcur[:, 0:1], ALU.mult, ALU.add), "f")
            w_("f")
            v_hg.did(V.tensor_scalar(hk[:], hf[:], -1.0, 1.0, ALU.mult, ALU.add), "k")
            if lag:
                hg_gate_dve(i)
            else:
                v_hg.skip(dve, i, "gs")
            dve.wait_ge(a_hg.sem, a_hg.at("ln", i))
            for j in range(NT):
                ts = slice(j * P, (j + 1) * P)
                v_hg.did(V.tensor_tensor_scan(hb[:, ts], ones[:], hf[:, ts], 0.0, ALU.mult, ALU.add), f"b{j}")
            w_(f"b{NT - 1}")

            def halves(t, w):
                v = t[:].rearrange("p (n c) -> p n c", c=2 * w)
                return v[:, :, 0:w], v[:, :, w:2 * w]

            def diffs(n):
                w = LEVELS[n]
                if n >= 2:
                    w_(f"mr{LEVELS[n - 2]}")
                left, right = halves(hb, w)
                mid = left[:, :, w - 1:w].to_broadcast([P, T // (2 * w), w])
                dl, dr = halves(he[n % 2], w)
                v_hg.did(V.tensor_tensor(dl, mid, left, ALU.subtract), f"dl{w}")
                v_hg.did(V.tensor_tensor(dr, right, mid, ALU.subtract), f"dr{w}")

            def weighted(n):
                w = LEVELS[n]
                dve.wait_ge(a_hg.sem, a_hg.at(f"e{w}", i))
                if n >= 2:
                    dve.wait_ge(p_hg.sem, p_hg.at(f"S{LEVELS[n - 2]}", i))
                el, er = halves(he[n % 2], w)
                kl, _ = halves(hk, w)
                _, qr = halves(hq, w)
                ol, or_ = halves(hl[n % 2], w)
                v_hg.did(V.tensor_tensor(ol, kl, el, ALU.mult), f"ml{w}")
                v_hg.did(V.tensor_tensor(or_, qr, er, ALU.mult), f"mr{w}")

            def pick(n, step, pe_step):
                dve.wait_ge(p_hg.sem, p_hg.at(pe_step, i))
                if n:
                    w_(f"pc{LEVELS[n - 1]}")
                dve.sem_inc(turn_waited, 1)
                v_hg.did(V.copy_predicated(bass.AP(hsc, 0, [[NT * T, P], [T + P, NT], [1, P]]),
                                           levels[:, n, :].unsqueeze(1).to_broadcast([P, NT, P]),
                                           ps[5 + n % 2][:].rearrange("p (c t) -> p c t", t=P)), step)

            diffs(0)
            for n, w in enumerate(LEVELS):
                if n + 1 < len(LEVELS):
                    diffs(n + 1)
                weighted(n)
                if n:
                    pick(n - 1, f"pc{LEVELS[n - 1]}", f"S{LEVELS[n - 1]}")
                if n == 0:
                    if lag:
                        hg_norm_dve(i)
                    else:
                        v_hg.skip(dve, i, "o1", "o2")
                elif n == 1:
                    if lag:
                        hg_rest_dve(i)
                    else:
                        v_hg.skip(dve, i, "lo")
            dve.wait_ge(a_hg.sem, a_hg.at("eb", i))
            v_hg.did(V.tensor_tensor(hqd[:], hq[:], he[1][:], ALU.mult), "qd")
            dve.wait_ge(a_hg.sem, a_hg.at(f"ek{NT - 2}", i))
            v_hg.did(V.tensor_tensor(hkd[:, 0:3 * P], hk[:, 0:3 * P], he[0][:, 0:3 * P], ALU.mult), "kd")
            w_("kd")
            v_hg.did(V.tensor_scalar(hkx[:, 0, :], hkd[:, 0:P], het[:, 1:2], None, ALU.mult), "x20")
            v_hg.did(V.tensor_scalar(hkx[:, 1, :], hkd[:, P:2 * P], het[:, 2:3], None, ALU.mult), "x31")
            w_("x20")
            v_hg.did(V.tensor_scalar(hkx[:, 2, :], hkx[:, 0, :], het[:, 2:3], None, ALU.mult), "x30")
            pick(6, "pc1", "S1")
            pick(7, "pc0", "S0")

        v_hg.open(dve)
        hg_dve_turn(0, lag=False)
        with dve.Fori(1, HG_H) as i:
            hg_dve_turn(i)
        v_hg.skip(dve, HG_H, "cur", "f", "k")
        hg_gate_dve(HG_H)
        v_hg.skip(dve, HG_H, *hg_steps[hg_steps.index("b0"):hg_steps.index("o1")])
        hg_norm_dve(HG_H)
        v_hg.skip(dve, HG_H, *hg_steps[hg_steps.index("o2") + 1:hg_steps.index("lo")])
        hg_rest_dve(HG_H)
        out_dve(dve, outs[4])
        norm_dve(dve, norms[5], gains(1, 1), gains(1, 2), zero)
        ffn_dve(v_ff[1], a_ff[1], C_UP3)
        out_dve(dve, outs[5])
        norm_dve(dve, norms[6], gains(1, 3), None, None)

    ctx.close()


def _tiles(a):
    return np.ascontiguousarray(a.reshape(-1, P, a.shape[1]).transpose(1, 0, 2))


def _columns(v):
    return v.reshape(-1, P).T


def _stream(ins):
    out = np.zeros((C_END, P, D), np.float32)

    def chunk(c, w):
        w = w.reshape(-1, P, w.shape[1])
        out[c].reshape(P, KT, P)[:, :w.shape[0], :w.shape[2]] = w.transpose(1, 0, 2)

    def cols(w, n):
        return w[:, n * P:(n + 1) * P]

    w = ins["w_in"][0]
    g = 4 * D
    gates = out[C_GATE1].reshape(P, KT, P)
    gates[:, :, 0:H1] = w[:, g:g + H1].reshape(KT, P, H1).transpose(1, 0, 2)
    gates[:, :, 32:32 + H1] = w[:, g + H1:g + 2 * H1].reshape(KT, P, H1).transpose(1, 0, 2)
    a = w[:, g + 2 * H1:]
    for h in range(H1):
        parts = [cols(a, KT + 2 * h), cols(a, 2 * h), cols(a, KT + 2 * h + 1), cols(a, 2 * h + 1)]
        parts += [cols(w, KT * p + 2 * h + e) for p in range(4) for e in range(2)]
        for j, part in enumerate(parts):
            chunk(C_MIX + 12 * h + j, part)
    for n in range(KT):
        for j in range(2):
            chunk(C_WOUT1 + 2 * n + j, cols(ins["w_out"][0][D * j:D * (j + 1)], n))

    def ffn(up, down, c_up, c_down, gate_first):
        for j in range(FT):
            first, second = (j, FT + j) if gate_first else (FT + j, j)
            chunk(c_up + 2 * j, cols(up, first))
            chunk(c_up + 2 * j + 1, cols(up, second))
        for n in range(KT):
            k = 0
            for j, nk in enumerate(DOWN_K):
                chunk(c_down + 3 * n + j, cols(down[k * P:(k + nk) * P], n))
                k += nk

    ffn(ins["ffn_up"][0], ins["ffn_down"][0], C_UP1, C_DOWN1, False)
    w = ins["fox_w_in_2"][0]
    chunk(C_GATE2, w[:, 3 * D:])
    for i in range(KT):
        for j in range(3):
            chunk(C_FOX + 3 * i + j, cols(w, KT * j + i))
        chunk(C_FOXOUT + i, cols(ins["fox_w_out_2"][0], i))
    ffn(ins["ffn_w_in_2"][0], ins["ffn_w_out_2"][0], C_UP2, C_DOWN2, True)
    for i in range(KT):
        for j in range(4):
            chunk(C_HG + 4 * i + j, cols(ins["hgrn_w_in_2"][0], KT * j + i))
        chunk(C_HGOUT + i, cols(ins["hgrn_w_out_2"][0], i))
    ffn(ins["ffn_w_in_2"][1], ins["ffn_w_out_2"][1], C_UP3, C_DOWN3, True)
    return out


def _params(ins):
    out = np.zeros((P, NPRM), np.float32)

    def put(name, block_, at=0):
        out[:block_.shape[0], COL[name] + at:COL[name] + at + block_.shape[1]] = block_

    put("c", _columns(ins["c"][0]))
    put("ada_b", _columns(ins["ada_b"][0]))
    for name, key in (("mix_pre", "mix_pre_g"), ("mix_post", "mix_post_g"), ("ffn_pre", "ffn_pre_g"),
                      ("ffn_post", "ffn_post_g"), ("ln_g", "cv_ln_g"), ("ln_b", "cv_ln_b")):
        put(name, _columns(ins[key][0]))
    out[0:H1, COL["gate1_b"]] = ins["igate_b"][0]
    out[32:32 + H1, COL["gate1_b"]] = ins["fgate_b"][0]
    for h in range(H1):
        at = HEAD_COLS * h
        for e in range(2):
            ch = slice((2 * h + e) * P, (2 * h + e + 1) * P)
            put("head", ins["cv_dw_w"][0][:, ch].T, at + HP_CVW + CV_TAPS * e)
            put("head", ins["cv_dw_b"][0][ch][:, None], at + HP_CVB + e)
            put("head", ins["ml_norm_g"][0][ch][:, None], at + HP_G + e)
            for p in range(2):
                qc = slice(D * p + ch.start, D * p + ch.stop)
                put("head", ins["qk_conv_w"][0][:, qc].T, at + HP_QKW + QK_TAPS * (2 * p + e))
                put("head", ins["qk_conv_b"][0][qc][:, None], at + HP_QKB + 2 * p + e)
    for j in range(FT):
        for n, tile in enumerate((FT + j, j)):
            ch = slice(tile * P, (tile + 1) * P)
            put("ff", ins["ffn_conv_w"][0][:, ch].T, FF_COLS * j + FF_TAPS * n)
            put("ff", ins["ffn_conv_b"][0][ch][:, None], FF_COLS * j + 2 * FF_TAPS + n)
    out[0:FOX_H, COL["fox_b"]] = ins["fox_b_f_2"][0]
    for r in range(3):
        put("lb", _columns(ins["hgrn_lb_table_2"][r]), 8 * r)
    put("gnorm", ins["hgrn_gnorm_2"][0][:, None])
    for layer in range(2):
        for which in range(4):
            put("gains", _columns(ins["norm_gains_2"][layer, which]), 32 * layer + 8 * which)
    return out


def kernel(**inputs):
    import concourse.bacc as bacc
    from concourse.bass_utils import run_bass_kernel_spmd

    ins = {k: np.asarray(v) for k, v in inputs.items()}
    n_ada = ADA_ALL
    arrays = {
        "xT": _tiles(ins["x"][0].T),
        "wstream": _stream(ins),
        "ada": np.ascontiguousarray(ins["ada_w"][0].reshape(KT, P, n_ada, ADA_COLS).transpose(2, 1, 0, 3)
                                    ).reshape(n_ada, P, KT * ADA_COLS),
        "params": _params(ins),
    }
    nc = bacc.Bacc("TRN2", target_bir_lowering=False, num_devices=1)
    f32 = mybir.dt.float32
    aps = [nc.dram_tensor(f"in_{k}", list(a.shape), f32, kind="ExternalInput").ap() for k, a in arrays.items()]
    out = nc.dram_tensor("out_T", [P, KT, T], f32, kind="ExternalOutput").ap()
    rows1 = nc.dram_tensor("gate_rows", [2, H1, T], f32, kind="Internal").ap()
    rows2 = nc.dram_tensor("decay_rows", [FOX_H, T], f32, kind="Internal").ap()
    build(nc, *aps, out, rows1, rows2)
    r = run_bass_kernel_spmd(nc, [{f"in_{k}": a for k, a in arrays.items()}], core_ids=[0])
    y = np.asarray(r.results[0]["out_T"])
    return np.ascontiguousarray(y.transpose(2, 1, 0)).reshape(1, T, D)
```
